# Optimizing a Trainium2 kernel written in Bass

```python
import jax, jax.numpy as jnp
from jax import lax
import numpy as np
import math

D_MODEL = 1024
BATCH = 1
SEQ = 512
DEPTH = 1

SB_HEADS = 8
SB_HEAD_DIM = 64
SB_WIDTH = SB_HEADS * SB_HEAD_DIM
SB_BLOCK = 128

GDN_HEADS = 4
GDN_HEAD_DIM = 128
GDN_WIDTH = GDN_HEADS * GDN_HEAD_DIM
GDN_CHUNK = 64
CONV_K = 4

EPS = 1e-6

SPLIT_SIZES = (3 * SB_WIDTH, SB_WIDTH, 3 * GDN_WIDTH, GDN_WIDTH, GDN_HEADS, GDN_HEADS, D_MODEL, D_MODEL)
N_IN = 3 * SB_WIDTH + SB_WIDTH + 3 * GDN_WIDTH + GDN_WIDTH + 2 * GDN_HEADS + 2 * D_MODEL


def rms_norm(x, w):
    xf = x.astype(jnp.float32)
    y = xf * lax.rsqrt(jnp.mean(xf * xf, axis=-1, keepdims=True) + EPS)
    return (y * w.astype(jnp.float32)).astype(x.dtype)

def l2_normalize(x):
    return x * lax.rsqrt(jnp.sum(x * x, axis=-1, keepdims=True) + EPS)

def split_heads(t, n_heads, head_dim):
    b, s, _ = t.shape
    return t.reshape(b, s, n_heads, head_dim).transpose(0, 2, 1, 3)

def merge_heads(t):
    b, h, s, d = t.shape
    return t.transpose(0, 2, 1, 3).reshape(b, s, h * d)

def stick_breaking_attention(q, k, v):
    seq = q.shape[2]
    scale = SB_HEAD_DIM ** -0.5
    outs = []
    for blk in range(seq // SB_BLOCK):
        t0 = blk * SB_BLOCK
        t1 = t0 + SB_BLOCK
        qb = q[:, :, t0:t1].astype(jnp.float32)
        kb = k[:, :, :t1].astype(jnp.float32)
        vb = v[:, :, :t1].astype(jnp.float32)
        z = jnp.einsum('bhqd,bhkd->bhqk', qb, kb) * scale
        q_pos = t0 + jnp.arange(SB_BLOCK)[:, None]
        k_pos = jnp.arange(t1)[None, :]
        causal = k_pos < q_pos
        log_keep = jnp.where(causal, -jax.nn.softplus(z), 0.0)
        suffix = lax.cumsum(log_keep, axis=3, reverse=True) - log_keep
        log_a = jax.nn.log_sigmoid(z) + suffix
        a = jnp.where(causal, jnp.exp(log_a), 0.0)
        outs.append(jnp.einsum('bhqk,bhkd->bhqd', a, vb))
    return jnp.concatenate(outs, axis=2).astype(q.dtype)

def causal_depthwise_conv(x, w):
    channels = x.shape[-1]
    return lax.conv_general_dilated(
        x, w[:, None, :].astype(x.dtype), window_strides=(1,), padding=[(CONV_K - 1, 0)],
        dimension_numbers=('NWC', 'WIO', 'NWC'), feature_group_count=channels)

def gated_delta_rule_chunked(q, k, v, g, beta):
    b, h, seq, dk = q.shape
    dv = v.shape[-1]
    c = GDN_CHUNK
    n = seq // c
    q = q * dk ** -0.5
    q = q.reshape(b, h, n, c, dk)
    k = k.reshape(b, h, n, c, dk)
    v = v.reshape(b, h, n, c, dv)
    beta = beta.reshape(b, h, n, c)
    g = jnp.cumsum(g.reshape(b, h, n, c), axis=-1)
    idx = jnp.arange(c)
    lower_incl = idx[:, None] >= idx[None, :]
    strict = idx[:, None] > idx[None, :]
    decay = jnp.exp(jnp.where(lower_incl, g[..., :, None] - g[..., None, :], -jnp.inf))
    kk = jnp.einsum('bhnid,bhnjd->bhnij', k, k)
    m = jnp.where(strict, beta[..., :, None] * kk * decay, 0.0)
    rhs = jnp.concatenate([v * beta[..., None], k * (beta * jnp.exp(g))[..., None]], axis=-1)
    sol = lax.linalg.triangular_solve(m, rhs, left_side=True, lower=True, unit_diagonal=True)
    u = sol[..., :dv]
    w = sol[..., dv:]
    intra = jnp.where(lower_incl, jnp.einsum('bhnid,bhnjd->bhnij', q, k) * decay, 0.0)

    def step(state, inp):
        q_c, k_c, u_c, w_c, g_c, intra_c = inp
        v_new = u_c - jnp.einsum('bhcd,bhde->bhce', w_c, state)
        o = (jnp.einsum('bhcd,bhde->bhce', q_c * jnp.exp(g_c)[..., None], state)
             + jnp.einsum('bhij,bhje->bhie', intra_c, v_new))
        g_last = g_c[..., -1:]
        state = (state * jnp.exp(g_last)[..., None]
                 + jnp.einsum('bhcd,bhce->bhde', k_c * jnp.exp(g_last - g_c)[..., None], v_new))
        return state, o

    chunk_first = lambda t: jnp.moveaxis(t, 2, 0)
    xs = tuple(chunk_first(t) for t in (q, k, u, w, g, intra))
    state0 = jnp.zeros((b, h, dk, dv), jnp.float32)
    _, o = lax.scan(step, state0, xs)
    return jnp.moveaxis(o, 0, 2).reshape(b, h, seq, dv)

def hybrid_layer(x, pre_w, post_w, w_in, conv_w, a_log, dt_bias, gdn_norm_w,
                 w_branch_sb, w_branch_gdn, w_out):
    f32 = jnp.float32
    h = rms_norm(x, pre_w)
    proj = h @ w_in
    points = [int(p) for p in np.cumsum(SPLIT_SIZES)[:-1]]
    sb_qkv, sb_gate, gdn_qkv, gdn_gate, gdn_a, gdn_b, merge_sb, merge_gdn = jnp.split(proj, points, axis=-1)

    q_sb, k_sb, v_sb = [split_heads(t, SB_HEADS, SB_HEAD_DIM) for t in jnp.split(sb_qkv, 3, axis=-1)]
    o_sb = merge_heads(stick_breaking_attention(q_sb, k_sb, v_sb)) * jax.nn.silu(sb_gate)

    gdn_qkv = jax.nn.silu(causal_depthwise_conv(gdn_qkv, conv_w))
    q_g, k_g, v_g = [split_heads(t, GDN_HEADS, GDN_HEAD_DIM).astype(f32) for t in jnp.split(gdn_qkv, 3, axis=-1)]
    q_g = l2_normalize(q_g)
    k_g = l2_normalize(k_g)
    g = (-jnp.exp(a_log.astype(f32)) * jax.nn.softplus(gdn_a.astype(f32) + dt_bias.astype(f32))).transpose(0, 2, 1)
    beta = jax.nn.sigmoid(gdn_b.astype(f32)).transpose(0, 2, 1)
    o_g = gated_delta_rule_chunked(q_g, k_g, v_g, g, beta)
    o_g = merge_heads(rms_norm(o_g, gdn_norm_w)).astype(x.dtype) * jax.nn.silu(gdn_gate)

    merged = (jax.nn.sigmoid(merge_sb) * (o_sb @ w_branch_sb)
              + jax.nn.sigmoid(merge_gdn) * (o_g @ w_branch_gdn))
    y = merged @ w_out
    return x + rms_norm(y, post_w)

def first_inputs(seed: int = 0) -> dict:
    key = jax.random.key(seed)
    ks = jax.random.split(key, 12)
    f32 = jnp.float32

    def normal(k, shape, scale):
        return jax.random.normal(k, shape, f32) * scale

    x = normal(ks[0], (BATCH, SEQ, D_MODEL), 1.0)
    pre_norm_w = 1.0 + normal(ks[1], (DEPTH, D_MODEL), 0.05)
    post_norm_w = 1.0 + normal(ks[2], (DEPTH, D_MODEL), 0.05)
    w_in = normal(ks[3], (DEPTH, D_MODEL, N_IN), D_MODEL ** -0.5)
    conv_w = normal(ks[4], (DEPTH, CONV_K, 3 * GDN_WIDTH), CONV_K ** -0.5)
    a_log = jnp.log(jax.random.uniform(ks[5], (DEPTH, GDN_HEADS), f32, minval=0.5, maxval=16.0))
    dt = jnp.exp(jax.random.uniform(ks[6], (DEPTH, GDN_HEADS), f32,
                                    minval=math_log(0.001), maxval=math_log(0.1)))
    dt_bias = dt + jnp.log(-jnp.expm1(-dt))
    gdn_norm_w = 1.0 + normal(ks[7], (DEPTH, GDN_HEAD_DIM), 0.05)
    w_branch_sb = normal(ks[8], (DEPTH, SB_WIDTH, D_MODEL), SB_WIDTH ** -0.5)
    w_branch_gdn = normal(ks[9], (DEPTH, GDN_WIDTH, D_MODEL), GDN_WIDTH ** -0.5)
    w_out = normal(ks[10], (DEPTH, D_MODEL, D_MODEL), D_MODEL ** -0.5)
    return {"x": x, "pre_norm_w": pre_norm_w, "post_norm_w": post_norm_w, "w_in": w_in,
            "conv_w": conv_w, "a_log": a_log, "dt_bias": dt_bias, "gdn_norm_w": gdn_norm_w,
            "w_branch_sb": w_branch_sb, "w_branch_gdn": w_branch_gdn, "w_out": w_out}

def math_log(v):
    return float(np.log(v))

def first_block(x, pre_norm_w, post_norm_w, w_in, conv_w, a_log, dt_bias, gdn_norm_w,
              w_branch_sb, w_branch_gdn, w_out):
    for layer in range(DEPTH):
        x = hybrid_layer(x, pre_norm_w[layer], post_norm_w[layer], w_in[layer], conv_w[layer],
                         a_log[layer], dt_bias[layer], gdn_norm_w[layer],
                         w_branch_sb[layer], w_branch_gdn[layer], w_out[layer])
    return x


DIFF_HEADS = 4
DIFF_HEAD_DIM = 64
DIFF_WIDTH = DIFF_HEADS * 2 * DIFF_HEAD_DIM
FOX_HEADS = 8
FOX_HEAD_DIM = 64
FOX_WIDTH = FOX_HEADS * FOX_HEAD_DIM
MIX_WIDTH = DIFF_WIDTH + FOX_WIDTH
IN_COLS = 3 * DIFF_WIDTH + 3 * FOX_WIDTH + FOX_HEADS
D_FF = 4 * D_MODEL
N_BUCKETS = 32
MAX_DISTANCE = 128
Q_BLOCK = 128
NEG = -1e30


def rmsnorm(x, g):
    xf = x.astype(jnp.float32)
    y = xf * lax.rsqrt(jnp.mean(xf * xf, axis=-1, keepdims=True) + EPS)
    return (y * g.astype(jnp.float32)).astype(x.dtype)

def t5_bucket(dist):
    max_exact = N_BUCKETS // 2
    d = jnp.maximum(dist, 1).astype(jnp.float32)
    large = max_exact + (jnp.log(d / max_exact) / math.log(MAX_DISTANCE / max_exact)
                         * (N_BUCKETS - max_exact))
    large = jnp.minimum(large.astype(jnp.int32), N_BUCKETS - 1)
    return jnp.where(dist < max_exact, dist, large)

def token_mixer(h, w_in, b_f, lam_q1, lam_k1, lam_q2, lam_k2, subln_g, rel_bias, lambda_init):
    B, S, _ = h.shape
    proj = h @ w_in
    o = 0
    dq = proj[..., o:o + DIFF_WIDTH].reshape(B, S, 2 * DIFF_HEADS, DIFF_HEAD_DIM); o += DIFF_WIDTH
    dk = proj[..., o:o + DIFF_WIDTH].reshape(B, S, 2 * DIFF_HEADS, DIFF_HEAD_DIM); o += DIFF_WIDTH
    dv = proj[..., o:o + DIFF_WIDTH].reshape(B, S, DIFF_HEADS, 2 * DIFF_HEAD_DIM); o += DIFF_WIDTH
    fq = proj[..., o:o + FOX_WIDTH].reshape(B, S, FOX_HEADS, FOX_HEAD_DIM); o += FOX_WIDTH
    fk = proj[..., o:o + FOX_WIDTH].reshape(B, S, FOX_HEADS, FOX_HEAD_DIM); o += FOX_WIDTH
    fv = proj[..., o:o + FOX_WIDTH].reshape(B, S, FOX_HEADS, FOX_HEAD_DIM); o += FOX_WIDTH
    f_logit = proj[..., o:o + FOX_HEADS].astype(jnp.float32) + b_f.astype(jnp.float32)
    cum = jnp.cumsum(jax.nn.log_sigmoid(f_logit), axis=1)
    cum_k = jnp.transpose(cum, (0, 2, 1))

    lam = (jnp.exp(jnp.sum(lam_q1.astype(jnp.float32) * lam_k1.astype(jnp.float32)))
           - jnp.exp(jnp.sum(lam_q2.astype(jnp.float32) * lam_k2.astype(jnp.float32)))
           + lambda_init)

    dist_bias = rel_bias[t5_bucket(jnp.arange(S))]
    kpos = jnp.arange(S)
    nb = S // Q_BLOCK

    def to_blocks(a):
        return jnp.swapaxes(a.reshape(B, nb, Q_BLOCK, *a.shape[2:]), 0, 1)

    def block(args):
        i, qd, qf, cq = args
        qpos = i * Q_BLOCK + jnp.arange(Q_BLOCK)
        rel = qpos[:, None] - kpos[None, :]
        causal = rel >= 0
        sd = jnp.einsum('bqhd,bkhd->bhqk', qd, dk).astype(jnp.float32) * (DIFF_HEAD_DIM ** -0.5)
        bias = jnp.transpose(dist_bias[jnp.maximum(rel, 0)], (2, 0, 1)).astype(jnp.float32)
        sd = sd.reshape(B, DIFF_HEADS, 2, Q_BLOCK, S) + bias[:, None]
        pd = jax.nn.softmax(jnp.where(causal, sd, NEG), axis=-1)
        ad = pd[:, :, 0] - lam * pd[:, :, 1]
        od = jnp.einsum('bhqk,bkhe->bqhe', ad.astype(dv.dtype), dv)
        od = rmsnorm(od, subln_g) * (1.0 - lambda_init)
        sf = jnp.einsum('bqhd,bkhd->bhqk', qf, fk).astype(jnp.float32) * (FOX_HEAD_DIM ** -0.5)
        sf = sf + jnp.transpose(cq, (0, 2, 1))[..., :, None] - cum_k[..., None, :]
        pf = jax.nn.softmax(jnp.where(causal, sf, NEG), axis=-1)
        of = jnp.einsum('bhqk,bkhd->bqhd', pf.astype(fv.dtype), fv)
        return jnp.concatenate([od.reshape(B, Q_BLOCK, DIFF_WIDTH),
                                of.reshape(B, Q_BLOCK, FOX_WIDTH)], axis=-1)

    out = lax.map(block, (jnp.arange(nb), to_blocks(dq), to_blocks(fq), to_blocks(cum)))
    return jnp.swapaxes(out, 0, 1).reshape(B, S, MIX_WIDTH)

def second_inputs(seed: int = 0) -> dict:
    key = jax.random.key(seed)
    ks = jax.random.split(key, 20)
    f32 = jnp.float32
    nrm = lambda k, shape, s: jax.random.normal(k, shape, f32) * s
    return {
        "x": jax.random.normal(ks[0], (BATCH, SEQ, D_MODEL), f32),
        "ln_attn_pre": 1.0 + nrm(ks[1], (DEPTH, D_MODEL), 0.05),
        "w_in": nrm(ks[2], (DEPTH, D_MODEL, IN_COLS), D_MODEL ** -0.5),
        "b_f": 2.0 + nrm(ks[3], (DEPTH, FOX_HEADS), 0.1),
        "lam_q1": nrm(ks[4], (DEPTH, DIFF_HEAD_DIM), 0.1),
        "lam_k1": nrm(ks[5], (DEPTH, DIFF_HEAD_DIM), 0.1),
        "lam_q2": nrm(ks[6], (DEPTH, DIFF_HEAD_DIM), 0.1),
        "lam_k2": nrm(ks[7], (DEPTH, DIFF_HEAD_DIM), 0.1),
        "subln_g": 1.0 + nrm(ks[8], (DEPTH, 2 * DIFF_HEAD_DIM), 0.05),
        "rel_bias": nrm(ks[9], (N_BUCKETS, DIFF_HEADS), 0.5),
        "w_out": nrm(ks[10], (DEPTH, MIX_WIDTH, D_MODEL), MIX_WIDTH ** -0.5),
        "ln_attn_post": 1.0 + nrm(ks[11], (DEPTH, D_MODEL), 0.05),
        "ln_mlp_pre": 1.0 + nrm(ks[12], (DEPTH, D_MODEL), 0.05),
        "w_up": nrm(ks[13], (DEPTH, D_MODEL, D_FF), D_MODEL ** -0.5),
        "w_down": nrm(ks[14], (DEPTH, D_FF, D_MODEL), D_FF ** -0.5),
        "ln_mlp_post": 1.0 + nrm(ks[15], (DEPTH, D_MODEL), 0.05),
    }

def second_block(x, ln_attn_pre, w_in, b_f, lam_q1, lam_k1, lam_q2, lam_k2, subln_g, rel_bias,
              w_out, ln_attn_post, ln_mlp_pre, w_up, w_down, ln_mlp_post):
    for l in range(DEPTH):
        lambda_init = 0.8 - 0.6 * math.exp(-0.3 * l)
        h = rmsnorm(x, ln_attn_pre[l])
        mix = token_mixer(h, w_in[l], b_f[l], lam_q1[l], lam_k1[l], lam_q2[l], lam_k2[l],
                          subln_g[l], rel_bias, lambda_init)
        x = x + rmsnorm(mix @ w_out[l], ln_attn_post[l])
        h = rmsnorm(x, ln_mlp_pre[l])
        u = jnp.square(jax.nn.relu(h @ w_up[l]))
        x = x + rmsnorm(u @ w_down[l], ln_mlp_post[l])
    return x


def setup_inputs(seed=0):
    out = dict(first_inputs(seed))
    for name, value in second_inputs(seed + 1).items():
        if name != "x":
            out[name + "_2"] = value
    return out


def reference(
    x, pre_norm_w, post_norm_w, w_in, conv_w, a_log, dt_bias, gdn_norm_w, w_branch_sb,
    w_branch_gdn, w_out, ln_attn_pre_2, w_in_2, b_f_2, lam_q1_2, lam_k1_2, lam_q2_2, lam_k2_2,
    subln_g_2, rel_bias_2, w_out_2, ln_attn_post_2, ln_mlp_pre_2, w_up_2, w_down_2,
    ln_mlp_post_2,
):
    x = first_block(
        x, pre_norm_w, post_norm_w, w_in, conv_w, a_log, dt_bias, gdn_norm_w, w_branch_sb,
        w_branch_gdn, w_out,
    )
    return second_block(
        x, ln_attn_pre_2, w_in_2, b_f_2, lam_q1_2, lam_k1_2, lam_q2_2, lam_k2_2, subln_g_2,
        rel_bias_2, w_out_2, ln_attn_post_2, ln_mlp_pre_2, w_up_2, w_down_2, ln_mlp_post_2,
    )


_drawn_inputs = setup_inputs


def setup_inputs(seed=0):
    import zlib

    import numpy as np

    out = dict(_drawn_inputs(seed))
    spreads = {}
    factors = {'b_f_2': 39.216, 'lam_q1_2': 26.158, 'lam_k1_2': 2.782, 'lam_q2_2': 8.0, 'lam_k2_2': 8.0}
    for name, (base, spread) in spreads.items():
        noise = np.random.default_rng([zlib.crc32(name.encode()), seed]).standard_normal(out[name].shape)
        drawn = base * np.exp(spread * noise) if base else spread * noise
        out[name] = __import__('jax').numpy.asarray(drawn.astype(out[name].dtype))
    for name, factor in factors.items():
        out[name] = (out[name] * factor).astype(out[name].dtype)
    return out
```

```python
from contextlib import contextmanager

import numpy as np

import concourse.bass as bass
from concourse import mybir

F32 = mybir.dt.float32
F32R = mybir.dt.float32r
ALU = mybir.AluOpType
ACT = mybir.ActivationFunctionType
AXX = mybir.AxisListType.X
ET = mybir.EngineType

P = 128
EPS = 1e-6
NEG = -1e30


class Counts:

    def __init__(self, nc, per):
        self.nc, self.per, self.found = nc, per, {}
        self.all, self.loop = [], None

    @contextmanager
    def fori(self, name, start, end, engines):
        with self.nc.Fori(start, end, engines=engines) as i:
            self.loop = (name, i, start)
            yield i
        for c in self.all:
            self.found[(name, c.name)] = c.local
            c.base, c.local = c.base + (end - start) * c.local, 0
        self.loop = None


class Count:
    def __init__(self, counts, name):
        self.counts, self.name, self.base, self.local = counts, name, 0, 0
        counts.all.append(self)

    def add(self, k=1):
        if self.counts.loop:
            self.local += k
        else:
            self.base += k

    def value(self):
        if not self.counts.loop:
            return self.base
        name, i, start = self.counts.loop
        per = self.counts.per.get((name, self.name), 0)
        least = self.base + self.local - start * per
        return i * per + least if per else least

    def zero(self):
        return self.base == 0 and self.local == 0


class Signal:

    def __init__(self, counts, name, step=1):
        self.sem, self.count, self.step = counts.nc.alloc_semaphore(name), Count(counts, name), step

    def prime(self, engine):
        assert self.step == 1
        engine.e.sem_inc(self.sem, 1)
        self.count.add(1)

    def by(self, instruction):
        instruction.then_inc(self.sem, self.step)
        self.count.add(self.step)
        return self.now()

    def now(self):
        return None if self.count.zero() else (self.sem, self.count.value(), self.count.base + self.count.local, self.count.counts.loop)


class Engine:

    def __init__(self, counts, engine, name):
        self.e, self.done, self.counts = engine, Signal(counts, name), counts
        self.waited = {}

    def did(self, instruction):
        return self.done.by(instruction)

    def now(self):
        return self.done.now()

    def wait(self, *signals):
        for s in signals:
            if s is None:
                continue
            sem, value, order, loop = s
            key = (id(sem), loop[0] if loop else None)
            if self.waited.get(key, -1) >= order and (loop is None) == (self.counts.loop is None):
                continue
            self.waited[key] = order
            self.e.wait_ge(sem, value)

    def hold(self, carrier):
        self.e.sem_inc(carrier, 1)

    def forget(self):
        self.waited = {}


def weave(main, others, every=1):
    others, n = list(others), 0
    for _ in main:
        n += 1
        if n % every == 0:
            for o in list(others):
                if next(o, StopIteration) is StopIteration:
                    others.remove(o)
    while others:
        for o in list(others):
            if next(o, StopIteration) is StopIteration:
                others.remove(o)


MATS = ["ident", "upper", "after", "negtri", "ones", "negones", "causal", "before", "notbefore"]
LEVELS = 7


def bucket(dist, n_buckets=32, max_distance=128):
    exact = n_buckets // 2
    d = np.maximum(dist, 1).astype(np.float32)
    large = exact + np.log(d / np.float32(exact)) / np.float32(np.log(max_distance / exact)) * (n_buckets - exact)
    large = np.minimum(large.astype(np.int32), n_buckets - 1)
    return np.where(dist < exact, dist, large)


def shape_constants():
    p, f = np.arange(P)[:, None], np.arange(P)[None, :]
    mats = {
        "ident": p == f, "upper": p <= f, "after": p > f, "negtri": -1.0 * (p >= f),
        "ones": np.ones((P, P)), "negones": -np.ones((P, P)), "causal": np.where(f > p, NEG, 0.0),
        "before": p < f, "notbefore": np.where(p >= f, NEG, 0.0),
    }
    out = [np.asarray(mats[m], np.float32) for m in MATS]

    def level(l, row, col):
        same = (row >> (l + 1)) == (col >> (l + 1))
        return (same & ((row >> l) % 2 == 1) & ((col >> l) % 2 == 0)).astype(np.float32)

    out.append(level(0, p, f))
    out += [level(l, f, p) for l in range(LEVELS)]
    return np.concatenate(out, axis=1)


def bias_constants():
    m = np.arange(384)
    hot = (bucket(np.maximum(255 - m, 0))[None, :] == np.arange(32)[:, None]).astype(np.float32)
    pick = np.zeros((32, 8, P), np.float32)
    for h in range(8):
        pick[h, h, :] = -1.0
    return np.concatenate([hot, pick.reshape(32, 8 * P)], axis=1)


def program(nc, t, out, per, stop=None, dbg=None):
    T, D = t["x"].shape[1:]
    NT, KT = T // P, D // P
    dma_counts = Counts(nc, per)
    counts = Counts(nc, per)
    PE = Engine(counts, nc.tensor, "pe_done")
    A = Engine(counts, nc.scalar, "act_done")
    V = Engine(counts, nc.vector, "dve_done")
    G = Engine(counts, nc.gpsimd, "pool_done")
    engines = [PE, A, V, G]
    pe, act, dve, pool = nc.tensor, nc.scalar, nc.vector, nc.gpsimd
    compute = [ET.Pool, ET.Activation, ET.PE, ET.DVE]

    @contextmanager
    def loop(name, start, end):
        for e in engines:
            e.forget()
        with counts.fori(name, start, end, compute) as i:
            yield i
        for e in engines:
            e.forget()

    base = 16512
    cursor = [base]

    def at(name, address, shape, dt=F32):
        return nc.alloc_sbuf_tensor_at(name, shape, dt, offset=address, align_bytes=4).ap()

    def region(nbytes):
        a = cursor[0]
        cursor[0] += nbytes
        return a

    KB = 1024
    hT = at("hT", region(32 * KB), [P, 2, KT, T], F32R)
    ring = at("ring", region(32 * KB), [P, 4, 2, 1024], F32R)
    raw_ring = at("raw_ring", region(16 * KB), [P, 4, 1024])
    r_res = region(16 * KB)
    x1 = at("x1", r_res, [P, NT, D])
    consts = at("consts", region(17 * 512), [P, 17, P])
    small = region(5 * 512)
    r4 = cursor[0]
    mat = {m: consts[:, n, :] for n, m in enumerate(MATS)}
    ident = mat["ident"]
    level0, levelT = consts[:, len(MATS), :], [consts[:, len(MATS) + 1 + l, :] for l in range(LEVELS)]
    so = [small]

    def little(name, cols):
        a = at(name, so[0], [P, cols])
        so[0] += 4 * cols
        return a

    colp = little("colp", 80)
    eps_c, one_c = little("eps_c", 1), little("one_c", 1)
    lam_c = little("lam_c", 1)
    gates = little("gates", 80).rearrange("p (h k c) -> p h k c", h=4, k=5)
    hs = little("hs", 20).rearrange("p (k c) -> p k c", k=5)
    cw = little("cw", 12).rearrange("p (k i) -> p k i", k=3)
    dtb, alog = little("dtb", 4), little("alog", 4)
    bfb = little("bfb", 8)
    stat = little("stat", 64)
    fl = little("fl", 32).rearrange("p (t h) -> p t h", t=4)
    wab = little("wab", 64)
    assert so[0] <= small + 5 * 512
    conv_col = colp[:, 0:48].rearrange("p (i k h) -> p k i h", i=4, k=3)
    prew_col, aprew_col, mprew_col, gnw_col = colp[:, 48:56], colp[:, 56:64], colp[:, 64:72], colp[:, 72:73]

    banks = [nc.alloc_psum_tensor(f"bank{b}", [P, 512], F32).ap() for b in range(8)]

    def v4(x):
        return x.rearrange("p (c f) -> p c f", c=4)

    def over4(m):
        return m.unsqueeze(1).broadcast_to([P, 4, P])

    def along(c4):
        return c4.unsqueeze(2).broadcast_to([P, 4, P])

    w1, w2 = t["w_in"], t["w_in_2"]
    filled = [Signal(counts, f"slab{s}_filled", 16) for s in range(4)]
    hi_done = [Signal(counts, f"slab{s}_hi") for s in range(4)]
    lo_done = [Signal(counts, f"slab{s}_lo") for s in range(4)]
    used = [Signal(counts, f"slab{s}_used") for s in range(4)]
    fills = [Count(dma_counts, f"fills{s}") for s in range(4)]

    sp_waited = nc.alloc_semaphore("sp_waited")

    def fill(s, parts):
        if not fills[s].zero():
            nc.sync.wait_ge(lo_done[s].sem, fills[s].value())
            nc.sync.sem_inc(sp_waited, 1)
        fills[s].add()
        for dst, src in parts:
            nc.sync.dma_start(dst, src).then_inc(filled[s].sem, 16)

    def cols(w, c0, k0=0):
        return w[0].rearrange("(k p) n -> p k n", p=P)[:, k0:k0 + 4, bass.ds(c0, P)]

    def tall(s, w, c0):
        fill(s, [(k8(s)[:, 0:4, :], cols(w, c0)), (k8(s)[:, 4:8, :], cols(w, c0, 4))])

    def wide(s, w, k0, c0):
        rows = w[0].rearrange("(k p) n -> p k n", p=P)
        fill(s, [(k2(s)[:, j:j + 1, :], rows[:, bass.ds(k0 + j, 1), c0:c0 + 512]) for j in range(2)])

    def slot(s):
        return raw_ring[:, s, :]

    def k8(s):
        return slot(s).rearrange("p (k n) -> p k n", k=8)

    def k2(s):
        return slot(s).rearrange("p (k n) -> p k n", k=2)

    A_COLS = [2048, 2560, 3072, 3584, 0, 512, 1024, 1536]
    B_COLS = [0, 512, 1024, 1536, 2048, 2560]
    MERGE0 = 4104

    boot = [Signal(counts, "boot_x", 16), Signal(counts, "boot_small", 16)]
    stage = at("stage", r4, [P, P])
    xnat = x1
    for j in range(NT):
        boot[0].by(nc.sync.dma_start(xnat[:, j, :], t["x"][0, j * P:(j + 1) * P, :]))
    b1 = boot[1]
    row = 0
    for name, n in (("conv_w", 48), ("pre_norm_w", 8), ("ln_attn_pre_2", 8), ("ln_mlp_pre_2", 8), ("gdn_norm_w", 1)):
        src = t[name]
        flat = src.rearrange("a i (n c) -> (a i n) c", c=P) if len(src.shape) == 3 else src.rearrange("a (n c) -> (a n) c", c=P)
        b1.by(nc.scalar.dma_start(stage[row:row + n, :], flat))
        row += n
    b1.by(nc.scalar.dma_start(consts.rearrange("p a b -> p (a b)"), t["shape_consts"]))
    b1.by(nc.scalar.dma_start(dtb, t["dt_bias"][0].partition_broadcast(P)))
    b1.by(nc.scalar.dma_start(alog, t["a_log"][0].partition_broadcast(P)))
    b1.by(nc.scalar.dma_start(bfb, t["b_f_2"][0].partition_broadcast(P)))
    lam_v = []
    for n, name in enumerate(("lam_q1_2", "lam_k1_2", "lam_q2_2", "lam_k2_2")):
        lam_v.append(at(name + "_b", r4 + 1024 + 256 * n, [P, 64]))
        lamv = lam_v[-1]
        b1.by(nc.scalar.dma_start(lamv, t[name][0].partition_broadcast(P)))
    b1.by(nc.scalar.dma_start(wab.rearrange("p (k n) -> p k n", k=8),
                              w1[0].rearrange("(k p) n -> p k n", p=P)[:, :, 4096:4104]))

    def sp_stream():
        n = [0]

        def nxt():
            n[0] += 1
            return (n[0] - 1) % 4

        for c in A_COLS:
            s = nxt()
            tall(s, w1, c)
        with dma_counts.fori("slabs_a", 1, 4, [ET.SP]) as i:
            for c in A_COLS:
                s = nxt()
                tall(s, w1, i * P + c)
        with dma_counts.fori("slabs_merge", 0, 4, [ET.SP]) as i:
            for c in range(4):
                s = nxt()
                tall(s, w1, i * 512 + (MERGE0 + c * P))
        if stop == "A":
            for c in range(2):
                s = nxt()
                fill(s, [(k8(s)[:, 0:4, :], cols(t["w_branch_sb"], c * P)),
                         (k8(s)[:, 4:8, :], cols(t["w_branch_gdn"], c * P))])
            return
        with dma_counts.fori("slabs_branch", 0, 2, [ET.SP]) as i:
            for c in range(4):
                s = nxt()
                fill(s, [(k8(s)[:, 0:4, :], cols(t["w_branch_sb"], i * 512 + c * P)),
                         (k8(s)[:, 4:8, :], cols(t["w_branch_gdn"], i * 512 + c * P))])
        for half in range(2):
            for kk in range(4):
                s = nxt()
                wide(s, t["w_out"], 2 * kk, half * 512)
        for i in range(1):
            for n_, c in enumerate(B_COLS[:2] if stop == "Y" else B_COLS):
                tall(n_ % 4, w2, c)
        if stop == "Y":
            return
        with dma_counts.fori("slabs_b", 1, 4, [ET.SP]) as i:
            for n_, c in enumerate(B_COLS):
                tall(n_ % 4, w2, i * P + c)
        for half in range(2):
            for kk in range(4):
                if stop == "M" and (half or kk > 1):
                    break
                s = nxt()
                wide(s, t["w_out_2"], 2 * kk, half * 512)
        if stop == "M":
            return
        with dma_counts.fori("slabs_up", 0, 8, [ET.SP]) as i:
            for c in range(4):
                s = nxt()
                tall(s, t["w_up_2"], i * 512 + c * P)
        for half in range(2):
            with dma_counts.fori(f"slabs_down{half}", 0, 4, [ET.SP]) as i:
                for c in range(4):
                    s = nxt()
                    wide(s, t["w_down_2"], i * 8 + 2 * c, half * 512)

    sp_stream()

    n_split = [0]
    TOTAL = 10 ** 9

    def split(s):
        filled[s].count.add(32)
        A.wait((filled[s].sem, filled[s].count.value(), filled[s].count.base + filled[s].count.local, counts.loop))
        A.wait(used[s].now())
        h = hi_done[s].by(act.copy(ring[:, s, 0, :], slot(s)))
        G.wait(h)
        lo_done[s].by(pool.tensor_tensor(ring[:, s, 1, :], slot(s), ring[:, s, 0, :].bitcast(F32), ALU.subtract))

    acc_free = [Signal(counts, f"acc{b}_free") for b in range(2)]

    def product(s, acc, terms, pieces=4, first_wait=(), opened=False):
        PE.wait(lo_done[s].now(), *first_wait)
        n = len(terms)
        for j, (o, l, r, a, b) in enumerate(terms):
            m = pe.matmul(o, l, r, start=a, stop=b, skip_group_check=opened)
            if j == n - 1:
                used[s].by(m)
            elif (j + 1) % (n // pieces) == 0:
                yield
        yield

    def terms_T(s, acc, ks=range(8), src=None):
        src = hT if src is None else src
        w = ring[:, s].rearrange("p two (k n) -> p two k n", k=8)
        out_ = []
        ks = list(ks)
        for n, (kw, kx) in enumerate(ks):
            for m, (a, b) in enumerate(((0, 0), (0, 1), (1, 0))):
                out_.append((acc, w[:, a, kw, :], src[:, b, kx, :], n == 0 and m == 0, n == len(ks) - 1 and m == 2))
        return out_

    all_k = [(k, k) for k in range(KT)]

    def ahead(s):
        split(s)

    b1_all = b1.now()
    x_all = boot[0].now()
    act.preload_act_table_set("natural_log_exp_and_others")
    V.did(dve.memset(eps_c, EPS))
    V.did(dve.memset(one_c, 1.0))
    half_c = little("half_c", 4)
    neghalf = V.did(dve.memset(half_c, -0.5))

    PE.wait(b1_all)
    A.wait(neghalf)
    tok = PE.did(pe.transpose(banks[2][:, 0:row], stage[0:row, :], ident[0:row, 0:row]))
    V.wait(tok)
    V.did(dve.tensor_copy(colp[:, 0:row], banks[2][:, 0:row]))
    V.wait(b1_all)
    lq1, lk1, lq2, lk2 = lam_v
    V.did(dve.tensor_tensor(lq1, lq1, lk1, ALU.mult))
    tok = V.did(dve.tensor_tensor(lq2, lq2, lk2, ALU.mult))
    V.wait(tok)
    V.did(dve.tensor_reduce(stat[:, 60:61], lq1, AXX, ALU.add))
    tok = V.did(dve.tensor_reduce(stat[:, 61:62], lq2, AXX, ALU.add))
    A.wait(tok)
    tok = A.did(act.activation(stat[:, 62:64], stat[:, 60:62], ACT.Exp))
    V.wait(tok)
    tok = V.did(dve.tensor_tensor(lam_c, stat[:, 62:63], stat[:, 63:64], ALU.subtract))
    V.wait(tok)
    lam_init = 0.8 - 0.6 * float(np.exp(-0.3 * 0))
    V.did(dve.tensor_scalar(lam_c, lam_c, lam_init, None, ALU.add))

    pool_held = nc.alloc_semaphore("pool_held")

    def rstd(dst, total, n, ready):
        G.wait(ready)
        if counts.loop:
            G.hold(pool_held)
        a = G.did(pool.tensor_scalar(dst, total, 1.0 / n, EPS, ALU.mult, ALU.add))
        G.wait(a)
        w = dst.shape[1]
        return G.did(pool.tensor_tensor(dst, dst, half_c[:, 0:1].broadcast_to([P, w]) if w > 1 else half_c[:, 0:1], ALU.pow))

    def norm_transpose(src, weight_col, scratch, src_ready, stats, norm_banks=(2, 3, 4, 5)):
        toks = []
        for j in range(NT):
            A.wait(src_ready[j])
            toks.append(A.did(act.activation(scratch[:, j, :], src[:, j, :], ACT.Square, accum_out=stats[:, j:j + 1])))
        scaled = []
        for j in range(NT):
            r = rstd(stats[:, j:j + 1], stats[:, j:j + 1], D, toks[j])
            V.wait(r)
            scaled.append(V.did(dve.tensor_scalar(scratch[:, j, :], src[:, j, :], stats[:, j:j + 1], None, ALU.mult)))
        free = {b: None for b in norm_banks}
        last = None
        for k in range(KT):
            b = norm_banks[k % len(norm_banks)]
            PE.wait(free[b], scaled[-1])
            for j in range(NT):
                m = pe.transpose(banks[b][:, j * P:(j + 1) * P], scratch[:, j, k * P:(k + 1) * P], ident)
            tp = PE.did(m)
            A.wait(tp)
            h = A.did(act.activation(hT[:, 0, k, :], banks[b], ACT.Copy, scale=weight_col[:, k:k + 1]))
            V.wait(h)
            last = free[b] = V.did(dve.scalar_tensor_tensor(hT[:, 1, k, :], banks[b], weight_col[:, k:k + 1],
                                                            hT[:, 0, k, :].bitcast(F32), ALU.mult, ALU.subtract))
        return last

    scr = at("norm_scratch", r4 + 2 * KB, [P, NT, D])
    A.wait(V.now())
    PE.wait(V.now())
    h_ready = norm_transpose(xnat, prew_col, scr, [x_all] * NT, stat[:, 0:4])

    split(0)
    split(1)

    PE.wait(h_ready)
    ab = at("ab", r4 + 20 * KB, [P, 4, 8])
    wab_s = at("wab_s", r4 + 20 * KB + 256, [P, 2, 64], F32R)
    A.wait(b1_all)
    tok = A.did(act.copy(wab_s[:, 0, :], wab))
    V.wait(tok)
    tok = V.did(dve.tensor_tensor(wab_s[:, 1, :], wab, wab_s[:, 0, :].bitcast(F32), ALU.subtract))
    PE.wait(tok)
    wabk = wab_s.rearrange("p two (k n) -> p two k n", k=8)

    def narrow(acc, w, n):
        for j in range(NT):
            for k in range(KT):
                for m, (a, b) in enumerate(((0, 0), (0, 1), (1, 0))):
                    q = pe.matmul(acc[:, j * n:(j + 1) * n], hT[:, b, k, j * P:(j + 1) * P], w[:, a, k, :],
                                  start=k == 0 and m == 0, stop=k == KT - 1 and m == 2)
        return PE.did(q)

    tok = narrow(banks[6], wabk, 8)
    V.wait(tok)
    tok = V.did(dve.tensor_copy(ab, banks[6][:, 0:32].rearrange("p (c n) -> p c n", c=4)))
    V.wait(tok, b1_all)
    sp_z = at("sp_z", r4 + 21 * KB, [P, 4, 4])
    sp_e = at("sp_e", r4 + 21 * KB + 64, [P, 4, 4])
    be = at("be", r4 + 21 * KB + 128, [P, 4, 4])
    ea = at("ea", r4 + 21 * KB + 192, [P, 4])
    tok = V.did(dve.tensor_tensor(sp_z, ab[:, :, 0:4], dtb.unsqueeze(1).broadcast_to([P, 4, 4]), ALU.add))
    V.wait(tok)
    A.wait(tok)
    tok = A.did(act.activation(sp_e, sp_z, ACT.Abs))
    A.wait(tok)
    tok = A.did(act.activation(sp_e, sp_e, ACT.Exp, scale=-1.0))
    A.wait(tok)
    A.did(act.activation(sp_e, sp_e, ACT.Ln, bias=one_c))
    A.did(act.activation(ea, alog, ACT.Exp))
    tok = A.did(act.activation(be, ab[:, :, 4:8], ACT.Exp, scale=-1.0))
    V.wait(tok)
    tok = V.did(dve.scalar_tensor_tensor(sp_z, sp_z, 0.0, sp_e, ALU.max, ALU.add))
    V.did(dve.tensor_scalar(be, be, 1.0, None, ALU.add))
    tok = V.now()
    V.wait(tok)
    V.did(dve.scalar_tensor_tensor(gates[:, :, 0, :].rearrange("p h c -> p c h"), sp_z, -1.0,
                                   ea.unsqueeze(1).broadcast_to([P, 4, 4]), ALU.mult, ALU.mult))
    tok = V.did(dve.reciprocal(gates[:, :, 1, :].rearrange("p h c -> p c h"), be))
    g_all = gates[:, :, 0, :]
    PE.wait(tok)
    gb = banks[7].rearrange("p (a n) -> p a n", a=8)
    for n, m in enumerate(("upper", "after", "ones")):
        q = pe.matmul(gb[:, n, 0:16].rearrange("p (h c) -> p h c", h=4), mat[m], g_all, start=True, stop=True)
    tok = PE.did(q)
    A.wait(tok)
    for n in range(3):
        tok = A.did(act.activation(gates[:, :, 2 + n, :], gb[:, n, 0:16].rearrange("p (h c) -> p h c", h=4), ACT.Exp))
    V.wait(tok)
    gates_ready = V.did(dve.tensor_tensor(gates[:, :, 2, :], gates[:, :, 2, :], gates[:, :, 1, :], ALU.mult))

    off = [r4]

    def take(name, shape, dt=F32):
        n = int(np.prod(shape[1:])) * 4
        a = at(name, off[0], shape, dt)
        off[0] += n
        return a

    osb = take("osb", [P, 2, 4, T], F32R)
    ogd = take("ogd", [P, 2, 4, T], F32R)
    r_work = off[0]
    rawA = off[0]
    cin = take("cin", [P, 3, T + 4])
    rawg = take("rawg", [P, T])
    rawsb = take("rawsb", [P, 4, T])
    gbuf = [take(f"g{n}", [P, T]) for n in range(16)]
    sbuf_ = [take(f"s{n}", [P, T]) for n in range(9)]
    assert off[0] <= nc.sbuf_usable_end, off[0] - r4

    for e in engines:
        for o in engines:
            e.wait(o.now())
    zeros = V.did(dve.memset(cin[:, :, 0:4], 0.0))

    raw_tiles = [cin[:, 0, 3:3 + T], cin[:, 1, 3:3 + T], cin[:, 2, 3:3 + T], rawg] + [rawsb[:, n, :] for n in range(4)]

    def project(tiles, slots, reads, nslab):
        for n, dst in enumerate(tiles):
            s, b = slots[n], n % 2
            yield from product(s, banks[b], terms_T(s, banks[b], all_k), first_wait=(acc_free[b].now(),))
            split((s + 2) % 4)
            assert reads is None or n in reads, n
            A.wait(used[s].now(), reads[n] if reads else None)
            acc_free[b].by(act.copy(dst, banks[b]))

    def fence(main_only=False):
        marks = [e.now() for e in engines] + [a.now() for a in acc_free]
        return marks

    def sigmoid(dst, x, ready):
        A.wait(ready)
        a = A.did(act.activation(dst, x, ACT.Abs))
        A.wait(a)
        a = A.did(act.activation(dst, dst, ACT.Exp, scale=-1.0))
        A.wait(a)
        a = A.did(act.activation(dst, dst, ACT.Ln, bias=one_c))
        V.wait(a)
        b = V.did(dve.scalar_tensor_tensor(dst, x, 0.0, dst, ALU.min, ALU.subtract))
        A.wait(b)
        return A.did(act.activation(dst, dst, ACT.Exp))

    def silu(x, tmp, ready, to=None):
        c = sigmoid(tmp, x, ready)
        V.wait(c)
        return V.did(dve.tensor_tensor(x if to is None else to, x, tmp, ALU.mult))

    def delta_head(i, reads, marks):
        qT, kT, bv, bk, kd, qg, intra, MT, Ca, Cb, X, XT, PP, misc, tmp, gate = gbuf
        S, sg = misc[:, 0:P], misc
        for e in engines:
            e.wait(*marks)
        V.did(dve.tensor_copy(hs, gates[:, i]))
        tok = V.did(dve.tensor_copy(cw, conv_col[:, :, :, i]))
        V.wait(tok)
        conv = {}
        for n, dst in enumerate((qT, kT, PP)):
            tok = V.did(dve.tensor_scalar(dst, cin[:, n, 0:T], cw[:, n, 0:1], None, ALU.mult))
            for j in range(1, 4):
                V.wait(tok)
                tok = V.did(dve.scalar_tensor_tensor(dst, cin[:, n, j:j + T], cw[:, n, j:j + 1], dst, ALU.mult, ALU.add))
            reads[n] = tok
            conv[n] = tok
            if n < 2:
                yield
        cq = silu(qT, tmp, conv[0])
        ck = silu(kT, XT, conv[1])
        cv = silu(PP, X, conv[2])
        reads[3] = silu(rawg, gate, None, gate)
        yield
        for n, (x, ready, bank, scale) in enumerate(((qT, cq, 5, P ** -0.5), (kT, ck, 6, 1.0))):
            sq = (tmp, XT)[n]
            A.wait(ready)
            a = A.did(act.activation(sq, x, ACT.Square))
            PE.wait(a)
            p_ = PE.did(pe.matmul(banks[bank], mat["ones"], sq, start=True, stop=True))
            yield
            A.wait(p_)
            a = A.did(act.activation(sq, banks[bank], ACT.Ln, bias=eps_c))
            A.wait(a)
            a = A.did(act.activation(sq, sq, ACT.Exp, scale=-0.5))
            V.wait(a)
            tok = V.did(dve.scalar_tensor_tensor(x, x, scale, sq, ALU.mult, ALU.mult))
        normed = tok
        G.wait(cv, normed)
        G.did(pool.tensor_tensor(v4(X), over4(mat["upper"]), along(hs[:, 0, :]), ALU.mult))
        ug = G.now()
        slg = G.did(pool.tensor_tensor(v4(XT), over4(mat["after"]), along(hs[:, 0, :]), ALU.mult))
        PE.wait(normed)
        for c in range(4):
            m = pe.transpose(banks[7][:, c * P:(c + 1) * P], kT[:, c * P:(c + 1) * P], ident)
        p_ = PE.did(m)
        V.wait(p_)
        V.did(dve.tensor_tensor(v4(bk), v4(banks[7]), along(hs[:, 2, :]), ALU.mult))
        tok = V.did(dve.tensor_tensor(v4(kd), v4(banks[7]), along(hs[:, 3, :]), ALU.mult))
        yield
        PE.wait(tok, cv)
        for c in range(4):
            m = pe.transpose(banks[7][:, c * P:(c + 1) * P], PP[:, c * P:(c + 1) * P], ident)
        p_ = PE.did(m)
        V.wait(p_)
        vready = V.did(dve.tensor_tensor(v4(bv), v4(banks[7]), along(hs[:, 1, :]), ALU.mult))
        yield
        PE.wait(ug, normed)
        p1 = PE.did(pe.matmul(banks[5], mat["after"], X, start=True, stop=True))
        yield
        A.wait(p1)
        eDT = A.did(act.activation(Ca, banks[5], ACT.Exp))
        PE.wait(slg)
        p2 = PE.did(pe.matmul(banks[6], mat["upper"], XT, start=True, stop=True))
        yield
        A.wait(p2)
        eD = A.did(act.activation(Cb, banks[6], ACT.Exp))
        PE.wait(vready)
        p3 = PE.did(pe.matmul(banks[7], mat["ones"], X, start=True, stop=True))
        yield
        A.wait(p3)
        er = A.did(act.activation(misc, banks[7], ACT.Exp))
        V.wait(er)
        qgr = V.did(dve.tensor_tensor(qg, qT, misc, ALU.mult))
        G.wait(eDT)
        mDT = G.did(pool.tensor_tensor(v4(Ca), v4(Ca), over4(mat["upper"]), ALU.mult))
        G.wait(eD)
        a = G.did(pool.tensor_tensor(v4(Cb), v4(Cb), over4(mat["after"]), ALU.mult))
        G.wait(a)
        mD = G.did(pool.tensor_tensor(v4(Cb), v4(Cb), along(hs[:, 1, :]), ALU.mult))
        PE.wait(eDT)
        for c in range(4):
            k_ = kT[:, c * P:(c + 1) * P]
            m = pe.matmul(banks[5][:, c * P:(c + 1) * P], k_, k_, start=True, stop=True)
        kk = PE.did(m)
        yield
        PE.wait(eD)
        for c in range(4):
            m = pe.matmul(banks[6][:, c * P:(c + 1) * P], kT[:, c * P:(c + 1) * P], qT[:, c * P:(c + 1) * P], start=True, stop=True)
        qk = PE.did(m)
        V.wait(kk, mD, p1, p3)
        mready = V.did(dve.tensor_tensor(X, banks[5], Cb, ALU.mult))
        V.wait(qk, mDT)
        iready = V.did(dve.tensor_tensor(intra, banks[6], Ca, ALU.mult))
        yield
        PE.wait(mready, er)
        for c in range(4):
            m = pe.transpose(banks[7][:, c * P:(c + 1) * P], X[:, c * P:(c + 1) * P], ident)
        p_ = PE.did(m)
        A.wait(p_)
        mt = A.did(act.copy(MT, banks[7]))
        yield
        V.wait(p_, p2)
        a = V.did(dve.tensor_tensor(v4(X), v4(X), over4(level0), ALU.mult))
        V.wait(a)
        V.did(dve.tensor_tensor(v4(X), over4(ident), v4(X), ALU.subtract))
        V.wait(mt)
        a = V.did(dve.tensor_tensor(v4(XT), v4(MT), over4(levelT[0]), ALU.mult))
        V.wait(a)
        xr = V.did(dve.tensor_tensor(v4(XT), over4(ident), v4(XT), ALU.subtract))
        G.wait(mt, iready, mready)
        cm = {}
        Cs = (Ca, Cb)
        for l in (1, 2):
            cm[l] = G.did(pool.tensor_tensor(v4(Cs[l % 2]), v4(MT), over4(levelT[l]), ALU.mult))
        for l in range(1, LEVELS):
            C = Cs[l % 2]
            PE.wait(cm[l], xr)
            for c in range(4):
                f = slice(c * P, (c + 1) * P)
                m = pe.matmul(banks[5][:, f], C[:, f], X[:, f], start=True, stop=True)
            p1 = PE.did(m)
            A.wait(p1)
            pr = A.did(act.copy(PP, banks[5]))
            if l + 2 < LEVELS:
                G.wait(p1)
                cm[l + 2] = G.did(pool.tensor_tensor(v4(C), v4(MT), over4(levelT[l + 2]), ALU.mult))
            yield
            PE.wait(pr)
            for c in range(4):
                f = slice(c * P, (c + 1) * P)
                m = pe.matmul(banks[6][:, f], PP[:, f], XT[:, f], start=True, stop=True)
            p2 = PE.did(m)
            if l < LEVELS - 1:
                for c in range(4):
                    f = slice(c * P, (c + 1) * P)
                    m = pe.matmul(banks[7][:, f], XT[:, f], PP[:, f], start=True, stop=True)
                p3 = PE.did(m)
                V.wait(p3)
                V.did(dve.tensor_tensor(XT, XT, banks[6], ALU.subtract))
                xr = V.did(dve.tensor_tensor(X, X, banks[7], ALU.subtract))
            else:
                V.wait(p2)
                xr = V.did(dve.tensor_tensor(XT, XT, banks[6], ALU.subtract))
            yield
        PE.wait(xr)
        for c in range(4):
            f = slice(c * P, (c + 1) * P)
            m = pe.matmul(banks[5][:, f], XT[:, f], bv[:, f], start=True, stop=True)
        pu = PE.did(m)
        V.wait(pu)
        u, wT = Ca, Cb
        ur = V.did(dve.tensor_copy(u, banks[5]))
        for c in range(4):
            f = slice(c * P, (c + 1) * P)
            m = pe.matmul(banks[7][:, f], bk[:, f], XT[:, f], start=True, stop=True)
        pw = PE.did(m)
        A.wait(pw)
        wr = A.did(act.copy(wT, banks[7]))
        yield
        V.wait(qgr)
        srd = None
        for c in range(4):
            f = slice(c * P, (c + 1) * P)
            if c:
                PE.wait(srd, wr)
                pa = PE.did(pe.matmul(banks[5][:, 0:P], wT[:, f], S, start=True, stop=True))
                V.wait(pa)
                ur = V.did(dve.tensor_tensor(u[:, f], u[:, f], banks[5][:, 0:P], ALU.subtract))
                pe.matmul(banks[7][:, f], S, qg[:, f], start=True, stop=False)
                yield
            PE.wait(ur, iready, wr)
            po = PE.did(pe.matmul(banks[7][:, f], u[:, f], intra[:, f], start=c == 0, stop=True))
            if c < 3:
                ps = PE.did(pe.matmul(banks[6][:, 0:P], kd[:, f], u[:, f], start=True, stop=True))
                V.wait(ps)
                if c == 0:
                    srd = V.did(dve.tensor_copy(S, banks[6][:, 0:P]))
                else:
                    srd = V.did(dve.scalar_tensor_tensor(S, S, hs[:, 4, c:c + 1], banks[6][:, 0:P], ALU.mult, ALU.add))
                yield
        V.wait(po)
        oc = V.did(dve.tensor_copy(X, banks[7]))
        A.wait(oc)
        a = A.did(act.activation(tmp, X, ACT.Square))
        PE.wait(a)
        p_ = PE.did(pe.matmul(banks[5], mat["ones"], tmp, start=True, stop=True))
        yield
        A.wait(p_)
        b = A.did(act.activation(tmp, banks[5], ACT.Ln, bias=eps_c, scale=1.0 / P))
        A.wait(b)
        b = A.did(act.activation(tmp, tmp, ACT.Exp, scale=-0.5))
        V.wait(b, oc)
        d_ = V.did(dve.scalar_tensor_tensor(X, X, gnw_col, tmp, ALU.mult, ALU.mult))
        V.wait(d_)
        d_ = V.did(dve.tensor_tensor(X, X, gate, ALU.mult))
        A.wait(d_)
        a = A.did(act.copy(ogd[:, 0, i, :], X))
        V.wait(a)
        V.did(dve.tensor_tensor(ogd[:, 1, i, :], X, ogd[:, 0, i, :].bitcast(F32), ALU.subtract))
        yield

    def stick_pair(i, reads, marks):
        qc, kc, vn, L0, L1, a0, a1, Cs, gate = sbuf_
        for e in engines:
            e.wait(*marks)
        V.did(dve.tensor_scalar(qc, rawsb[:, 0, :], 64 ** -0.5, None, ALU.mult))
        reads[4] = V.now()
        reads[5] = qk = V.did(dve.tensor_copy(kc, rawsb[:, 1, :]))
        reads[7] = silu(rawsb[:, 3, :], gate, None, gate)
        for c in range(4):
            m = pe.transpose(banks[4][:, c * P:(c + 1) * P], rawsb[:, 2, c * P:(c + 1) * P], ident)
        reads[6] = p_ = PE.did(m)
        A.wait(p_)
        vr = A.did(act.copy(vn, banks[4]))
        yield
        bank_read = [None, None]
        lread, aread = [None, None], [None, None]
        n = 0
        PE.wait(vr)
        pending = []
        for h in range(2):
            hp = slice(64 * h, 64 * h + 64)
            csum = None
            for j in (3, 2, 1, 0):
                b, n = n % 2, n + 1
                w = T - P * j
                q0 = P * j
                Lb, ab_, bank = (L0, L1)[b], (a0, a1)[b], banks[2 + b]
                PE.wait(qk, bank_read[b])
                z = PE.did(pe.matmul(bank[:, 0:w], kc[hp, q0:q0 + P], qc[hp, q0:T], start=True, stop=True))
                A.wait(z, aread[b])
                s_ = A.did(act.activation(ab_[:, 0:w], bank[:, 0:w], ACT.Abs))
                A.wait(s_)
                s_ = A.did(act.activation(ab_[:, 0:w], ab_[:, 0:w], ACT.Exp, scale=-1.0))
                A.wait(s_)
                s_ = A.did(act.activation(ab_[:, 0:w], ab_[:, 0:w], ACT.Ln, bias=one_c))
                V.wait(s_, lread[b])
                l_ = V.did(dve.scalar_tensor_tensor(Lb[:, 0:w], bank[:, 0:w], 0.0, ab_[:, 0:w], ALU.max, ALU.add))
                G.wait(l_)
                l_ = G.did(pool.tensor_tensor(Lb[:, 0:P], Lb[:, 0:P], mat["before"], ALU.mult))
                yield
                PE.wait(l_, csum)
                pe.matmul(bank[:, 0:P], ident, mat["notbefore"], start=False, stop=False, skip_group_check=True)
                m = pe.matmul(bank[:, 0:w], mat["negtri"], Lb[:, 0:w], start=False, stop=j == 3, skip_group_check=True)
                if j < 3:
                    m = pe.matmul(bank[:, P:w], mat["negones"], Cs[:, q0 + P:T], start=False, stop=True, skip_group_check=True)
                la = PE.did(m)
                if j:
                    G.wait(la)
                    if j < 3:
                        G.did(pool.tensor_tensor(Cs[:, q0 + P:T], Cs[:, q0 + P:T], Lb[:, P:w], ALU.add))
                    csum = lread[b] = G.did(pool.tensor_tensor(Cs[:, q0:q0 + P], Lb[:, 0:P], mat["ones"], ALU.mult))
                else:
                    csum = None
                    lread[b] = la
                A.wait(la)
                a_ = bank_read[b] = A.did(act.activation(ab_[:, 0:w], bank[:, 0:w], ACT.Exp))
                yield
                PE.wait(a_)
                aread[b] = av = PE.did(pe.matmul(banks[4][hp, q0:T], vn[:, j * P + 64 * h:j * P + 64 * h + 64],
                                                 ab_[:, 0:w], start=j == 3, stop=j == 0, skip_group_check=True))
        tg = L1
        V.wait(lread[0], lread[1], av)
        b = V.did(dve.tensor_tensor(tg, gate, banks[4], ALU.mult))
        A.wait(b)
        a = A.did(act.copy(osb[:, 0, i, :], tg))
        V.wait(a)
        V.did(dve.tensor_tensor(osb[:, 1, i, :], tg, osb[:, 0, i, :].bitcast(F32), ALU.subtract))
        yield

    slotsA = [n % 4 for n in range(8)]
    A.wait(zeros)
    for _ in project(raw_tiles, slotsA, None, 8):
        pass
    with loop("stage_a", 1, 4) as i:
        reads, marks = {}, fence()
        weave(project(raw_tiles, slotsA, reads, 8), [delta_head(i - 1, reads, marks), stick_pair(i - 1, reads, marks)])

    sig_sb = at("sig_sb", r_res, [P, 8, T])
    sig_gd = at("sig_gd", rawA, [P, 8, T])
    reads, marks = {}, fence()

    def merge_gates():
        for n in range(16):
            s, b = n % 4, n % 2
            yield from product(s, banks[b], terms_T(s, banks[b], all_k), first_wait=(acc_free[b].now(),))
            split((s + 2) % 4)
            dst = sig_sb[:, n, :] if n < 8 else sig_gd[:, n - 8, :]
            A.wait(used[s].now())
            if n == 8:
                A.wait(*[reads[r] for r in range(8)])
            e_ = A.did(act.activation(dst, banks[b], ACT.Abs))
            A.wait(e_)
            e_ = A.did(act.activation(dst, dst, ACT.Exp, scale=-1.0))
            A.wait(e_)
            e_ = A.did(act.activation(dst, dst, ACT.Ln, bias=one_c))
            V.wait(e_)
            e_ = acc_free[b].by(dve.scalar_tensor_tensor(dst, banks[b], 0.0, dst, ALU.min, ALU.subtract))
            A.wait(e_)
            A.did(act.activation(dst, dst, ACT.Exp))

    weave(merge_gates(), [delta_head(3, reads, marks), stick_pair(3, reads, marks)])
    def dump(parts):
        nc.sync.wait_ge(*[(s[0], s[1]) for s in [A.now()]][0])
        for e in engines + acc_free:
            if e.now():
                nc.sync.wait_ge(*e.now()[:2])
        d = Signal(counts, "dump", 16)
        c0 = 0
        for p_ in parts:
            n_ = int(np.prod(p_.shape[1:]))
            d.by(nc.sync.dma_start(dbg[0:p_.shape[0], c0:c0 + n_], p_.bitcast(F32) if p_.dtype == F32R else p_))
            c0 += n_
        nc.sync.wait_ge(d.sem, d.count.value())

    if stop == "A":
        fl_ = lambda x: x.rearrange("p a b -> p (a b)") if len(x.shape) == 3 else x.rearrange("p a b c -> p (a b c)")
        dump([fl_(osb), fl_(ogd), fl_(sig_sb)])
        return counts.found | dma_counts.found
    merged = at("merged", rawA + 16 * KB + 512, [P, 2, 8, T], F32R)
    mtmp = at("mtmp", rawA + 48 * KB + 512, [P, 2, 2, T])
    for e in engines:
        e.wait(*fence())
    pair_free = [Signal(counts, f"pair{b}_free") for b in range(2)]
    mhi = [Signal(counts, f"mtmp{b}_hi") for b in range(2)]
    mlo = [Signal(counts, f"mtmp{b}_lo") for b in range(2)]
    for x in pair_free + mhi + mlo:
        x.prime(V)
    with loop("branch", 0, 2) as i:
        for c in range(4):
            s, b = c, c % 2
            ba, bb = banks[2 * b], banks[2 * b + 1]
            terms = terms_T(s, ba, [(k, k) for k in range(4)], osb) + terms_T(s, bb, [(4 + k, k) for k in range(4)], ogd)
            for _ in product(s, None, terms, first_wait=(pair_free[b].now(),)):
                pass
            split((s + 2) % 4)
            m = 4 * i + c
            V.wait(used[s].now(), mhi[b].now(), mlo[b].now())
            a1 = V.did(dve.tensor_tensor(mtmp[:, b, 0, :], ba, sig_sb[:, m, :], ALU.mult))
            a2 = pair_free[b].by(dve.tensor_tensor(mtmp[:, b, 1, :], bb, sig_gd[:, m, :], ALU.mult))
            V.wait(a1, a2)
            a3 = V.did(dve.tensor_tensor(mtmp[:, b, 0, :], mtmp[:, b, 0, :], mtmp[:, b, 1, :], ALU.add))
            A.wait(a3)
            h_ = mhi[b].by(act.copy(merged[:, 0, m, :], mtmp[:, b, 0, :]))
            V.wait(h_)
            mlo[b].by(dve.tensor_tensor(merged[:, 1, m, :], mtmp[:, b, 0, :], merged[:, 0, m, :].bitcast(F32), ALU.subtract))

    def half_terms(s, src, kk, half_banks, first, last):
        w = ring[:, s].rearrange("p two (k n) -> p two k n", k=2)
        o = []
        for kl in range(2):
            for j in range(NT):
                for m, (a, b) in enumerate(((0, 0), (0, 1), (1, 0))):
                    o.append((banks[half_banks[j]], src[:, a, kk + kl, j * P:(j + 1) * P], w[:, b, kl, :],
                              first and kl == 0 and m == 0, last and kl == 1 and m == 2))
        return o

    def token_terms(src, j, bank):
        o = []
        for s in range(4):
            w = ring[:, s].rearrange("p two (k n) -> p two k n", k=2)
            for kl in range(2):
                for m, (a, b) in enumerate(((0, 0), (0, 1), (1, 0))):
                    o.append((s, banks[bank], src[:, a, 2 * s + kl, j * P:(j + 1) * P], w[:, b, kl, :],
                              s == 0 and kl == 0 and m == 0, s == 3 and kl == 1 and m == 2, kl == 1 and m == 2))
        return o

    def add_normed(j, lo_bank, hi_bank, w_bc, junk, res, stats, done_hi, done_lo, junk_free):
        A.wait(done_lo, done_hi, junk_free)
        a = A.did(act.activation(junk[:, 0:512], banks[lo_bank], ACT.Square, accum_out=stats[:, 3 * j:3 * j + 1]))
        a = A.did(act.activation(junk[:, 512:1024], banks[hi_bank], ACT.Square, accum_out=stats[:, 3 * j + 1:3 * j + 2]))
        V.wait(a)
        a = V.did(dve.tensor_tensor(stats[:, 3 * j + 2:3 * j + 3], stats[:, 3 * j:3 * j + 1], stats[:, 3 * j + 1:3 * j + 2], ALU.add))
        r = rstd(stats[:, 3 * j + 2:3 * j + 3], stats[:, 3 * j + 2:3 * j + 3], D, a)
        V.wait(r)
        for h_, bank in enumerate((lo_bank, hi_bank)):
            f = slice(512 * h_, 512 * h_ + 512)
            b = V.did(dve.scalar_tensor_tensor(junk[:, f], banks[bank], stats[:, 3 * j + 2:3 * j + 3], w_bc[:, f], ALU.mult, ALU.mult))
        V.wait(b)
        return V.did(dve.tensor_tensor(res[:, j, :], res[:, j, :], junk, ALU.add))

    def out_projection(src, w_bc, junk, res, res_ready, stats):
        for kk in range(4):
            s = kk
            for _ in product(s, None, half_terms(s, src, 2 * kk, (4, 5, 6, 7), kk == 0, kk == 3)):
                pass
            split((s + 2) % 4)
        left = used[3].now()
        V.wait(res_ready)
        ready = []
        for j in range(NT):
            terms = token_terms(src, j, j)
            for (s, o, l, r, a, b, slab_end) in terms:
                if j == 0:
                    PE.wait(lo_done[s].now())
                m = pe.matmul(o, l, r, start=a, stop=b)
                if j == NT - 1 and slab_end:
                    used[s].by(m)
                if j == 0 and slab_end and s < 2:
                    split(s + 2)
            if j < NT - 1:
                tokd = PE.did(m)
            else:
                tokd = used[3].now()
            ready.append(add_normed(j, 4 + j, j, w_bc, junk[:, j % 2, :], res, stats, tokd, left, ready[j - 2] if j > 1 else None))
        split(0)
        split(1)
        return ready

    for e in engines:
        e.wait(*fence(), *[x.now() for x in pair_free + mhi + mlo])
    ydma = Signal(counts, "reload_x", 16)
    wdma = Signal(counts, "post_w_loaded", 16)
    post_bc = at("post_bc", r4, [P, D])
    junk1 = at("junk1", r4 + 4 * KB, [P, 2, D])
    scr2 = at("norm_scratch2", r4 + 12 * KB, [P, NT, D])
    for j in range(NT):
        xr_ = ydma.by(act.dma_start(x1[:, j, :], t["x"][0, j * P:(j + 1) * P, :]))
    wr_ = wdma.by(act.dma_start(post_bc, t["post_norm_w"][0].partition_broadcast(P)))
    V.wait(wr_)
    ready = out_projection(merged, post_bc, junk1, x1, xr_, stat[:, 8:20])
    if stop == "Y":
        dump([x1.rearrange("p a b -> p (a b)")])
        return counts.found | dma_counts.found
    PE.wait(ready[-1])
    h_ready = norm_transpose(x1, aprew_col, scr2, ready, stat[:, 4:8])

    off[0] = r4
    mix = take("mix", [P, 2, 8, T], F32R)
    ncum = take("ncum", [P, 8, T])
    bias_w = take("bias_w", [P, 4, T])
    rawb = take("rawb", [P, 6, T])
    bbuf = [take(f"b{n}", [P, T]) for n in range(15)]
    assert off[0] <= nc.sbuf_usable_end, off[0] - r4
    for e in engines:
        e.wait(*fence())
    bb_ = at("bias_consts_s", off[0] - 28 * KB, [32, 384 + 8 * P])
    relb = at("relb", off[0] - 20 * KB, [32, 4, P])
    rel = at("rel", off[0] - 17 * KB, [32, 4])
    wf = at("wf", off[0] - 16 * KB, [P, 64])
    wf_s = at("wf_s", off[0] - 15 * KB, [P, 2, 64], F32R)
    cumT = at("cumT", off[0] - 14 * KB, [8, T])
    fw = at("fw", off[0] - 12 * KB, [P, 4, 384])
    sg_bc = little("sg_bc", P)
    bdma = Signal(counts, "bias_in", 16)
    for dst, src in ((bb_, t["bias_consts"]), (rel, t["rel_bias_2"]), (sg_bc, t["subln_g_2"][0].partition_broadcast(P)),
                     (wf.rearrange("p (k n) -> p k n", k=8), w2[0].rearrange("(k p) n -> p k n", p=P)[:, :, 3072:3080])):
        bd = bdma.by(act.dma_start(dst, src))
    V.wait(bd)
    A.wait(bd)
    rb = V.did(dve.tensor_copy(relb, rel.unsqueeze(2).broadcast_to([32, 4, P])))
    PE.wait(rb)
    for h in range(4):
        m = pe.matmul(banks[2 + h][:, 0:384], relb[:, h, :], bb_[:, 0:384], start=True, stop=True)
    p_ = PE.did(m)
    A.wait(p_)
    for h in range(4):
        fr = A.did(act.copy(fw[:, h, :], banks[2 + h][:, 0:384]))
    skew = nc.dram_tensor("skew", (4, P * 384 + 128), F32, kind="Internal").ap()
    kdma = Signal(counts, "skew_written", 16)
    A.wait(fr)
    for h in range(4):
        kd_ = kdma.by(act.dma_start(skew[h, 0:P * 384].rearrange("(p m) -> p m", p=P), fw[:, h, :]))
    rdma = Signal(counts, "skew_read", 16)
    A.wait(kd_)
    for h in range(4):
        src = skew[h, 127:127 + P * 383].rearrange("(p m) -> p m", m=383)[:, 0:256]
        rd_ = rdma.by(act.dma_start(bias_w[:, h, 256:512], src))
    V.wait(fr)
    V.did(dve.tensor_copy(bias_w[:, :, 0:256], fw[:, :, 0:1].broadcast_to([P, 4, 256])))
    V.wait(rd_)
    for h in range(4):
        V.did(dve.tensor_tensor(bias_w[:, h, 384:512], bias_w[:, h, 384:512], mat["causal"], ALU.add))
    a = A.did(act.copy(wf_s[:, 0, :], wf))
    V.wait(a)
    a = V.did(dve.tensor_tensor(wf_s[:, 1, :], wf, wf_s[:, 0, :].bitcast(F32), ALU.subtract))
    PE.wait(a, h_ready)
    p_ = narrow(banks[6], wf_s.rearrange("p two (k n) -> p two k n", k=8), 8)
    fz, fe = stat[:, 0:32].rearrange("p (t h) -> p t h", t=4), stat[:, 32:64].rearrange("p (t h) -> p t h", t=4)
    V.wait(p_)
    a = V.did(dve.tensor_tensor(fz, banks[6][:, 0:32].rearrange("p (t h) -> p t h", t=4),
                                bfb.unsqueeze(1).broadcast_to([P, 4, 8]), ALU.add))
    A.wait(a)
    a = A.did(act.activation(fe, fz, ACT.Abs))
    A.wait(a)
    a = A.did(act.activation(fe, fe, ACT.Exp, scale=-1.0))
    A.wait(a)
    a = A.did(act.activation(fe, fe, ACT.Ln, bias=one_c))
    V.wait(a)
    a = V.did(dve.scalar_tensor_tensor(fl, fz, 0.0, fe, ALU.min, ALU.subtract))
    PE.wait(a)
    for j in range(NT):
        p_ = pe.matmul(banks[7][0:8, j * P:(j + 1) * P], fl[:, j, :], mat["upper"], start=j == 0, stop=j == 3, skip_group_check=True)
        if j < 3:
            pe.matmul(banks[7][0:8, (j + 1) * P:T].rearrange("p (c f) -> p c f", f=P), fl[:, j, :],
                      mat["ones"].unsqueeze(1).broadcast_to([P, 3 - j, P]), start=False, stop=False, skip_group_check=True)
    V.wait(PE.did(p_))
    a = V.did(dve.tensor_copy(cumT, banks[7][0:8, :]))
    PE.wait(a, fr)
    fb = [None] * 4
    for h in range(8):
        b = 2 + h % 4
        PE.wait(fb[h % 4])
        p_ = PE.did(pe.matmul(banks[b], bb_[0:8, 384 + h * P:384 + (h + 1) * P], cumT, start=True, stop=True))
        A.wait(p_)
        fb[h % 4] = A.did(act.copy(ncum[:, h, :], banks[b]))

    v_wait = nc.alloc_semaphore("dve_held")
    tiles_b = [rawb[:, n, :] for n in range(6)]
    slots_b = [0, 1, 2, 3, 0, 1]

    def project_b(reads, last=False):
        for n, dst in enumerate(tiles_b):
            s, b = slots_b[n], n % 2
            yield from product(s, banks[b], terms_T(s, banks[b], all_k), first_wait=(acc_free[b].now(),))
            split(slots_b[(n + 2) % 6])
            assert reads is None or n in reads, n
            A.wait(used[s].now(), reads[n] if reads else None)
            acc_free[b].by(act.copy(dst, banks[b]))

    qd, kd2, qf, kf, vd, vf, scA, scB, pTd, pTf, od, of_, bwh, nch0, sc3 = bbuf

    def softmax_scores(bank, w, in1, dst, mx, sm, ready):
        V.wait(ready)
        V.hold(v_wait)
        a = V.did(dve.tensor_tensor_reduce(out=dst[:, 0:w], in0=bank[:, 0:w], in1=in1, scale=1.0, scalar=-3.0e38,
                                           op0=ALU.add, op1=ALU.max, accum_out=mx))
        V.wait(a)
        a = V.did(dve.tensor_scalar(mx, mx, -1.0, None, ALU.mult))
        A.wait(a)
        return a, A.did(act.activation(dst[:, 0:w], dst[:, 0:w], ACT.Exp, bias=mx, accum_out=sm))

    def prepare_b(q_raw, k_raw, v_raw, q, k, v, bank, reads, n0, marks):
        for e in engines:
            e.wait(*marks)
        reads[n0] = V.did(dve.tensor_scalar(q, rawb[:, n0, :], 64 ** -0.5, None, ALU.mult))
        reads[n0 + 1] = qk = V.did(dve.tensor_copy(k, rawb[:, n0 + 1, :]))
        for c in range(4):
            m = pe.transpose(bank[:, c * P:(c + 1) * P], rawb[:, n0 + 2, c * P:(c + 1) * P], ident)
        reads[n0 + 2] = p_ = PE.did(m)
        A.wait(p_)
        return qk, A.did(act.copy(v, bank))

    def to_mix(src, bank, m, ready):
        PE.wait(ready)
        for c in range(4):
            q = pe.transpose(bank[:, c * P:(c + 1) * P], src[:, c * P:(c + 1) * P], ident)
        p_ = PE.did(q)
        A.wait(p_)
        a = A.did(act.copy(mix[:, 0, m, :], bank))
        V.wait(a)
        return V.did(dve.tensor_tensor(mix[:, 1, m, :], bank, mix[:, 0, m, :].bitcast(F32), ALU.subtract))

    def diff_head(i, reads, marks):
        c0 = 0
        qk, vr = prepare_b(None, None, None, qd, kd2, vd, banks[4], reads, 0, marks)
        V.wait(V.did(dve.tensor_copy(bwh, bias_w[:, i, :])))
        yield
        st = stat
        pt_free = None
        PE.wait(vr)
        for t_ in range(NT):
            w = (t_ + 1) * P
            es = []
            for m_ in range(2):
                hp = slice(64 * m_, 64 * m_ + 64)
                dst = (scA, scB)[m_]
                PE.wait(qk, pt_free)
                z = PE.did(pe.matmul(banks[2 + m_][:, 0:w], qd[hp, t_ * P:w], kd2[hp, 0:w], start=True, stop=True))
                V.wait(pt_free)
                rd, e_ = softmax_scores(banks[2 + m_], w, bwh[:, T - w:T], dst, st[:, 2 * m_:2 * m_ + 1], st[:, 2 * m_ + 1:2 * m_ + 2], z)
                es.append(e_)
            yield
            V.wait(es[1])
            V.did(dve.reciprocal(st[:, 4:5], st[:, 1:2]))
            a = V.did(dve.reciprocal(st[:, 5:6], st[:, 3:4]))
            V.wait(a)
            a = V.did(dve.scalar_tensor_tensor(st[:, 5:6], st[:, 5:6], -1.0, lam_c, ALU.mult, ALU.mult))
            b_ = V.did(dve.tensor_scalar(scA[:, 0:w], scA[:, 0:w], st[:, 4:5], None, ALU.mult))
            V.wait(a, b_)
            pr = V.did(dve.scalar_tensor_tensor(scA[:, 0:w], scB[:, 0:w], st[:, 5:6], scA[:, 0:w], ALU.mult, ALU.add))
            PE.wait(pr, vr)
            for c in range(t_ + 1):
                q = pe.transpose(banks[4][:, c * P:(c + 1) * P], scA[:, c * P:(c + 1) * P], ident)
            pt_free = p_ = PE.did(q)
            A.wait(p_)
            ev = A.did(act.copy(pTd[:, 0:w], banks[4][:, 0:w]))
            yield
            PE.wait(ev)
            for c in range(t_ + 1):
                q = pe.matmul(banks[6][:, 0:P], pTd[:, c * P:(c + 1) * P], vd[:, c * P:(c + 1) * P], start=c == 0, stop=c == t_)
            p_ = PE.did(q)
            V.wait(p_)
            a = V.did(dve.tensor_copy(od[:, t_ * P:w], banks[6][:, 0:P]))
            A.wait(a)
            a = A.did(act.activation(pTd[:, 0:P], od[:, t_ * P:w], ACT.Square, accum_out=st[:, 6:7]))
            r = rstd(st[:, 6:7], st[:, 6:7], P, a)
            V.wait(r)
            a = V.did(dve.scalar_tensor_tensor(od[:, t_ * P:w], od[:, t_ * P:w], st[:, 6:7], sg_bc, ALU.mult, ALU.mult))
            V.wait(a)
            last = V.did(dve.tensor_scalar(od[:, t_ * P:w], od[:, t_ * P:w], 1.0 - lam_init, None, ALU.mult))
            PE.wait(r)
            yield
        to_mix(od, banks[4], i, last)
        yield

    def fox_pair(i, reads, marks):
        qk, vr = prepare_b(None, None, None, qf, kf, vf, banks[5], reads, 3, marks)
        st = stat
        yield
        PE.wait(vr)
        pt_free = None
        for e_ in range(2):
            hp = slice(64 * e_, 64 * e_ + 64)
            V.wait(pt_free)
            nrow = V.did(dve.tensor_copy(nch0, ncum[:, 2 * i + e_, :]))
            for t_ in range(NT):
                w = (t_ + 1) * P
                PE.wait(qk, pt_free)
                pe.matmul(banks[7][:, 0:w], qf[hp, t_ * P:w], kf[hp, 0:w], start=True, stop=True)
                z = PE.did(pe.matmul(banks[7][:, t_ * P:w], ident, mat["causal"], start=False, stop=True, skip_group_check=True))
                V.wait(pt_free, nrow)
                rd, ex = softmax_scores(banks[7], w, nch0[:, 0:w], sc3, st[:, 10:11], st[:, 11:12], z)
                yield
                PE.wait(ex)
                for c in range(t_ + 1):
                    q = pe.transpose(banks[5][:, c * P:(c + 1) * P], sc3[:, c * P:(c + 1) * P], ident)
                p_ = PE.did(q)
                A.wait(p_)
                ev = A.did(act.copy(pTf[:, 0:w], banks[5][:, 0:w]))
                V.wait(ex)
                r = V.did(dve.reciprocal(st[:, 12:13], st[:, 11:12]))
                yield
                PE.wait(ev)
                for c in range(t_ + 1):
                    q = pe.matmul(banks[5][:, 0:64], pTf[:, c * P:(c + 1) * P], vf[:, c * P + 64 * e_:c * P + 64 * e_ + 64],
                                  start=c == 0, stop=c == t_)
                p_ = PE.did(q)
                V.wait(p_, r)
                pt_free = last = V.did(dve.tensor_scalar(of_[:, t_ * P + 64 * e_:t_ * P + 64 * e_ + 64], banks[5][:, 0:64],
                                                  st[:, 12:13], None, ALU.mult))
        to_mix(of_, banks[5], 4 + i, last)
        yield

    for e in engines:
        e.wait(*fence())
    for _ in project_b(None):
        pass
    with loop("stage_b", 1, 4) as i:
        reads, marks = {}, fence()
        weave(project_b(reads), [diff_head(i - 1, reads, marks), fox_pair(i - 1, reads, marks)])
    reads, marks = {}, fence()
    weave(iter(()), [diff_head(3, reads, marks), fox_pair(3, reads, marks)])
    if stop == "M":
        dump([mix.rearrange("p a b c -> p (a b c)")])
        return counts.found | dma_counts.found

    for e in engines:
        e.wait(*fence())
    b2dma = Signal(counts, "post_w2_loaded", 16)
    post2 = at("post2", r4 + 32 * KB, [P, D])
    junk2 = at("junk2", r4 + 36 * KB, [P, 2, D])
    scr3 = at("norm_scratch3", r4 + 44 * KB, [P, NT, D])
    V.wait(b2dma.by(act.dma_start(post2, t["ln_attn_post_2"][0].partition_broadcast(P))))
    ready = out_projection(mix, post2, junk2, x1, None, stat[:, 8:20])
    PE.wait(ready[-1])
    h_ready = norm_transpose(x1, mprew_col, scr3, ready, stat[:, 4:8])
    for e in engines:
        e.wait(*fence(), h_ready)
    u = at("u", r4, [P, 34, T])
    ring_u = at("ring_u", r4 + 68 * KB, [P, 4, 2, 2 * T], F32R)
    relu_done = [Signal(counts, f"relu{b}") for b in range(2)]
    for x in relu_done:
        x.prime(A)
    with loop("up", 0, 8) as i:
        for c in range(4):
            s, b = c, c % 2
            for _ in product(s, banks[b], terms_T(s, banks[b], all_k), first_wait=(relu_done[b].now(),)):
                pass
            split((s + 2) % 4)
            A.wait(used[s].now())
            r_ = relu_done[b].by(act.activation(u[:, 4 * i + c, :], banks[b], ACT.Relu))
            V.wait(r_)
            sq_done = V.did(dve.tensor_tensor(u[:, 4 * i + c, :], u[:, 4 * i + c, :], u[:, 4 * i + c, :], ALU.mult))

    u_split = [Signal(counts, f"u{s}_split") for s in range(4)]
    r1 = base
    post3 = at("post3", r1, [P, D])
    junk3 = at("junk3", r1 + 4 * KB, [P, 2, D])
    zero_r = at("zero_r", r1 + 12 * KB, [P, T], F32R)

    def split_u(k0, s):
        x = u[:, bass.ds(k0, 2), :].rearrange("p a b -> p (a b)")
        A.wait(used[s].now())
        h_ = A.did(act.copy(ring_u[:, s, 0, :], x))
        V.wait(h_)
        u_split[s].by(dve.tensor_tensor(ring_u[:, s, 1, :], x, ring_u[:, s, 0, :].bitcast(F32), ALU.subtract))

    for e in engines:
        e.wait(*fence(), *[x.now() for x in relu_done + used])
    b3dma = Signal(counts, "post_w3_loaded", 16)
    w3 = b3dma.by(act.dma_start(post3, t["ln_mlp_post_2"][0].partition_broadcast(P)))
    tok = V.did(dve.tensor_copy(u[:, 32:34, :], u[:, 0:2, :]))
    zr = V.did(dve.memset(zero_r.bitcast(F32), 0.0))
    A.wait(tok)
    split_u(0, 0)

    def down_slab(i, s, hb, opened=True):
        w = ring[:, s].rearrange("p two (k n) -> p two k n", k=2)
        xs = ring_u[:, s].rearrange("p two (k n) -> p two k n", k=2)
        PE.wait(u_split[s].now())
        split_u(i * 8 + 2 * s + 2, (s + 1) % 4)
        terms = []
        for kl in range(2):
            for j in range(NT):
                for a, b in ((0, 0), (0, 1), (1, 0)):
                    terms.append((banks[hb[j]], xs[:, a, kl, j * P:(j + 1) * P], w[:, b, kl, :], False, True))
        for _ in product(s, None, terms, opened=True):
            pass
        split((s + 2) % 4)

    PE.wait(zr)
    for half in range(2):
        hb = [4 * half + j for j in range(4)]
        for j in range(4):
            pe.matmul(banks[hb[j]], zero_r[:, 0:P], zero_r, start=True, stop=True)
        with loop(f"down{half}", 0, 4 - half) as i:
            for s in range(4):
                down_slab(i, s, hb)
    split(2)
    split(3)
    for s in range(1, 4):
        split_u(24 + 2 * s, s)
    PE.wait(*[x.now() for x in u_split + lo_done])
    last_half0 = used[3].now()
    V.wait(w3)
    outs = Signal(counts, "out_stored", 16)
    done = []
    for j in range(NT):
        for s in range(4):
            w = ring[:, s].rearrange("p two (k n) -> p two k n", k=2)
            xs = ring_u[:, s].rearrange("p two (k n) -> p two k n", k=2)
            for kl in range(2):
                for a, b in ((0, 0), (0, 1), (1, 0)):
                    m = pe.matmul(banks[4 + j], xs[:, a, kl, j * P:(j + 1) * P], w[:, b, kl, :], start=False, stop=True,
                                  skip_group_check=True)
        done.append(add_normed(j, j, 4 + j, post3, junk3[:, j % 2, :], x1, stat[:, 8:20], PE.did(m), last_half0,
                               done[j - 2] if j > 1 else None))
        nc.sync.wait_ge(*done[j][:2])
        outs.by(nc.sync.dma_start(out[0, j * P:(j + 1) * P, :], x1[:, j, :]))
    nc.sync.wait_ge(outs.sem, outs.count.value())
    return counts.found | dma_counts.found


def all_inputs(inputs):
    return {**{n: np.ascontiguousarray(inputs[n]) for n in inputs},
            "shape_consts": shape_constants(), "bias_consts": bias_constants()}


_INS = ["x", "pre_norm_w", "post_norm_w", "w_in", "conv_w", "a_log", "dt_bias", "gdn_norm_w", "w_branch_sb",
        "w_branch_gdn", "w_out", "ln_attn_pre_2", "w_in_2", "b_f_2", "lam_q1_2", "lam_k1_2", "lam_q2_2",
        "lam_k2_2", "subln_g_2", "rel_bias_2", "w_out_2", "ln_attn_post_2", "ln_mlp_pre_2", "w_up_2",
        "w_down_2", "ln_mlp_post_2"]


def declared(nc, shapes, per):
    t = {n: nc.dram_tensor(f"in_{n}", s, F32, kind="ExternalInput").ap() for n, s in shapes.items()}
    out = nc.dram_tensor("out_0", shapes["x"], F32, kind="ExternalOutput").ap()
    return program(nc, t, out, per)


def kernel(**inputs):
    import concourse.bacc as _bacc
    from concourse.bass_utils import run_bass_kernel_spmd as _run

    arrays = {n: np.ascontiguousarray(inputs[n]) for n in _INS}
    arrays["shape_consts"] = shape_constants()
    arrays["bias_consts"] = bias_constants()
    shapes = {n: a.shape for n, a in arrays.items()}
    per = declared(_bacc.Bacc("TRN2", target_bir_lowering=False, num_devices=1), shapes, {})
    nc = _bacc.Bacc("TRN2", target_bir_lowering=False, num_devices=1)
    declared(nc, shapes, per)
    r = _run(nc, [{f"in_{n}": a for n, a in arrays.items()}], core_ids=[0])
    return r.results[0]["out_0"]
```

```python
from contextlib import contextmanager

import numpy as np

import concourse.bass as bass
from concourse import mybir

F32 = mybir.dt.float32
F32R = mybir.dt.float32r
BF16 = mybir.dt.bfloat16
ALU = mybir.AluOpType
ACT = mybir.ActivationFunctionType
AXX = mybir.AxisListType.X
ET = mybir.EngineType

P = 128
EPS = 1e-6
NEG = -1e30


class Counts:

    def __init__(self, nc, per):
        self.nc, self.per, self.found = nc, per, {}
        self.all, self.loop = [], None

    @contextmanager
    def fori(self, name, start, end, engines):
        with self.nc.Fori(start, end, engines=engines) as i:
            self.loop = (name, i, start)
            yield i
        for c in self.all:
            self.found[(name, c.name)] = c.local
            c.base, c.local = c.base + (end - start) * c.local, 0
        self.loop = None


class Count:
    def __init__(self, counts, name):
        self.counts, self.name, self.base, self.local = counts, name, 0, 0
        counts.all.append(self)

    def add(self, k=1):
        if self.counts.loop:
            self.local += k
        else:
            self.base += k

    def value(self):
        if not self.counts.loop:
            return self.base
        name, i, start = self.counts.loop
        per = self.counts.per.get((name, self.name), 0)
        least = self.base + self.local - start * per
        return i * per + least if per else least

    def zero(self):
        return self.base == 0 and self.local == 0


class Signal:

    def __init__(self, counts, name, step=1):
        self.sem, self.count, self.step = counts.nc.alloc_semaphore(name), Count(counts, name), step

    def prime(self, engine):
        assert self.step == 1
        engine.e.sem_inc(self.sem, 1)
        self.count.add(1)

    def by(self, instruction):
        instruction.then_inc(self.sem, self.step)
        self.count.add(self.step)
        return self.now()

    def before(self, k):
        sem, value, order, loop = self.now()
        return sem, value - k, order - k, loop

    def now(self):
        return None if self.count.zero() else (self.sem, self.count.value(), self.count.base + self.count.local, self.count.counts.loop)


class Engine:

    def __init__(self, counts, engine, name):
        self.e, self.done, self.counts = engine, Signal(counts, name), counts
        self.waited = {}

    def did(self, instruction):
        return self.done.by(instruction)

    def now(self):
        return self.done.now()

    def wait(self, *signals):
        for s in signals:
            if s is None:
                continue
            sem, value, order, loop = s
            key = (id(sem), loop[0] if loop else None)
            if self.waited.get(key, -1) >= order and (loop is None) == (self.counts.loop is None):
                continue
            self.waited[key] = order
            self.e.wait_ge(sem, value)

    def hold(self, carrier):
        self.e.sem_inc(carrier, 1)

    def forget(self):
        self.waited = {}


class TensorE:

    def __init__(self, engine):
        self.engine, self.time = engine, 0.0

    def matmul(self, out, lhsT, rhs, **flags):
        passes = 4 if rhs.dtype == F32 else 1
        self.time += passes * max(64, int(np.prod(rhs.shape[1:]))) / 2400
        return self.engine.matmul(out, lhsT, rhs, **flags)

    def transpose(self, out, in_, identity):
        self.time += P / 2400
        return self.engine.transpose(out, in_, identity)


def interleave(pe, filler, chains):
    queue = [[pe.time, n, c] for n, c in enumerate(chains)]
    while queue or filler is not None:
        first = min(queue, default=None)
        if first is not None and (first[0] <= pe.time or filler is None):
            pe.time = max(pe.time, first[0])
            after = next(first[2], None)
            if after is None:
                queue.remove(first)
            else:
                first[0] = pe.time + after
        elif next(filler, filler) is filler:
            filler = None


MATS = ["ident", "upper", "after", "negtri", "ones", "negones", "causal", "before", "notbefore"]
LEVELS = 7


def bucket(dist, n_buckets=32, max_distance=128):
    exact = n_buckets // 2
    d = np.maximum(dist, 1).astype(np.float32)
    large = exact + np.log(d / np.float32(exact)) / np.float32(np.log(max_distance / exact)) * (n_buckets - exact)
    large = np.minimum(large.astype(np.int32), n_buckets - 1)
    return np.where(dist < exact, dist, large)


def shape_constants():
    p, f = np.arange(P)[:, None], np.arange(P)[None, :]
    mats = {
        "ident": p == f, "upper": p <= f, "after": p > f, "negtri": -1.0 * (p >= f),
        "ones": np.ones((P, P)), "negones": -np.ones((P, P)), "causal": np.where(f > p, NEG, 0.0),
        "before": p < f, "notbefore": np.where(p >= f, NEG, 0.0),
    }
    out = [np.asarray(mats[m], np.float32) for m in MATS]

    def level(l, row, col):
        same = (row >> (l + 1)) == (col >> (l + 1))
        return (same & ((row >> l) % 2 == 1) & ((col >> l) % 2 == 0)).astype(np.float32)

    out.append(level(0, p, f))
    out += [level(l, f, p) for l in range(LEVELS)]
    return np.concatenate(out, axis=1)


def bias_constants():
    m = np.arange(384)
    hot = (bucket(np.maximum(255 - m, 0))[None, :] == np.arange(32)[:, None]).astype(np.float32)
    pick = np.zeros((32, 8, P), np.float32)
    for h in range(8):
        pick[h, h, :] = -1.0
    return np.concatenate([hot, pick.reshape(32, 8 * P)], axis=1)


def program(nc, t, out, per, stop=None, dbg=None):
    T, D = t["x"].shape[1:]
    NT, KT = T // P, D // P
    dma_counts = Counts(nc, per)
    counts = Counts(nc, per)
    PE = Engine(counts, nc.tensor, "pe_done")
    A = Engine(counts, nc.scalar, "act_done")
    V = Engine(counts, nc.vector, "dve_done")
    G = Engine(counts, nc.gpsimd, "pool_done")
    engines = [PE, A, V, G]
    pe, act, dve, pool = TensorE(nc.tensor), nc.scalar, nc.vector, nc.gpsimd
    compute = [ET.Pool, ET.Activation, ET.PE, ET.DVE]

    @contextmanager
    def loop(name, start, end):
        for e in engines:
            e.forget()
        with counts.fori(name, start, end, compute) as i:
            yield i
        for e in engines:
            e.forget()

    base = 16512
    cursor = [base]

    def at(name, address, shape, dt=F32):
        return nc.alloc_sbuf_tensor_at(name, shape, dt, offset=address, align_bytes=4).ap()

    def region(nbytes):
        a = cursor[0]
        cursor[0] += nbytes
        return a

    KB = 1024
    hT = at("hT", region(32 * KB), [P, 2, KT, T], F32R)
    ring = at("ring", region(32 * KB), [P, 4, 2, 1024], F32R)
    raw_ring = at("raw_ring", region(16 * KB), [P, 4, 1024])
    r_res = region(16 * KB)
    x1 = at("x1", r_res, [P, NT, D])
    consts = at("consts", region(17 * 512), [P, 17, P])
    small = region(4 * 560 + 768)
    r4 = cursor[0]
    mat = {m: consts[:, n, :] for n, m in enumerate(MATS)}
    ident = mat["ident"]
    level0, levelT = consts[:, len(MATS), :], [consts[:, len(MATS) + 1 + l, :] for l in range(LEVELS)]
    so = [small]

    def little(name, cols):
        a = at(name, so[0], [P, cols])
        so[0] += 4 * cols
        return a

    colp = little("colp", 80)
    eps_c, one_c = little("eps_c", 1), little("one_c", 1)
    lam_c = little("lam_c", 1)
    gates = little("gates", 80).rearrange("p (h k c) -> p h k c", h=4, k=5)
    hs = little("hs", 20).rearrange("p (k c) -> p k c", k=5)
    cw = little("cw", 12).rearrange("p (k i) -> p k i", k=3)
    dtb, alog = little("dtb", 4), little("alog", 4)
    bfb = little("bfb", 8)
    stat = little("stat", 64)
    fl = little("fl", 32).rearrange("p (t h) -> p t h", t=4)
    wab = little("wab", 64)
    assert so[0] <= small + 4 * 560
    conv_col = colp[:, 0:48].rearrange("p (i k h) -> p k i h", i=4, k=3)
    prew_col, aprew_col, mprew_col, gnw_col = colp[:, 48:56], colp[:, 56:64], colp[:, 64:72], colp[:, 72:73]

    banks = [nc.alloc_psum_tensor(f"bank{b}", [P, 512], F32).ap() for b in range(8)]

    ident_b = at("ident_b", small + 4 * 560, [P, P], BF16)
    causal_b = at("causal_b", small + 4 * 560 + 256, [P, P], BF16)
    notbefore_b = at("notbefore_b", small + 4 * 560 + 512, [P, P], BF16)

    def v4(x):
        return x.rearrange("p (c f) -> p c f", c=4)

    def over4(m):
        return m.unsqueeze(1).broadcast_to([P, 4, P])

    def along(c4):
        return c4.unsqueeze(2).broadcast_to([P, 4, P])

    w1, w2 = t["w_in"], t["w_in_2"]
    filled = [Signal(counts, f"slab{s}_filled", 16) for s in range(4)]
    hi_done = [Signal(counts, f"slab{s}_hi") for s in range(4)]
    lo_done = [Signal(counts, f"slab{s}_lo") for s in range(4)]
    used = [Signal(counts, f"slab{s}_used") for s in range(4)]
    fills = [Count(dma_counts, f"fills{s}") for s in range(4)]

    sp_waited = nc.alloc_semaphore("sp_waited")

    def fill(s, parts):
        if not fills[s].zero():
            nc.sync.wait_ge(lo_done[s].sem, fills[s].value())
            nc.sync.sem_inc(sp_waited, 1)
        fills[s].add()
        for dst, src in parts:
            nc.sync.dma_start(dst, src).then_inc(filled[s].sem, 16)

    def cols(w, c0, k0=0):
        return w[0].rearrange("(k p) n -> p k n", p=P)[:, k0:k0 + 4, bass.ds(c0, P)]

    def tall(s, w, c0):
        fill(s, [(k8(s)[:, 0:4, :], cols(w, c0)), (k8(s)[:, 4:8, :], cols(w, c0, 4))])

    def wide(s, w, k0, c0):
        rows = w[0].rearrange("(k p) n -> p k n", p=P)
        fill(s, [(k2(s)[:, j:j + 1, :], rows[:, bass.ds(k0 + j, 1), c0:c0 + 512]) for j in range(2)])

    def slot(s):
        return raw_ring[:, s, :]

    def k8(s):
        return slot(s).rearrange("p (k n) -> p k n", k=8)

    def k2(s):
        return slot(s).rearrange("p (k n) -> p k n", k=2)

    A_COLS = [2048, 2560, 3072, 0, 512, 1024, 1536, 3584]
    B_COLS = [0, 512, 1024, 1536, 2048, 2560]
    MERGE0 = 4104

    stage = at("stage", r4, [P, P])
    xnat = x1
    x_in = []
    for j in range(NT):
        x_in.append(Signal(counts, f"x{j}_in", 16).by(nc.sync.dma_start(xnat[:, j, :], t["x"][0, j * P:(j + 1) * P, :])))
    rows_dma = Signal(counts, "rows_in", 16)
    rows_dma.by(nc.scalar.dma_start(consts[:, 0, :], t["shape_consts"][:, 0:P]))
    row = 0
    for name, n in (("conv_w", 48), ("pre_norm_w", 8), ("ln_attn_pre_2", 8), ("ln_mlp_pre_2", 8), ("gdn_norm_w", 1)):
        src = t[name]
        flat = src.rearrange("a i (n c) -> (a i n) c", c=P) if len(src.shape) == 3 else src.rearrange("a (n c) -> (a n) c", c=P)
        rows_in = rows_dma.by(nc.scalar.dma_start(stage[row:row + n, :], flat))
        row += n
    wab_dma, mats_dma, small_dma = (Signal(counts, n, 16) for n in ("wab_in", "mats_in", "small_in"))
    hot = at("bucket_hot", r4 + 54 * KB, [32, 384])
    rel = at("rel", r4 + 56 * KB, [32, 4])
    lam_v = [at(f"lam{n}", r4 + 1024 + 256 * n, [P, 64]) for n in range(4)]

    def small_inputs():
        wab_dma.by(nc.sync.dma_start(wab.rearrange("p (k n) -> p k n", k=8),
                                     w1[0].rearrange("(k p) n -> p k n", p=P)[:, :, 4096:4104]))
        mats_dma.by(nc.sync.dma_start(consts[:, 1:17, :].rearrange("p a b -> p (a b)"), t["shape_consts"][:, P:]))
        small = [(dtb, t["dt_bias"][0].partition_broadcast(P)), (alog, t["a_log"][0].partition_broadcast(P)),
                 (bfb, t["b_f_2"][0].partition_broadcast(P)), (hot, t["bias_consts"][:, 0:384]), (rel, t["rel_bias_2"])]
        small += [(v, t[n][0].partition_broadcast(P)) for v, n in zip(lam_v, ("lam_q1_2", "lam_k1_2", "lam_q2_2", "lam_k2_2"))]
        for dst, src in small:
            small_dma.by(nc.sync.dma_start(dst, src))

    def sp_stream():
        n = [0]

        def nxt():
            n[0] += 1
            return (n[0] - 1) % 4

        for n_, c in enumerate(A_COLS):
            s = nxt()
            tall(s, w1, c)
            if n_ == 1:
                small_inputs()
        with dma_counts.fori("slabs_a", 1, 4, [ET.SP]) as i:
            for c in A_COLS:
                s = nxt()
                tall(s, w1, i * P + c)
        with dma_counts.fori("slabs_merge", 0, 4, [ET.SP]) as i:
            for c in range(4):
                s = nxt()
                tall(s, w1, i * 512 + (MERGE0 + c * P))
        if stop == "A":
            for c in range(2):
                s = nxt()
                fill(s, [(k8(s)[:, 0:4, :], cols(t["w_branch_sb"], c * P)),
                         (k8(s)[:, 4:8, :], cols(t["w_branch_gdn"], c * P))])
            return
        with dma_counts.fori("slabs_branch", 0, 2, [ET.SP]) as i:
            for c in range(4):
                s = nxt()
                fill(s, [(k8(s)[:, 0:4, :], cols(t["w_branch_sb"], i * 512 + c * P)),
                         (k8(s)[:, 4:8, :], cols(t["w_branch_gdn"], i * 512 + c * P))])
        for half in range(2):
            for kk in range(4):
                s = nxt()
                wide(s, t["w_out"], 2 * kk, half * 512)
        for i in range(1):
            for n_, c in enumerate(B_COLS[:2] if stop == "Y" else B_COLS):
                tall(n_ % 4, w2, c)
        if stop == "Y":
            return
        with dma_counts.fori("slabs_b", 1, 4, [ET.SP]) as i:
            for n_, c in enumerate(B_COLS):
                tall(n_ % 4, w2, i * P + c)
        for half in range(2):
            for kk in range(4):
                if stop == "M" and (half or kk > 1):
                    break
                s = nxt()
                wide(s, t["w_out_2"], 2 * kk, half * 512)
        if stop == "M":
            return
        with dma_counts.fori("slabs_up", 0, 8, [ET.SP]) as i:
            for c in range(4):
                s = nxt()
                tall(s, t["w_up_2"], i * 512 + c * P)
        for half in range(2):
            with dma_counts.fori(f"slabs_down{half}", 0, 4, [ET.SP]) as i:
                for c in range(4):
                    s = nxt()
                    wide(s, t["w_down_2"], i * 8 + 2 * c, half * 512)

    sp_stream()
    wab_in, mats_in, small_in = wab_dma.now(), mats_dma.now(), small_dma.now()

    n_split = [0]
    TOTAL = 10 ** 9

    def split(s):
        filled[s].count.add(32)
        A.wait((filled[s].sem, filled[s].count.value(), filled[s].count.base + filled[s].count.local, counts.loop))
        A.wait(used[s].now())
        h = hi_done[s].by(act.copy(ring[:, s, 0, :], slot(s)))
        G.wait(h)
        lo_done[s].by(pool.tensor_tensor(ring[:, s, 1, :], slot(s), ring[:, s, 0, :].bitcast(F32), ALU.subtract))

    acc_free = [Signal(counts, f"acc{b}_free") for b in range(2)]

    def product(s, acc, terms, pieces=24, first_wait=(), opened=False, k_ready=None):
        PE.wait(lo_done[s].now(), *first_wait)
        n = len(terms)
        for j, (o, l, r, a, b) in enumerate(terms):
            if k_ready and j % 3 == 0:
                PE.wait(k_ready[j // 3])
            m = pe.matmul(o, l, r, start=a, stop=b, skip_group_check=opened)
            if j == n - 1:
                used[s].by(m)
            elif (j + 1) % (n // pieces) == 0:
                yield 0
        yield 0

    def terms_T(s, acc, ks=range(8), src=None):
        src = hT if src is None else src
        w = ring[:, s].rearrange("p two (k n) -> p two k n", k=8)
        out_ = []
        ks = list(ks)
        for n, (kw, kx) in enumerate(ks):
            for m, (a, b) in enumerate(((0, 0), (0, 1), (1, 0))):
                out_.append((acc, w[:, a, kw, :], src[:, b, kx, :], n == 0 and m == 0, n == len(ks) - 1 and m == 2))
        return out_

    all_k = [(k, k) for k in range(KT)]

    def ahead(s):
        split(s)

    act.preload_act_table_set("natural_log_exp_and_others")
    V.did(dve.memset(eps_c, EPS))
    V.did(dve.memset(one_c, 1.0))
    half_c = little("half_c", 4)
    neghalf = V.did(dve.memset(half_c, -0.5))
    G.wait(neghalf)
    A.wait(neghalf)
    lam_init = 0.8 - 0.6 * float(np.exp(-0.3 * 0))
    PE.wait(rows_in)
    tok = PE.did(pe.transpose(banks[2][:, 0:row], stage[0:row, :], ident[0:row, 0:row]))
    V.wait(tok)
    cols_ready = V.did(dve.tensor_copy(colp[:, 0:row], banks[2][:, 0:row]))

    def small_constants():
        yield 20
        V.wait(mats_in, small_in)
        V.did(dve.tensor_copy(ident_b, ident))
        V.did(dve.tensor_copy(causal_b, mat["causal"]))
        V.did(dve.tensor_copy(notbefore_b, mat["notbefore"]))
        lq1, lk1, lq2, lk2 = lam_v
        V.did(dve.tensor_tensor(lq1, lq1, lk1, ALU.mult))
        tok = V.did(dve.tensor_tensor(lq2, lq2, lk2, ALU.mult))
        V.wait(tok)
        V.did(dve.tensor_reduce(stat[:, 60:61], lq1, AXX, ALU.add))
        tok = V.did(dve.tensor_reduce(stat[:, 61:62], lq2, AXX, ALU.add))
        A.wait(tok)
        tok = A.did(act.activation(stat[:, 62:64], stat[:, 60:62], ACT.Exp))
        V.wait(tok)
        tok = V.did(dve.tensor_tensor(lam_c, stat[:, 62:63], stat[:, 63:64], ALU.subtract))
        V.wait(tok)
        V.did(dve.tensor_scalar(lam_c, lam_c, lam_init, None, ALU.add))

    far = little("far", 4)
    skew = nc.dram_tensor("skew", (4, P * 384 + 128), F32, kind="Internal").ap()
    skew_dma = Signal(counts, "skew_written", 16)

    def distance_bias():
        relb = at("relb", r4 + 57 * KB, [32, 4, P])
        fw = at("fw", r4 + 60 * KB, [P, 4, 384])
        yield 24
        V.wait(small_in)
        rb = V.did(dve.tensor_copy(relb, rel.unsqueeze(2).broadcast_to([32, 4, P])))
        yield 2
        PE.wait(rb, *bank_free)
        for h in range(4):
            m = pe.matmul(banks[2 + h][:, 0:384], relb[:, h, :], hot, start=True, stop=True)
        p_ = PE.did(m)
        A.wait(p_)
        for h in range(4):
            fr = A.did(act.copy(fw[:, h, :], banks[2 + h][:, 0:384]))
        A.wait(fr)
        V.wait(fr)
        V.did(dve.tensor_copy(far, fw[:, :, 0]))
        for h in range(4):
            skew_dma.by(act.dma_start(skew[h, 0:P * 384].rearrange("(p m) -> p m", p=P), fw[:, h, :]))

    WARM = [5.2, 6.0]
    pool_held = nc.alloc_semaphore("pool_held")

    def rstd(dst, total, n, ready):
        G.wait(ready)
        if counts.loop:
            G.hold(pool_held)
        a = G.did(pool.tensor_scalar(dst, total, 1.0 / n, EPS, ALU.mult, ALU.add))
        G.wait(a)
        w = dst.shape[1]
        return G.did(pool.tensor_tensor(dst, dst, half_c[:, 0:1].broadcast_to([P, w]) if w > 1 else half_c[:, 0:1], ALU.pow))

    def keep_warm(bank, us):
        for _ in range(int(us * 2400 / (4 * T))):
            m = pe.matmul(bank, ident, over4(ident), start=True, stop=True)
        return m

    def norm_tile(j, src, scratch, stats, ready):
        A.wait(ready)
        a = A.did(act.activation(scratch[:, j, :], src[:, j, :], ACT.Square, accum_out=stats[:, j:j + 1]))
        r = rstd(stats[:, j:j + 1], stats[:, j:j + 1], D, a)
        V.wait(r)
        return V.did(dve.tensor_scalar(scratch[:, j, :], src[:, j, :], stats[:, j:j + 1], None, ALU.mult))

    def transpose_normed(scratch, weight_col, scaled):
        norm_banks = (2, 3, 4, 5, 6, 7, 1)
        free = {b: None for b in norm_banks}
        ready = []
        split(0)
        for k in range(KT):
            b = norm_banks[k % len(norm_banks)]
            PE.wait(free[b], *scaled)
            for j in range(NT):
                m = pe.transpose(banks[b][:, j * P:(j + 1) * P], scratch[:, j, k * P:(k + 1) * P], ident)
            tp = PE.did(m)
            A.wait(tp)
            h = A.did(act.activation(hT[:, 0, k, :], banks[b], ACT.Copy, scale=weight_col[:, k:k + 1]))
            V.wait(h)
            free[b] = V.did(dve.scalar_tensor_tensor(hT[:, 1, k, :], banks[b], weight_col[:, k:k + 1],
                                                     hT[:, 0, k, :].bitcast(F32), ALU.mult, ALU.subtract))
            ready.append(free[b])
            if k == 1:
                split(1)
        return ready

    PE.did(keep_warm(banks[3], WARM[0]))
    scr = at("norm_scratch", r4 + 2 * KB, [P, NT, D])
    PE.wait(cols_ready)
    A.wait(cols_ready)
    scaled = [norm_tile(j, xnat, scr, stat[:, 0:4], x_in[j]) for j in range(NT)]
    h_ready = bank_free = transpose_normed(scr, prew_col, scaled)

    def narrow(w, sums, accT, acc, free):
        PE.wait(*free)
        for k in range(KT):
            for m, (a, b) in enumerate(((0, 0), (0, 1), (1, 0))):
                q = pe.matmul(accT[0:8, :], w[:, a, k, :], hT[:, b, k, :], start=k == 0 and m == 0, stop=k == KT - 1 and m == 2)
        tok = PE.did(q)
        V.wait(tok)
        tok = V.did(dve.tensor_copy(sums, accT[0:8, :]))
        yield 1.5
        PE.wait(tok)
        for j in range(NT):
            q = pe.transpose(acc[:, j * 8:(j + 1) * 8], sums[:, j * P:(j + 1) * P], ident[0:8, 0:8])
        return PE.did(q)

    def step_gates():
        yield 16
        ab = at("ab", r4 + 20 * KB, [P, 4, 8])
        wab_s = at("wab_s", r4 + 20 * KB + 256, [P, 2, 64], F32R)
        A.wait(wab_in)
        tok = A.did(act.copy(wab_s[:, 0, :], wab))
        V.wait(tok)
        tok = V.did(dve.tensor_tensor(wab_s[:, 1, :], wab, wab_s[:, 0, :].bitcast(F32), ALU.subtract))
        yield 2
        wabk = wab_s.rearrange("p two (k n) -> p two k n", k=8)

        tok = yield from narrow(wabk, at("ab_sums", r4 + 22 * KB, [8, T]), banks[5], banks[6], (tok, *bank_free))
        V.wait(tok)
        tok = V.did(dve.tensor_copy(ab, banks[6][:, 0:32].rearrange("p (c n) -> p c n", c=4)))
        V.wait(tok, small_in, mats_in)
        sp_z = at("sp_z", r4 + 21 * KB, [P, 4, 4])
        sp_e = at("sp_e", r4 + 21 * KB + 64, [P, 4, 4])
        be = at("be", r4 + 21 * KB + 128, [P, 4, 4])
        ea = at("ea", r4 + 21 * KB + 192, [P, 4])
        tok = V.did(dve.tensor_tensor(sp_z, ab[:, :, 0:4], dtb.unsqueeze(1).broadcast_to([P, 4, 4]), ALU.add))
        V.wait(tok)
        A.wait(tok)
        tok = A.did(act.activation(sp_e, sp_z, ACT.Abs))
        A.wait(tok)
        tok = A.did(act.activation(sp_e, sp_e, ACT.Exp, scale=-1.0))
        A.wait(tok)
        A.did(act.activation(sp_e, sp_e, ACT.Ln, bias=one_c))
        A.did(act.activation(ea, alog, ACT.Exp))
        tok = A.did(act.activation(be, ab[:, :, 4:8], ACT.Exp, scale=-1.0))
        V.wait(tok)
        tok = V.did(dve.scalar_tensor_tensor(sp_z, sp_z, 0.0, sp_e, ALU.max, ALU.add))
        V.did(dve.tensor_scalar(be, be, 1.0, None, ALU.add))
        tok = V.now()
        V.wait(tok)
        V.did(dve.scalar_tensor_tensor(gates[:, :, 0, :].rearrange("p h c -> p c h"), sp_z, -1.0,
                                       ea.unsqueeze(1).broadcast_to([P, 4, 4]), ALU.mult, ALU.mult))
        tok = V.did(dve.reciprocal(gates[:, :, 1, :].rearrange("p h c -> p c h"), be))
        g_all = gates[:, :, 0, :]
        yield 3
        PE.wait(tok)
        gb = banks[7].rearrange("p (a n) -> p a n", a=8)
        for n, m in enumerate(("upper", "after", "ones")):
            q = pe.matmul(gb[:, n, 0:16].rearrange("p (h c) -> p h c", h=4), mat[m], g_all, start=True, stop=True)
        tok = PE.did(q)
        A.wait(tok)
        for n in range(3):
            tok = A.did(act.activation(gates[:, :, 2 + n, :], gb[:, n, 0:16].rearrange("p (h c) -> p h c", h=4), ACT.Exp))
        V.wait(tok)
        V.did(dve.tensor_tensor(gates[:, :, 2, :], gates[:, :, 2, :], gates[:, :, 1, :], ALU.mult))

    off = [r4]

    def take(name, shape, dt=F32):
        n = int(np.prod(shape[1:])) * 4
        a = at(name, off[0], shape, dt)
        off[0] += n
        return a

    osb = take("osb", [P, 2, 4, T], F32R)
    ogd = take("ogd", [P, 2, 4, T], F32R)
    r_work = off[0]
    rawA = off[0]
    cin = take("cin", [P, 3, T + 4])
    rawg = take("rawg", [P, T])
    rawsb = take("rawsb", [P, 4, T])
    gbuf = [take(f"g{n}", [P, T]) for n in range(16)]
    sbuf_ = [take(f"s{n}", [P, T]) for n in range(10)]
    assert off[0] <= nc.sbuf_usable_end, off[0] - r4

    zeros = V.did(dve.memset(cin[:, :, 0:4], 0.0))

    raw_tiles = [cin[:, 0, 3:3 + T], cin[:, 1, 3:3 + T], cin[:, 2, 3:3 + T]] + [rawsb[:, n, :] for n in range(4)] + [rawg]

    def project(tiles, slots, reads, nslab, k_ready=None):
        for n, dst in enumerate(tiles):
            s, b = slots[n], n % 2
            yield from product(s, banks[b], terms_T(s, banks[b], all_k), first_wait=(acc_free[b].now(),),
                               k_ready=None if n else k_ready)
            split((s + 2) % 4)
            assert reads is None or n in reads, n
            A.wait(used[s].now(), reads[n] if reads else None)
            acc_free[b].by(act.copy(dst, banks[b]))

    def fence(main_only=False):
        marks = [e.now() for e in engines] + [a.now() for a in acc_free]
        return marks

    def sigmoid_ln(dst, x, ready):
        A.wait(ready)
        a = A.did(act.activation(dst, x, ACT.Abs))
        A.wait(a)
        a = A.did(act.activation(dst, dst, ACT.Exp, scale=-1.0))
        A.wait(a)
        return A.did(act.activation(dst, dst, ACT.Ln, bias=one_c))

    def sigmoid_exp(dst, x, ready):
        V.wait(ready)
        b = V.did(dve.scalar_tensor_tensor(dst, x, 0.0, dst, ALU.min, ALU.subtract))
        A.wait(b)
        return A.did(act.activation(dst, dst, ACT.Exp))

    def times(dst, x, y, ready):
        V.wait(ready)
        return V.did(dve.tensor_tensor(dst, x, y, ALU.mult))

    heads_end = [None, None]

    def delta_head(i, reads, marks):
        qT, kT, bv, bk, kd, qg, intra, MT, Ca, Cb, X, XT, PP, misc, tmp, gate = gbuf
        S, sg = misc[:, 0:P], misc
        for e in engines:
            e.wait(*marks)
        V.did(dve.tensor_copy(hs, gates[:, i]))
        tok = V.did(dve.tensor_copy(cw, conv_col[:, :, :, i]))
        G.wait(tok)
        ug = G.did(pool.tensor_tensor(v4(Ca), over4(mat["upper"]), along(hs[:, 0, :]), ALU.mult))
        slg = G.did(pool.tensor_tensor(v4(Cb), over4(mat["after"]), along(hs[:, 0, :]), ALU.mult))
        V.wait(tok)

        def conv(n, dst):
            tok = V.did(dve.tensor_scalar(dst, cin[:, n, 0:T], cw[:, n, 0:1], None, ALU.mult))
            for j in range(1, 4):
                V.wait(tok)
                tok = V.did(dve.scalar_tensor_tensor(dst, cin[:, n, j:j + T], cw[:, n, j:j + 1], dst, ALU.mult, ALU.add))
            reads[n] = tok
            return tok

        cq = conv(0, qT)
        yield 1
        lq = sigmoid_ln(tmp, qT, cq)
        ck = conv(1, kT)
        PE.wait(ug)
        pe.matmul(banks[5], mat["after"], Ca, start=True, stop=True)
        p3 = PE.did(pe.matmul(banks[7], mat["ones"], Ca, start=True, stop=True))
        yield 2
        lk = sigmoid_ln(XT, kT, ck)
        sq_ = sigmoid_exp(tmp, qT, lq)
        cv = conv(2, PP)
        PE.wait(slg)
        p2 = PE.did(pe.matmul(banks[6], mat["upper"], Cb, start=True, stop=True))
        yield 2.5
        sk_ = sigmoid_exp(XT, kT, lk)
        cq = times(qT, qT, tmp, sq_)
        A.wait(cq)
        aq = A.did(act.activation(tmp, qT, ACT.Square))
        A.wait(p2)
        eDT = A.did(act.activation(Ca, banks[5], ACT.Exp))
        yield 2
        lv = sigmoid_ln(X, PP, cv)
        ck = times(kT, kT, XT, sk_)
        A.wait(ck)
        ak = A.did(act.activation(XT, kT, ACT.Square))
        PE.wait(aq, eDT)
        pq = PE.did(pe.matmul(banks[5], mat["ones"], tmp, start=True, stop=True))
        yield 1.5
        eD = A.did(act.activation(Cb, banks[6], ACT.Exp))
        er = A.did(act.activation(misc, banks[7], ACT.Exp))
        G.wait(eDT)
        mDT = G.did(pool.tensor_tensor(v4(Ca), v4(Ca), over4(mat["upper"]), ALU.mult))
        G.wait(eD)
        a = G.did(pool.tensor_tensor(v4(Cb), v4(Cb), over4(mat["after"]), ALU.mult))
        G.wait(a)
        mD = G.did(pool.tensor_tensor(v4(Cb), v4(Cb), along(hs[:, 1, :]), ALU.mult))
        sv_ = sigmoid_exp(X, PP, lv)
        cv = times(PP, PP, X, sv_)
        yield 3
        PE.wait(ak, eD)
        pk = PE.did(pe.matmul(banks[6], mat["ones"], XT, start=True, stop=True))
        PE.wait(cv, er)
        for c in range(4):
            m = pe.transpose(banks[7][:, c * P:(c + 1) * P], PP[:, c * P:(c + 1) * P], ident)
        pv = PE.did(m)
        A.wait(pq)
        a = A.did(act.activation(tmp, banks[5], ACT.Ln, bias=eps_c))
        A.wait(pk)
        b = A.did(act.activation(XT, banks[6], ACT.Ln, bias=eps_c))
        A.wait(a)
        a = A.did(act.activation(tmp, tmp, ACT.Exp, scale=-0.5))
        A.wait(b)
        b = A.did(act.activation(XT, XT, ACT.Exp, scale=-0.5))
        V.wait(a)
        nq = V.did(dve.scalar_tensor_tensor(qT, qT, P ** -0.5, tmp, ALU.mult, ALU.mult))
        V.wait(b)
        nk = times(kT, kT, XT, b)
        V.wait(pv)
        vready = V.did(dve.tensor_tensor(v4(bv), v4(banks[7]), along(hs[:, 1, :]), ALU.mult))
        yield 3
        lg = sigmoid_ln(gate, rawg, None)
        yield 0.3
        PE.wait(nq, nk)
        for c in range(4):
            k_ = kT[:, c * P:(c + 1) * P]
            m = pe.matmul(banks[5][:, c * P:(c + 1) * P], k_, k_, start=True, stop=True)
        kk = PE.did(m)
        V.wait(kk, mD)
        mready = V.did(dve.tensor_tensor(X, banks[5], Cb, ALU.mult))
        for c in range(4):
            m = pe.matmul(banks[6][:, c * P:(c + 1) * P], kT[:, c * P:(c + 1) * P], qT[:, c * P:(c + 1) * P], start=True, stop=True)
        qk = PE.did(m)
        PE.wait(vready)
        for c in range(4):
            m = pe.transpose(banks[7][:, c * P:(c + 1) * P], kT[:, c * P:(c + 1) * P], ident)
        pk = PE.did(m)
        V.wait(qk, mDT)
        iready = V.did(dve.tensor_tensor(intra, banks[6], Ca, ALU.mult))
        PE.wait(mready)
        for c in range(4):
            m = pe.transpose(banks[5][:, c * P:(c + 1) * P], X[:, c * P:(c + 1) * P], ident)
        p_ = PE.did(m)
        A.wait(p_)
        mt = A.did(act.copy(MT, banks[5]))
        V.wait(p_)
        a = V.did(dve.tensor_tensor(v4(X), v4(X), over4(level0), ALU.mult))
        V.wait(a, mt)
        V.did(dve.tensor_tensor(v4(X), over4(ident), v4(X), ALU.subtract))
        a = V.did(dve.tensor_tensor(v4(XT), v4(MT), over4(levelT[0]), ALU.mult))
        V.wait(a)
        xr = V.did(dve.tensor_tensor(v4(XT), over4(ident), v4(XT), ALU.subtract))
        G.wait(mt, iready, mready)
        cm = {}
        Cs = (Ca, Cb)
        for l in (1, 2):
            cm[l] = G.did(pool.tensor_tensor(v4(Cs[l % 2]), v4(MT), over4(levelT[l]), ALU.mult))
        yield 5
        kr = None
        for l in range(1, LEVELS):
            C, w_ = Cs[l % 2], 1 << l
            halves = lambda x: x.rearrange("p (cb two w) -> p cb two w", two=2, w=w_)
            chunk_half = lambda x, c, h_: halves(x[:, c * P:(c + 1) * P])[:, :, h_, :]
            compact = lambda x: x[:, 0:T // 2].rearrange("p (cb w) -> p cb w", w=w_)
            PE.wait(cm[l], xr)
            for c in range(4):
                f = slice(c * P, (c + 1) * P)
                m = pe.matmul(banks[5][:, f], C[:, f], X[:, f], start=True, stop=True)
            p1 = PE.did(m)
            A.wait(p1)
            pr = A.did(act.copy(PP, banks[5]))
            if l == 1:
                V.wait(pk)
                V.did(dve.tensor_tensor(v4(bk), v4(banks[7]), along(hs[:, 2, :]), ALU.mult))
                kr = V.did(dve.tensor_tensor(v4(kd), v4(banks[7]), along(hs[:, 3, :]), ALU.mult))
            elif l == 2:
                V.wait(er)
                qgr = V.did(dve.tensor_tensor(qg, qT, misc, ALU.mult))
            elif l == 3:
                sg_ = sigmoid_exp(gate, rawg, lg)
            elif l == 4:
                reads[7] = times(gate, rawg, gate, sg_)
            if l + 2 < LEVELS:
                G.wait(p1)
                cm[l + 2] = G.did(pool.tensor_tensor(v4(C), v4(MT), over4(levelT[l + 2]), ALU.mult))
            yield 1.1
            PE.wait(pr, kr)
            for c in range(4):
                f = slice(c * P, (c + 1) * P)
                o = banks[6][:, c * 64:(c + 1) * 64].rearrange("p (b w) -> p b w", w=w_)
                m = pe.matmul(o, PP[:, f], chunk_half(XT, c, 1), start=True, stop=True)
            p2 = PE.did(m)
            if l < LEVELS - 1:
                for c in range(4):
                    f = slice(c * P, (c + 1) * P)
                    o = banks[7][:, c * 64:(c + 1) * 64].rearrange("p (b w) -> p b w", w=w_)
                    m = pe.matmul(o, XT[:, f], chunk_half(PP, c, 0), start=True, stop=True)
                p3 = PE.did(m)
                V.wait(p3)
                V.did(dve.tensor_tensor(halves(XT)[:, :, 1, :], halves(XT)[:, :, 1, :], compact(banks[6]), ALU.subtract))
                xr = V.did(dve.tensor_tensor(halves(X)[:, :, 0, :], halves(X)[:, :, 0, :], compact(banks[7]), ALU.subtract))
            else:
                V.wait(p2)
                xr = V.did(dve.tensor_tensor(halves(XT)[:, :, 1, :], halves(XT)[:, :, 1, :], compact(banks[6]), ALU.subtract))
            yield 1.3
        PE.wait(xr)
        for c in range(4):
            f = slice(c * P, (c + 1) * P)
            m = pe.matmul(banks[5][:, f], XT[:, f], bv[:, f], start=True, stop=True)
        pu = PE.did(m)
        V.wait(pu)
        u, wT = Ca, Cb
        ur = V.did(dve.tensor_copy(u, banks[5]))
        for c in range(4):
            f = slice(c * P, (c + 1) * P)
            m = pe.matmul(banks[7][:, f], bk[:, f], XT[:, f], start=True, stop=True)
        pw = PE.did(m)
        A.wait(pw)
        wr = A.did(act.copy(wT, banks[7]))
        yield 1
        V.wait(qgr)
        srd = None
        for c in range(4):
            f = slice(c * P, (c + 1) * P)
            if c:
                PE.wait(srd, wr)
                pa = PE.did(pe.matmul(banks[5][:, 0:P], wT[:, f], S, start=True, stop=True))
                V.wait(pa)
                ur = V.did(dve.tensor_tensor(u[:, f], u[:, f], banks[5][:, 0:P], ALU.subtract))
                pe.matmul(banks[7][:, f], S, qg[:, f], start=True, stop=False)
                yield 0.3
            PE.wait(ur, iready, wr)
            po = PE.did(pe.matmul(banks[7][:, f], u[:, f], intra[:, f], start=c == 0, stop=True))
            if c < 3:
                ps = PE.did(pe.matmul(banks[6][:, 0:P], kd[:, f], u[:, f], start=True, stop=True))
                V.wait(ps)
                if c == 0:
                    srd = V.did(dve.tensor_copy(S, banks[6][:, 0:P]))
                else:
                    srd = V.did(dve.scalar_tensor_tensor(S, S, hs[:, 4, c:c + 1], banks[6][:, 0:P], ALU.mult, ALU.add))
                yield 0.6
        yield 0.5
        V.wait(po)
        oc = V.did(dve.tensor_copy(X, banks[7]))
        A.wait(oc)
        a = A.did(act.activation(tmp, X, ACT.Square))
        PE.wait(a)
        p_ = PE.did(pe.matmul(banks[5], mat["ones"], tmp, start=True, stop=True))
        A.wait(p_)
        b = A.did(act.activation(tmp, banks[5], ACT.Ln, bias=eps_c, scale=1.0 / P))
        A.wait(b)
        b = A.did(act.activation(tmp, tmp, ACT.Exp, scale=-0.5))
        V.wait(b, oc)
        d_ = V.did(dve.scalar_tensor_tensor(X, X, gnw_col, tmp, ALU.mult, ALU.mult))
        V.wait(d_)
        d_ = V.did(dve.tensor_tensor(X, X, gate, ALU.mult))
        A.wait(d_)
        a = A.did(act.copy(ogd[:, 0, i, :], X))
        V.wait(a)
        heads_end[1] = V.did(dve.tensor_tensor(ogd[:, 1, i, :], X, ogd[:, 0, i, :].bitcast(F32), ALU.subtract))

    def stick_pair(i, reads, marks):
        qc, kc, vn, La, Lb, pa, pb, Csa, Csb, gate = sbuf_
        state = {}

        def start():
            for e in engines:
                e.wait(*marks)
            reads[3] = V.did(dve.tensor_scalar(qc, rawsb[:, 0, :], 64 ** -0.5, None, ALU.mult))
            reads[4] = state["qk"] = V.did(dve.tensor_copy(kc, rawsb[:, 1, :]))
            for c in range(4):
                m = pe.transpose(banks[4][:, c * P:(c + 1) * P], rawsb[:, 2, c * P:(c + 1) * P], ident)
            reads[5] = p_ = PE.did(m)
            A.wait(p_)
            state["v"] = A.did(act.copy(vn, banks[4]))

        def head(h):
            yield 12
            if not h:
                start()
            yield 2.5
            L, a_buf, Cs, bank = ((La, pa, Csa, banks[2]), (Lb, pb, Csb, banks[3]))[h]
            hp = slice(64 * h, 64 * h + 64)
            PE.wait(state["qk"], state["v"])
            z = PE.did(pe.matmul(bank[:, 0:P], kc[hp, 3 * P:T], qc[hp, 3 * P:T], start=True, stop=True))
            csum = av = None
            for j in (3, 2, 1, 0):
                q0, w = P * j, T - P * j
                A.wait(z, av)
                s_ = A.did(act.activation(a_buf[:, 0:w], bank[:, 0:w], ACT.Abs))
                A.wait(s_)
                s_ = A.did(act.activation(a_buf[:, 0:w], a_buf[:, 0:w], ACT.Exp, scale=-1.0))
                A.wait(s_)
                s_ = A.did(act.activation(a_buf[:, 0:w], a_buf[:, 0:w], ACT.Ln, bias=one_c))
                V.wait(s_, csum)
                l_ = V.did(dve.scalar_tensor_tensor(L[:, 0:w], bank[:, 0:w], 0.0, a_buf[:, 0:w], ALU.max, ALU.add))
                V.wait(l_)
                l_ = V.did(dve.tensor_tensor(L[:, 0:P], L[:, 0:P], mat["before"], ALU.mult))
                yield 1.6 + 4 * w / 1000
                PE.wait(l_, csum)
                pe.matmul(bank[:, 0:P], ident_b, notbefore_b, start=False, stop=True, skip_group_check=True)
                m = pe.matmul(bank[:, 0:w], mat["negtri"], L[:, 0:w], start=False, stop=True, skip_group_check=True)
                if j < 3:
                    m = pe.matmul(bank[:, P:w], mat["negones"], Cs[:, q0 + P:T], start=False, stop=True, skip_group_check=True)
                la = PE.did(m)
                A.wait(la)
                a_ = A.did(act.activation(a_buf[:, 0:w], bank[:, 0:w], ACT.Exp))
                if j:
                    G.wait(la)
                    if j < 3:
                        G.did(pool.tensor_tensor(Cs[:, q0 + P:T], Cs[:, q0 + P:T], L[:, P:w], ALU.add))
                    csum = G.did(pool.tensor_tensor(Cs[:, q0:q0 + P], L[:, 0:P], mat["ones"], ALU.mult))
                if h == 0 and j == 2:
                    b = sigmoid_ln(gate, rawsb[:, 3, :], None)
                    b = sigmoid_exp(gate, rawsb[:, 3, :], b)
                    state["gate"] = reads[6] = times(gate, rawsb[:, 3, :], gate, b)
                yield 0.4 + w / 1000
                PE.wait(a_)
                if j:
                    z = PE.did(pe.matmul(bank[:, 0:w + P], kc[hp, q0 - P:q0], qc[hp, q0 - P:T], start=True, stop=True))
                av = PE.did(pe.matmul(banks[4][hp, q0:T], vn[:, j * P + 64 * h:j * P + 64 * h + 64],
                                      a_buf[:, 0:w], start=j == 3, stop=True, skip_group_check=True))
            state[h] = av
            if (1 - h) in state:
                V.wait(state[0], state[1], state["gate"])
                b = V.did(dve.tensor_tensor(La, gate, banks[4], ALU.mult))
                A.wait(b)
                a = A.did(act.copy(osb[:, 0, i, :], La))
                V.wait(a)
                heads_end[0] = V.did(dve.tensor_tensor(osb[:, 1, i, :], La, osb[:, 0, i, :].bitcast(F32), ALU.subtract))

        return [head(0), head(1)]

    slotsA = [n % 4 for n in range(8)]
    A.wait(zeros)
    interleave(pe, project(raw_tiles, slotsA, None, 8, h_ready), [step_gates(), distance_bias(), small_constants()])
    skew_written = skew_dma.now()
    for e in engines:
        e.wait(skew_written)
    with loop("stage_a", 1, 4) as i:
        reads, marks = {}, fence()
        interleave(pe, project(raw_tiles, slotsA, reads, 8), [delta_head(i - 1, reads, marks), *stick_pair(i - 1, reads, marks)])

    sig_sb = at("sig_sb", r_res, [P, 8, T])
    sig_gd = at("sig_gd", rawA, [P, 8, T])
    reads, marks = {}, fence()

    def merge_gates():
        last_exp = None
        for n in range(16):
            s, b = n % 4, n % 2
            yield from product(s, banks[b], terms_T(s, banks[b], all_k), first_wait=(acc_free[b].now(),))
            split((s + 2) % 4)
            if last_exp:
                A.wait(last_exp[1])
                A.did(act.activation(last_exp[0], last_exp[0], ACT.Exp))
            dst = sig_sb[:, n, :] if n < 8 else sig_gd[:, n - 8, :]
            A.wait(used[s].now())
            if n == 8:
                A.wait(*[reads[r] for r in range(8)])
            e_ = A.did(act.activation(dst, banks[b], ACT.Abs))
            A.wait(e_)
            e_ = A.did(act.activation(dst, dst, ACT.Exp, scale=-1.0))
            A.wait(e_)
            e_ = A.did(act.activation(dst, dst, ACT.Ln, bias=one_c))
            V.wait(e_)
            last_exp = dst, acc_free[b].by(dve.scalar_tensor_tensor(dst, banks[b], 0.0, dst, ALU.min, ALU.subtract))
        A.wait(last_exp[1])
        A.did(act.activation(last_exp[0], last_exp[0], ACT.Exp))

    interleave(pe, merge_gates(), [delta_head(3, reads, marks), *stick_pair(3, reads, marks)])
    def dump(parts):
        nc.sync.wait_ge(*[(s[0], s[1]) for s in [A.now()]][0])
        for e in engines + acc_free:
            if e.now():
                nc.sync.wait_ge(*e.now()[:2])
        d = Signal(counts, "dump", 16)
        c0 = 0
        for p_ in parts:
            n_ = int(np.prod(p_.shape[1:]))
            d.by(nc.sync.dma_start(dbg[0:p_.shape[0], c0:c0 + n_], p_.bitcast(F32) if p_.dtype == F32R else p_))
            c0 += n_
        nc.sync.wait_ge(d.sem, d.count.value())

    if stop == "A":
        fl_ = lambda x: x.rearrange("p a b -> p (a b)") if len(x.shape) == 3 else x.rearrange("p a b c -> p (a b c)")
        dump([fl_(osb), fl_(ogd), fl_(sig_sb)])
        return counts.found | dma_counts.found
    merged = at("merged", rawA + 16 * KB + 512, [P, 2, 8, T], F32R)
    mtmp = at("mtmp", rawA + 48 * KB + 512, [P, 2, 2, T])
    marks = fence()
    PE.wait(*heads_end)
    gates_read = acc_free[0].now(), acc_free[1].now()
    pair_free = [Signal(counts, f"pair{b}_free") for b in range(2)]
    mhi = [Signal(counts, f"mtmp{b}_hi") for b in range(2)]
    mlo = [Signal(counts, f"mtmp{b}_lo") for b in range(2)]
    for x in pair_free + mhi + mlo:
        x.prime(V)
    for e in (A, V, G):
        e.wait(*marks)
    with loop("branch", 0, 2) as i:
        for c in range(4):
            s, b = c, c % 2
            ba, bb = banks[2 - 2 * b], banks[3 - 2 * b]
            terms = terms_T(s, ba, [(k, k) for k in range(4)], osb) + terms_T(s, bb, [(4 + k, k) for k in range(4)], ogd)
            for _ in product(s, None, terms, first_wait=(pair_free[b].now(), *(gates_read if b else ()))):
                pass
            split((s + 2) % 4)
            m = 4 * i + c
            V.wait(used[s].now(), mhi[b].now(), mlo[b].now())
            a1 = V.did(dve.tensor_tensor(mtmp[:, b, 0, :], ba, sig_sb[:, m, :], ALU.mult))
            a2 = pair_free[b].by(dve.tensor_tensor(mtmp[:, b, 1, :], bb, sig_gd[:, m, :], ALU.mult))
            V.wait(a1, a2)
            a3 = V.did(dve.tensor_tensor(mtmp[:, b, 0, :], mtmp[:, b, 0, :], mtmp[:, b, 1, :], ALU.add))
            A.wait(a3)
            h_ = mhi[b].by(act.copy(merged[:, 0, m, :], mtmp[:, b, 0, :]))
            V.wait(h_)
            mlo[b].by(dve.tensor_tensor(merged[:, 1, m, :], mtmp[:, b, 0, :], merged[:, 0, m, :].bitcast(F32), ALU.subtract))

    def half_terms(s, src, kk, half_banks, first, last):
        w = ring[:, s].rearrange("p two (k n) -> p two k n", k=2)
        o = []
        for kl in range(2):
            for j in range(NT):
                for m, (a, b) in enumerate(((0, 0), (0, 1), (1, 0))):
                    o.append((banks[half_banks[j]], src[:, a, kk + kl, j * P:(j + 1) * P], w[:, b, kl, :],
                              first and kl == 0 and m == 0, last and kl == 1 and m == 2))
        return o

    def token_terms(src, j, bank):
        o = []
        for s in range(4):
            w = ring[:, s].rearrange("p two (k n) -> p two k n", k=2)
            for kl in range(2):
                for m, (a, b) in enumerate(((0, 0), (0, 1), (1, 0))):
                    o.append((s, banks[bank], src[:, a, 2 * s + kl, j * P:(j + 1) * P], w[:, b, kl, :],
                              s == 0 and kl == 0 and m == 0, s == 3 and kl == 1 and m == 2, kl == 1 and m == 2))
        return o

    def add_normed(j, lo_bank, hi_bank, w_bc, junk, res, stats, done_hi, done_lo, junk_free):
        A.wait(done_lo, junk_free)
        A.did(act.activation(junk[:, 0:512], banks[lo_bank], ACT.Square, accum_out=stats[:, 3 * j:3 * j + 1]))
        A.wait(done_hi)
        a = A.did(act.activation(junk[:, 512:1024], banks[hi_bank], ACT.Square, accum_out=stats[:, 3 * j + 1:3 * j + 2]))
        V.wait(a)
        a = V.did(dve.tensor_tensor(stats[:, 3 * j + 2:3 * j + 3], stats[:, 3 * j:3 * j + 1], stats[:, 3 * j + 1:3 * j + 2], ALU.add))
        r = rstd(stats[:, 3 * j + 2:3 * j + 3], stats[:, 3 * j + 2:3 * j + 3], D, a)
        V.wait(r)
        halves = [(slice(0, 512), lo_bank), (slice(512, 1024), hi_bank)]
        scaled = [V.did(dve.scalar_tensor_tensor(junk[:, f], banks[bank], stats[:, 3 * j + 2:3 * j + 3], w_bc[:, f],
                                                 ALU.mult, ALU.mult)) for f, bank in halves]
        added = []
        for (f, _), s_ in zip(halves, scaled):
            V.wait(s_)
            added.append(V.did(dve.tensor_tensor(res[:, j, f], res[:, j, f], junk[:, f], ALU.add)))
        return added

    def out_projection(src, w_bc, junk, res, res_ready, stats, tiles_done, scratch, norm_stats):
        for kk in range(4):
            s = kk
            PE.wait(*tiles_done.get(kk, ()))
            for _ in product(s, None, half_terms(s, src, 2 * kk, (4, 5, 6, 7), kk == 0, kk == 3)):
                pass
            split((s + 2) % 4)
        left = used[3].now()
        V.wait(res_ready)
        ready, scaled = [], []
        for j in range(NT):
            terms = token_terms(src, j, j)
            for (s, o, l, r, a, b, slab_end) in terms:
                if j == 0:
                    PE.wait(lo_done[s].now())
                m = pe.matmul(o, l, r, start=a, stop=b)
                if j == NT - 1 and slab_end:
                    used[s].by(m)
                if j == 0 and slab_end and s < 2:
                    split(s + 2)
            if j < NT - 1:
                tokd = PE.did(m)
            else:
                tokd = used[3].now()
            ready.append(add_normed(j, 4 + j, j, w_bc, junk[:, j % 2, :], res, stats, tokd, left, ready[j - 2] if j > 1 else None)[-1])
            if j:
                scaled.append(norm_tile(j - 1, res, scratch, norm_stats, ready[j - 1]))
        scaled.append(norm_tile(NT - 1, res, scratch, norm_stats, ready[-1]))
        PE.wait(ready[0])
        keep_warm(banks[0], WARM[1])
        return scaled

    A.wait(*[x.now() for x in pair_free + used])
    ydma = Signal(counts, "reload_x", 16)
    wdma = Signal(counts, "post_w_loaded", 16)
    post_bc = at("post_bc", r4, [P, D])
    junk1 = at("junk1", r4 + 4 * KB, [P, 2, D])
    scr2 = at("norm_scratch2", r4 + 12 * KB, [P, NT, D])
    for j in range(NT):
        xr_ = ydma.by(act.dma_start(x1[:, j, :], t["x"][0, j * P:(j + 1) * P, :]))
    wr_ = wdma.by(act.dma_start(post_bc, t["post_norm_w"][0].partition_broadcast(P)))
    bias_w = at("bias_w", r4 + 32 * KB, [P, 4, T])
    skew_read = Signal(counts, "skew_read", 16)
    for h in range(4):
        src = skew[h, 127:127 + P * 383].rearrange("(p m) -> p m", m=383)[:, 0:256]
        bias_in = skew_read.by(act.dma_start(bias_w[:, h, 256:512], src))
    V.wait(wr_)
    tiles_done = {0: tuple(x.before(1) for x in mlo), 3: tuple(x.now() for x in mlo)}
    scaled = out_projection(merged, post_bc, junk1, x1, xr_, stat[:, 8:20], tiles_done, scr2, stat[:, 4:8])
    if stop == "Y":
        dump([x1.rearrange("p a b -> p (a b)")])
        return counts.found | dma_counts.found
    h_ready = transpose_normed(scr2, aprew_col, scaled)

    off[0] = r4
    mix = take("mix", [P, 2, 8, T], F32R)
    off[0] += 8 * KB
    rawb = take("rawb", [P, 6, T])
    pick = take("pick", [8, 8 * P])
    pick_h = take("pick_h", [8, 2 * P])
    cumT = take("cumT", [8, T])
    wf = take("wf", [P, 64])
    wf_s = take("wf_s", [P, 2, 64], F32R)
    sg_bc = take("sg_bc", [P, P])
    bbuf = [take(f"b{n}", [P, T]) for n in range(17)]
    assert off[0] <= nc.sbuf_usable_end, off[0] - r4
    b2_dma = Signal(counts, "forget_in", 16)
    A.wait(h_ready[-1], PE.now())
    for dst, src in ((wf.rearrange("p (k n) -> p k n", k=8), w2[0].rearrange("(k p) n -> p k n", p=P)[:, :, 3072:3080]),
                     (sg_bc, t["subln_g_2"][0].partition_broadcast(P)), (pick, t["bias_consts"][0:8, 384:])):
        forget_in = b2_dma.by(act.dma_start(dst, src))

    def forget_gates():
        V.wait(bias_in)
        V.did(dve.tensor_copy(bias_w[:, :, 0:256], far.unsqueeze(2).broadcast_to([P, 4, 256])))
        for h in range(4):
            V.did(dve.tensor_tensor(bias_w[:, h, 384:512], bias_w[:, h, 384:512], mat["causal"], ALU.add))
        yield 4
        A.wait(forget_in)
        a = A.did(act.copy(wf_s[:, 0, :], wf))
        V.wait(a)
        V.did(dve.tensor_scalar(sg_bc, sg_bc, 1.0 - lam_init, None, ALU.mult))
        a = V.did(dve.tensor_tensor(wf_s[:, 1, :], wf, wf_s[:, 0, :].bitcast(F32), ALU.subtract))
        yield 2
        p_ = yield from narrow(wf_s.rearrange("p two (k n) -> p two k n", k=8), cumT, banks[5], banks[6], (a, *h_ready))
        fz, fe = stat[:, 0:32].rearrange("p (t h) -> p t h", t=4), stat[:, 32:64].rearrange("p (t h) -> p t h", t=4)
        V.wait(p_)
        a = V.did(dve.tensor_tensor(fz, banks[6][:, 0:32].rearrange("p (t h) -> p t h", t=4),
                                    bfb.unsqueeze(1).broadcast_to([P, 4, 8]), ALU.add))
        A.wait(a)
        a = A.did(act.activation(fe, fz, ACT.Abs))
        A.wait(a)
        a = A.did(act.activation(fe, fe, ACT.Exp, scale=-1.0))
        A.wait(a)
        a = A.did(act.activation(fe, fe, ACT.Ln, bias=one_c))
        V.wait(a)
        a = V.did(dve.scalar_tensor_tensor(fl, fz, 0.0, fe, ALU.min, ALU.subtract))
        yield 4
        PE.wait(a)
        for j in range(NT):
            p_ = pe.matmul(banks[7][0:8, j * P:(j + 1) * P], fl[:, j, :], mat["upper"], start=j == 0, stop=j == 3, skip_group_check=True)
            if j < 3:
                pe.matmul(banks[7][0:8, (j + 1) * P:T].rearrange("p (c f) -> p c f", f=P), fl[:, j, :],
                          mat["ones"].unsqueeze(1).broadcast_to([P, 3 - j, P]), start=False, stop=False, skip_group_check=True)
        V.wait(PE.did(p_))
        V.did(dve.tensor_copy(cumT, banks[7][0:8, :]))

    YB = [3, 2, 5, 3, 1.2, 1, 1, 2.5, 2.5, 1.5]
    v_wait = nc.alloc_semaphore("dve_held")
    tiles_b = [rawb[:, n, :] for n in range(6)]
    slots_b = [0, 1, 2, 3, 0, 1]

    def project_b(reads, k_ready=None):
        for n, dst in enumerate(tiles_b):
            s, b = slots_b[n], n % 2
            yield from product(s, banks[b], terms_T(s, banks[b], all_k), first_wait=(acc_free[b].now(),),
                               k_ready=None if n else k_ready)
            split(slots_b[(n + 2) % 6])
            assert reads is None or n in reads, n
            A.wait(used[s].now(), reads[n] if reads else None)
            acc_free[b].by(act.copy(dst, banks[b]))

    (qd, kd, vd, od, bias_h, *diff_rows) = bbuf[:9]
    (qf, kf, vf, of_, *fox_rows) = bbuf[9:]

    def softmax_scores(bank, w, in1, dst, mx, sm, ready):
        V.wait(*ready)
        V.hold(v_wait)
        a = V.did(dve.tensor_tensor_reduce(out=dst[:, 0:w], in0=bank[:, 0:w], in1=in1, scale=1.0, scalar=-3.0e38,
                                           op0=ALU.add, op1=ALU.max, accum_out=mx))
        V.wait(a)
        a = V.did(dve.tensor_scalar(mx, mx, -1.0, None, ALU.mult))
        A.wait(a)
        return A.did(act.activation(dst[:, 0:w], dst[:, 0:w], ACT.Exp, bias=mx, accum_out=sm))

    def transposed(bank, src, w, ready):
        PE.wait(*ready)
        for c in range(w // P):
            m = pe.transpose(bank[:, c * P:(c + 1) * P], src[:, c * P:(c + 1) * P], ident)
        p_ = PE.did(m)
        A.wait(p_)
        return A.did(act.copy(src[:, 0:w], bank[:, 0:w]))

    def prepare_b(q, k, v, bank, reads, n0):
        reads[n0] = V.did(dve.tensor_scalar(q, rawb[:, n0, :], 64 ** -0.5, None, ALU.mult))
        reads[n0 + 1] = qk = V.did(dve.tensor_copy(k, rawb[:, n0 + 1, :]))
        for c in range(4):
            m = pe.transpose(bank[:, c * P:(c + 1) * P], rawb[:, n0 + 2, c * P:(c + 1) * P], ident)
        reads[n0 + 2] = p_ = PE.did(m)
        A.wait(p_)
        return qk, A.did(act.copy(v, bank))

    def to_mix(src, bank, m, ready):
        PE.wait(*ready)
        for c in range(4):
            q = pe.transpose(bank[:, c * P:(c + 1) * P], src[:, c * P:(c + 1) * P], ident)
        p_ = PE.did(q)
        A.wait(p_)
        a = A.did(act.copy(mix[:, 0, m, :], bank))
        V.wait(a)
        return V.did(dve.tensor_tensor(mix[:, 1, m, :], bank, mix[:, 0, m, :].bitcast(F32), ALU.subtract))

    def diff_head(i, reads, marks):
        done = {}

        def rows(n):
            X, Y = banks[2 + 2 * n], banks[3 + 2 * n]
            scA, scB = diff_rows[2 * n:2 * n + 2]
            st = stat[:, 8 * n:8 * n + 8]
            yield YB[0]
            if n == 0:
                for e in engines:
                    e.wait(*marks)
                done["qk"], done["v"] = prepare_b(qd, kd, vd, X, reads, 0)
                done["bias"] = V.did(dve.tensor_copy(bias_h, bias_w[:, i, :]))
            yield YB[1]
            free = squared = None
            for t_ in ((3, 0), (2, 1))[n]:
                w = (t_ + 1) * P
                es = []
                for m_, (bank, dst) in enumerate(((X, scA), (Y, scB))):
                    hp = slice(64 * m_, 64 * m_ + 64)
                    PE.wait(done["qk"], done["v"], free)
                    z = PE.did(pe.matmul(bank[:, 0:w], qd[hp, t_ * P:w], kd[hp, 0:w], start=True, stop=True))
                    V.wait(squared)
                    es.append(softmax_scores(bank, w, bias_h[:, T - w:T], dst, st[:, 2 * m_:2 * m_ + 1],
                                             st[:, 2 * m_ + 1:2 * m_ + 2], (z, done["bias"])))
                V.wait(es[0])
                V.did(dve.reciprocal(st[:, 4:5], st[:, 1:2]))
                V.wait(es[1])
                a = V.did(dve.reciprocal(st[:, 5:6], st[:, 3:4]))
                V.wait(a)
                a = V.did(dve.scalar_tensor_tensor(st[:, 5:6], st[:, 5:6], -1.0, lam_c, ALU.mult, ALU.mult))
                b_ = V.did(dve.tensor_scalar(scA[:, 0:w], scA[:, 0:w], st[:, 4:5], None, ALU.mult))
                V.wait(b_)
                pr = V.did(dve.scalar_tensor_tensor(scA[:, 0:w], scB[:, 0:w], st[:, 5:6], scA[:, 0:w], ALU.mult, ALU.add))
                yield YB[2] + YB[3] * w / T
                ev = transposed(X, scA, w, (pr,))
                yield YB[4] + YB[5] * w / T
                PE.wait(ev)
                for c in range(t_ + 1):
                    q = pe.matmul(Y[:, 0:P], scA[:, c * P:(c + 1) * P], vd[:, c * P:(c + 1) * P], start=c == 0, stop=c == t_)
                p_ = PE.did(q)
                V.wait(p_)
                free = V.did(dve.tensor_copy(od[:, t_ * P:w], Y[:, 0:P]))
                A.wait(free)
                squared = done[t_] = A.did(act.activation(scA[:, 0:P], od[:, t_ * P:w], ACT.Square,
                                                accum_out=stat[:, 24 + t_:25 + t_]))
                yield YB[6]
            if all(t_ in done for t_ in range(NT)):
                r = rstd(stat[:, 24:28], stat[:, 24:28], P, A.now())
                V.wait(r)
                for t_ in range(NT):
                    f = slice(t_ * P, (t_ + 1) * P)
                    a = V.did(dve.scalar_tensor_tensor(od[:, f], od[:, f], stat[:, 24 + t_:25 + t_], sg_bc, ALU.mult, ALU.mult))
                yield YB[7]
                to_mix(od, X, i, (a,))

        return [rows(0), rows(1)]

    def fox_pair(i, reads, marks):
        done = {}

        def head(h):
            bank = banks[6 + h]
            sc, negcum = fox_rows[2 * h:2 * h + 2]
            st = stat[:, 16 + 4 * h:20 + 4 * h]
            hp = slice(64 * h, 64 * h + 64)
            yield YB[0]
            if h == 0:
                for e in engines:
                    e.wait(*marks)
                done["qk"], done["v"] = prepare_b(qf, kf, vf, bank, reads, 3)
                done["pick"] = V.did(dve.tensor_copy(pick_h, pick[:, bass.ds(2 * i * P, 2 * P)]))
            yield YB[1]
            PE.wait(done["pick"], done["v"])
            p_ = PE.did(pe.matmul(bank, pick_h[:, h * P:(h + 1) * P], cumT, start=True, stop=True))
            A.wait(p_)
            free = A.did(act.copy(negcum, bank))
            yield 1.5
            for t_ in range(NT):
                w = (t_ + 1) * P
                PE.wait(done["qk"], free)
                pe.matmul(bank[:, 0:w], qf[hp, t_ * P:w], kf[hp, 0:w], start=True, stop=True)
                z = PE.did(pe.matmul(bank[:, t_ * P:w], ident_b, causal_b, start=False, stop=True, skip_group_check=True))
                ex = softmax_scores(bank, w, negcum[:, 0:w], sc, st[:, 0:1], st[:, 1:2], (z, free))
                V.wait(ex)
                r = V.did(dve.reciprocal(st[:, 2:3], st[:, 1:2]))
                yield YB[8] + YB[9] * w / T
                ev = transposed(bank, sc, w, (ex,))
                yield YB[4] + YB[5] * w / T
                PE.wait(ev)
                for c in range(t_ + 1):
                    q = pe.matmul(bank[:, 0:64], sc[:, c * P:(c + 1) * P], vf[:, c * P + 64 * h:c * P + 64 * h + 64],
                                  start=c == 0, stop=c == t_)
                p_ = PE.did(q)
                V.wait(p_, r)
                free = V.did(dve.tensor_scalar(of_[:, t_ * P + 64 * h:t_ * P + 64 * h + 64], bank[:, 0:64],
                                               st[:, 2:3], None, ALU.mult))
                yield YB[6]
            done[h] = free
            if (1 - h) in done:
                to_mix(of_, bank, 4 + i, (done[0], done[1]))

        return [head(0), head(1)]

    interleave(pe, project_b(None, h_ready), [forget_gates()])
    with loop("stage_b", 1, 4) as i:
        reads, marks = {}, fence()
        interleave(pe, project_b(reads), [*diff_head(i - 1, reads, marks), *fox_pair(i - 1, reads, marks)])
    reads, marks = {}, fence()
    interleave(pe, None, [*diff_head(3, reads, marks), *fox_pair(3, reads, marks)])
    if stop == "M":
        dump([mix.rearrange("p a b c -> p (a b c)")])
        return counts.found | dma_counts.found

    marks = fence()
    for e in engines:
        e.wait(*marks)
    b2dma = Signal(counts, "post_w2_loaded", 16)
    post2 = at("post2", r4 + 32 * KB, [P, D])
    junk2 = at("junk2", r4 + 36 * KB, [P, 2, D])
    scr3 = at("norm_scratch3", r4 + 44 * KB, [P, NT, D])
    V.wait(b2dma.by(act.dma_start(post2, t["ln_attn_post_2"][0].partition_broadcast(P))))
    scaled = out_projection(mix, post2, junk2, x1, None, stat[:, 8:20], {}, scr3, stat[:, 4:8])
    h_ready = transpose_normed(scr3, mprew_col, scaled)
    u = at("u", r4, [P, 34, T])
    ring_u = at("ring_u", r4 + 68 * KB, [P, 4, 2, 2 * T], F32R)
    relu_done = [Signal(counts, f"relu{b}") for b in range(2)]

    def up_slab(i, c, k_ready=None):
        s, b = c, c % 2
        for _ in product(s, banks[b], terms_T(s, banks[b], all_k), first_wait=(relu_done[b].now(),), k_ready=k_ready):
            pass
        split((s + 2) % 4)
        A.wait(used[s].now())
        r_ = relu_done[b].by(act.activation(u[:, 4 * i + c, :], banks[b], ACT.Relu))
        V.wait(r_)
        V.did(dve.tensor_tensor(u[:, 4 * i + c, :], u[:, 4 * i + c, :], u[:, 4 * i + c, :], ALU.mult))

    for c in range(4):
        up_slab(0, c, None if c else h_ready)
    u_split = [Signal(counts, f"u{s}_split") for s in range(4)]
    r1 = base
    post3 = at("post3", r1, [P, D])
    junk3 = at("junk3", r1 + 4 * KB, [P, 2, D])

    def split_u(k0, s):
        x = u[:, bass.ds(k0, 2), :].rearrange("p a b -> p (a b)")
        A.wait(used[s].now())
        h_ = A.did(act.copy(ring_u[:, s, 0, :], x))
        V.wait(h_)
        u_split[s].by(dve.tensor_tensor(ring_u[:, s, 1, :], x, ring_u[:, s, 0, :].bitcast(F32), ALU.subtract))

    V.wait(V.now())
    A.wait(V.did(dve.tensor_copy(u[:, 32:34, :], u[:, 0:2, :])))
    split_u(0, 0)
    zeros_b = notbefore_b
    zeroed = V.did(dve.memset(zeros_b, 0.0))
    with loop("up", 1, 8) as i:
        for c in range(4):
            up_slab(i, c)
    A.wait(V.now())
    b3dma = Signal(counts, "post_w3_loaded", 16)
    w3 = b3dma.by(act.dma_start(post3, t["ln_mlp_post_2"][0].partition_broadcast(P)))

    def down_slab(i, s, hb, opened=True):
        w = ring[:, s].rearrange("p two (k n) -> p two k n", k=2)
        xs = ring_u[:, s].rearrange("p two (k n) -> p two k n", k=2)
        PE.wait(u_split[s].now())
        split_u(i * 8 + 2 * s + 2, (s + 1) % 4)
        terms = []
        for kl in range(2):
            for j in range(NT):
                for a, b in ((0, 0), (0, 1), (1, 0)):
                    terms.append((banks[hb[j]], xs[:, a, kl, j * P:(j + 1) * P], w[:, b, kl, :], False, True))
        for _ in product(s, None, terms, opened=True):
            pass
        split((s + 2) % 4)

    PE.wait(zeroed)
    for half in range(2):
        hb = [4 - 4 * half + j for j in range(4)]
        PE.wait(*([x.now() for x in relu_done] if half else ()))
        for j in range(4):
            pe.matmul(banks[hb[j]], zeros_b, over4(ident_b), start=True, stop=True)
        with loop(f"down{half}", 0, 4 - half) as i:
            for s in range(4):
                down_slab(i, s, hb)
    split_u(26, 1)
    split(2)
    split_u(28, 2)
    split(3)
    split_u(30, 3)
    last_half0 = used[3].now()
    V.wait(w3)
    outs = Signal(counts, "out_stored", 16)
    done = []
    for j in range(NT):
        for s in range(4):
            w = ring[:, s].rearrange("p two (k n) -> p two k n", k=2)
            xs = ring_u[:, s].rearrange("p two (k n) -> p two k n", k=2)
            PE.wait(u_split[s].now(), lo_done[s].now())
            for kl in range(2):
                for a, b in ((0, 0), (0, 1), (1, 0)):
                    m = pe.matmul(banks[j], xs[:, a, kl, j * P:(j + 1) * P], w[:, b, kl, :], start=False, stop=True,
                                  skip_group_check=True)
        done.append(add_normed(j, 4 + j, j, post3, junk3[:, j % 2, :], x1, stat[:, 8:20], PE.did(m), last_half0,
                               done[j - 2][-1] if j > 1 else None))
        for half, added in enumerate(done[j]):
            nc.sync.wait_ge(*added[:2])
            f = slice(512 * half, 512 * half + 512)
            outs.by(nc.sync.dma_start(out[0, j * P:(j + 1) * P, f], x1[:, j, f]))
    nc.sync.wait_ge(outs.sem, outs.count.value())
    return counts.found | dma_counts.found


def all_inputs(inputs):
    return {**{n: np.ascontiguousarray(inputs[n]) for n in inputs},
            "shape_consts": shape_constants(), "bias_consts": bias_constants()}


_INS = ["x", "pre_norm_w", "post_norm_w", "w_in", "conv_w", "a_log", "dt_bias", "gdn_norm_w", "w_branch_sb",
        "w_branch_gdn", "w_out", "ln_attn_pre_2", "w_in_2", "b_f_2", "lam_q1_2", "lam_k1_2", "lam_q2_2",
        "lam_k2_2", "subln_g_2", "rel_bias_2", "w_out_2", "ln_attn_post_2", "ln_mlp_pre_2", "w_up_2",
        "w_down_2", "ln_mlp_post_2"]


def declared(nc, shapes, per):
    t = {n: nc.dram_tensor(f"in_{n}", s, F32, kind="ExternalInput").ap() for n, s in shapes.items()}
    out = nc.dram_tensor("out_0", shapes["x"], F32, kind="ExternalOutput").ap()
    return program(nc, t, out, per)


def kernel(**inputs):
    import concourse.bacc as _bacc
    from concourse.bass_utils import run_bass_kernel_spmd as _run

    arrays = {n: np.ascontiguousarray(inputs[n]) for n in _INS}
    arrays["shape_consts"] = shape_constants()
    arrays["bias_consts"] = bias_constants()
    shapes = {n: a.shape for n, a in arrays.items()}
    per = declared(_bacc.Bacc("TRN2", target_bir_lowering=False, num_devices=1), shapes, {})
    nc = _bacc.Bacc("TRN2", target_bir_lowering=False, num_devices=1)
    declared(nc, shapes, per)
    r = _run(nc, [{f"in_{n}": a for n, a in arrays.items()}], core_ids=[0])
    return r.results[0]["out_0"]
```

```python
from contextlib import contextmanager

import numpy as np

import concourse.bass as bass
from concourse import mybir

F32 = mybir.dt.float32
F32R = mybir.dt.float32r
BF16 = mybir.dt.bfloat16
ALU = mybir.AluOpType
ACT = mybir.ActivationFunctionType
AXX = mybir.AxisListType.X
ET = mybir.EngineType

P = 128
PACE = {
    "delta": (1.1, 2.0, 3.12, 2.0, 0.9, 4.5, 3.45, 0.15, 5.0, 1.38, 0.86, 1.04, 0.36, 0.51, 1.22),
    "last delta": (1.5, 2.5, 2.5, 2.3, 0.75, 3.75, 3.0, 0.3, 5.0, 1.73, 1.69, 0.54, 0.75, 0.45, 0.05),
    "stick": (12.0, 5.0, 3.54, 4.0, 0.91),
    "last stick": (5.94, 23.16, 0.63, 3.0, 0.9),
    "diff": (2.7, 2.1, 1.02, 7.5, 3, 1.2, 0.18, 4.8, 5.0),
    "last diff": (3, 1.7, 4.5, 9.7, 3, 0.19, 0.5, 2.12, 1.05),
    "fox": (3.9, 2.5, 0.9, 3.75, 0.53, 1.2, 1.5, 2.4),
    "last fox": (3, 2, 2.04, 2.5, 0.42, 2.4, 1.5, 2.8),
}
EPS = 1e-6
NEG = -1e30


class Counts:

    def __init__(self, nc, per):
        self.nc, self.per, self.found = nc, per, {}
        self.all, self.loop = [], None

    @contextmanager
    def fori(self, name, start, end, engines):
        with self.nc.Fori(start, end, engines=engines) as i:
            self.loop = (name, i, start)
            yield i
        for c in self.all:
            self.found[(name, c.name)] = c.local
            c.base, c.local = c.base + (end - start) * c.local, 0
        self.loop = None


class Count:
    def __init__(self, counts, name):
        self.counts, self.name, self.base, self.local = counts, name, 0, 0
        counts.all.append(self)

    def add(self, k=1):
        if self.counts.loop:
            self.local += k
        else:
            self.base += k

    def value(self):
        if not self.counts.loop:
            return self.base
        name, i, start = self.counts.loop
        per = self.counts.per.get((name, self.name), 0)
        least = self.base + self.local - start * per
        return i * per + least if per else least

    def zero(self):
        return self.base == 0 and self.local == 0


class Signal:

    def __init__(self, counts, name, step=1):
        self.sem, self.count, self.step = counts.nc.alloc_semaphore(name), Count(counts, name), step

    def prime(self, engine):
        assert self.step == 1
        engine.e.sem_inc(self.sem, 1)
        self.count.add(1)

    def by(self, instruction):
        instruction.then_inc(self.sem, self.step)
        self.count.add(self.step)
        return self.now()

    def before(self, k):
        sem, value, order, loop = self.now()
        return sem, value - k, order - k, loop

    def now(self):
        return None if self.count.zero() else (self.sem, self.count.value(), self.count.base + self.count.local, self.count.counts.loop)


class Engine:

    def __init__(self, counts, engine, name):
        self.e, self.done, self.counts = engine, Signal(counts, name), counts
        self.waited = {}

    def did(self, instruction):
        return self.done.by(instruction)

    def now(self):
        return self.done.now()

    def wait(self, *signals):
        for s in signals:
            if s is None:
                continue
            sem, value, order, loop = s
            key = (id(sem), loop[0] if loop else None)
            if self.waited.get(key, -1) >= order and (loop is None) == (self.counts.loop is None):
                continue
            self.waited[key] = order
            self.e.wait_ge(sem, value)

    def hold(self, carrier):
        self.e.sem_inc(carrier, 1)

    def forget(self):
        self.waited = {}


class TensorE:

    def __init__(self, engine):
        self.engine, self.time = engine, 0.0

    def matmul(self, out, lhsT, rhs, **flags):
        passes = 4 if rhs.dtype == F32 else 1
        self.time += passes * max(64, int(np.prod(rhs.shape[1:]))) / 2400
        return self.engine.matmul(out, lhsT, rhs, **flags)

    def transpose(self, out, in_, identity):
        self.time += P / 2400
        return self.engine.transpose(out, in_, identity)


def interleave(pe, filler, chains):
    queue = [[pe.time, n, c] for n, c in enumerate(chains)]
    while queue or filler is not None:
        first = min(queue, default=None)
        if first is not None and (first[0] <= pe.time or filler is None):
            pe.time = max(pe.time, first[0])
            after = next(first[2], None)
            if after is None:
                queue.remove(first)
            else:
                first[0] = pe.time + after
        elif next(filler, filler) is filler:
            filler = None


MATS = ["ident", "upper", "after", "negtri", "ones", "negones", "causal", "before", "notbefore"]
LEVELS = 7


def bucket(dist, n_buckets=32, max_distance=128):
    exact = n_buckets // 2
    d = np.maximum(dist, 1).astype(np.float32)
    large = exact + np.log(d / np.float32(exact)) / np.float32(np.log(max_distance / exact)) * (n_buckets - exact)
    large = np.minimum(large.astype(np.int32), n_buckets - 1)
    return np.where(dist < exact, dist, large)


def shape_constants():
    p, f = np.arange(P)[:, None], np.arange(P)[None, :]
    mats = {
        "ident": p == f, "upper": p <= f, "after": p > f, "negtri": -1.0 * (p >= f),
        "ones": np.ones((P, P)), "negones": -np.ones((P, P)), "causal": np.where(f > p, NEG, 0.0),
        "before": p < f, "notbefore": np.where(p >= f, NEG, 0.0),
    }
    out = [np.asarray(mats[m], np.float32) for m in MATS]

    def level(l, row, col):
        same = (row >> (l + 1)) == (col >> (l + 1))
        return (same & ((row >> l) % 2 == 1) & ((col >> l) % 2 == 0)).astype(np.float32)

    out.append(level(0, p, f))
    out += [level(l, f, p) for l in range(LEVELS)]
    return np.concatenate(out, axis=1)


def bias_constants():
    m = np.arange(384)
    hot = (bucket(np.maximum(255 - m, 0))[None, :] == np.arange(32)[:, None]).astype(np.float32)
    pick = np.zeros((32, 8, P), np.float32)
    for h in range(8):
        pick[h, h, :] = -1.0
    return np.concatenate([hot, pick.reshape(32, 8 * P)], axis=1)


def program(nc, t, out, per):
    T, D = t["x"].shape[1:]
    NT, KT = T // P, D // P
    dma_counts = Counts(nc, per)
    counts = Counts(nc, per)
    PE = Engine(counts, nc.tensor, "pe_done")
    A = Engine(counts, nc.scalar, "act_done")
    V = Engine(counts, nc.vector, "dve_done")
    G = Engine(counts, nc.gpsimd, "pool_done")
    engines = [PE, A, V, G]
    pe, act, dve, pool = TensorE(nc.tensor), nc.scalar, nc.vector, nc.gpsimd
    compute = [ET.Pool, ET.Activation, ET.PE, ET.DVE]

    @contextmanager
    def loop(name, start, end):
        for e in engines:
            e.forget()
        with counts.fori(name, start, end, compute) as i:
            yield i
        for e in engines:
            e.forget()

    base = 16512
    cursor = [base]

    def at(name, address, shape, dt=F32):
        return nc.alloc_sbuf_tensor_at(name, shape, dt, offset=address, align_bytes=4).ap()

    def region(nbytes):
        a = cursor[0]
        cursor[0] += nbytes
        return a

    KB = 1024
    hT = at("hT", region(32 * KB), [P, 2, KT, T], F32R)
    ring = at("ring", region(32 * KB), [P, 4, 2, 1024], F32R)
    raw_ring = at("raw_ring", region(16 * KB), [P, 4, 1024])
    r_res = region(16 * KB)
    x1 = at("x1", r_res, [P, NT, D])
    consts = at("consts", region(17 * 512), [P, 17, P])
    small = region(4 * 560 + 768)
    r4 = cursor[0]
    mat = {m: consts[:, n, :] for n, m in enumerate(MATS)}
    ident = mat["ident"]
    level0, levelT = consts[:, len(MATS), :], [consts[:, len(MATS) + 1 + l, :] for l in range(LEVELS)]
    so = [small]

    def little(name, cols):
        a = at(name, so[0], [P, cols])
        so[0] += 4 * cols
        return a

    colp = little("colp", 80)
    eps_c, one_c = little("eps_c", 1), little("one_c", 1)
    lam_c = little("lam_c", 1)
    gates = little("gates", 80).rearrange("p (h k c) -> p h k c", h=4, k=5)
    hs = little("hs", 20).rearrange("p (k c) -> p k c", k=5)
    cw = little("cw", 12).rearrange("p (k i) -> p k i", k=3)
    dtb, alog = little("dtb", 4), little("alog", 4)
    bfb = little("bfb", 8)
    stat = little("stat", 64)
    fl = little("fl", 32).rearrange("p (t h) -> p t h", t=4)
    wab = little("wab", 64)
    assert so[0] <= small + 4 * 560
    conv_col = colp[:, 0:48].rearrange("p (i k h) -> p k i h", i=4, k=3)
    prew_col, aprew_col, mprew_col, gnw_col = colp[:, 48:56], colp[:, 56:64], colp[:, 64:72], colp[:, 72:73]

    banks = [nc.alloc_psum_tensor(f"bank{b}", [P, 512], F32).ap() for b in range(8)]

    ident_b = at("ident_b", small + 4 * 560, [P, P], BF16)
    causal_b = at("causal_b", small + 4 * 560 + 256, [P, P], BF16)
    notbefore_b = at("notbefore_b", small + 4 * 560 + 512, [P, P], BF16)

    def v4(x):
        return x.rearrange("p (c f) -> p c f", c=4)

    def over4(m):
        return m.unsqueeze(1).broadcast_to([P, 4, P])

    def along(c4):
        return c4.unsqueeze(2).broadcast_to([P, 4, P])

    w1, w2 = t["w_in"], t["w_in_2"]
    filled = [Signal(counts, f"slab{s}_filled", 16) for s in range(4)]
    hi_done = [Signal(counts, f"slab{s}_hi") for s in range(4)]
    lo_done = [Signal(counts, f"slab{s}_lo") for s in range(4)]
    used = [Signal(counts, f"slab{s}_used") for s in range(4)]
    fills = [Count(dma_counts, f"fills{s}") for s in range(4)]

    sp_waited = nc.alloc_semaphore("sp_waited")

    def fill(s, parts):
        if not fills[s].zero():
            nc.sync.wait_ge(lo_done[s].sem, fills[s].value())
            nc.sync.sem_inc(sp_waited, 1)
        fills[s].add()
        for dst, src in parts:
            nc.sync.dma_start(dst, src).then_inc(filled[s].sem, 16)

    def cols(w, c0, k0=0):
        return w[0].rearrange("(k p) n -> p k n", p=P)[:, k0:k0 + 4, bass.ds(c0, P)]

    def tall(s, w, c0):
        fill(s, [(k8(s)[:, 0:4, :], cols(w, c0)), (k8(s)[:, 4:8, :], cols(w, c0, 4))])

    def wide(s, w, k0, c0):
        rows = w[0].rearrange("(k p) n -> p k n", p=P)
        fill(s, [(k2(s)[:, j:j + 1, :], rows[:, bass.ds(k0 + j, 1), c0:c0 + 512]) for j in range(2)])

    def slot(s):
        return raw_ring[:, s, :]

    def k8(s):
        return slot(s).rearrange("p (k n) -> p k n", k=8)

    def k2(s):
        return slot(s).rearrange("p (k n) -> p k n", k=2)

    A_COLS = [2048, 2560, 3072, 0, 512, 1024, 1536, 3584]
    B_COLS = [0, 512, 1024, 1536, 2048, 2560]
    MERGE0 = 4104

    stage = at("stage", r4, [P, P])
    x_in = []
    for j in range(NT):
        x_in.append(Signal(counts, f"x{j}_in", 16).by(nc.sync.dma_start(x1[:, j, :], t["x"][0, j * P:(j + 1) * P, :])))
    rows_dma = Signal(counts, "rows_in", 16)
    rows_dma.by(nc.sync.dma_start(consts[:, 0, :], t["shape_consts"][:, 0:P]))
    row = 0
    for name, n in (("conv_w", 48), ("pre_norm_w", 8), ("ln_attn_pre_2", 8), ("ln_mlp_pre_2", 8), ("gdn_norm_w", 1)):
        src = t[name]
        flat = src.rearrange("a i (n c) -> (a i n) c", c=P) if len(src.shape) == 3 else src.rearrange("a (n c) -> (a n) c", c=P)
        rows_in = rows_dma.by(nc.sync.dma_start(stage[row:row + n, :], flat))
        row += n
    wab_dma, mats_dma, small_dma = (Signal(counts, n, 16) for n in ("wab_in", "mats_in", "small_in"))
    hot = at("bucket_hot", r4 + 54 * KB, [32, 384])
    rel = at("rel", r4 + 56 * KB, [32, 4])
    lam_v = [at(f"lam{n}", r4 + 1024 + 256 * n, [P, 64]) for n in range(4)]

    def small_inputs():
        wab_dma.by(nc.sync.dma_start(wab.rearrange("p (k n) -> p k n", k=8),
                                     w1[0].rearrange("(k p) n -> p k n", p=P)[:, :, 4096:4104]))
        mats_dma.by(nc.sync.dma_start(consts[:, 1:17, :].rearrange("p a b -> p (a b)"), t["shape_consts"][:, P:]))
        small = [(dtb, t["dt_bias"][0].partition_broadcast(P)), (alog, t["a_log"][0].partition_broadcast(P)),
                 (bfb, t["b_f_2"][0].partition_broadcast(P)), (hot, t["bias_consts"][:, 0:384]), (rel, t["rel_bias_2"])]
        small += [(v, t[n][0].partition_broadcast(P)) for v, n in zip(lam_v, ("lam_q1_2", "lam_k1_2", "lam_q2_2", "lam_k2_2"))]
        for dst, src in small:
            small_dma.by(nc.sync.dma_start(dst, src))

    def sp_stream():
        n = [0]

        def nxt():
            n[0] += 1
            return (n[0] - 1) % 4

        for n_, c in enumerate(A_COLS):
            s = nxt()
            tall(s, w1, c)
            if n_ == 1:
                small_inputs()
        with dma_counts.fori("slabs_a", 1, 4, [ET.SP]) as i:
            for c in A_COLS:
                s = nxt()
                tall(s, w1, i * P + c)
        with dma_counts.fori("slabs_merge", 0, 4, [ET.SP]) as i:
            for c in range(4):
                s = nxt()
                tall(s, w1, i * 512 + (MERGE0 + c * P))
        with dma_counts.fori("slabs_branch", 0, 2, [ET.SP]) as i:
            for c in range(4):
                s = nxt()
                fill(s, [(k8(s)[:, 0:4, :], cols(t["w_branch_sb"], i * 512 + c * P)),
                         (k8(s)[:, 4:8, :], cols(t["w_branch_gdn"], i * 512 + c * P))])
        for half in range(2):
            for kk in range(4):
                s = nxt()
                wide(s, t["w_out"], 2 * kk, half * 512)
        for n_, c in enumerate(B_COLS):
            tall(n_ % 4, w2, c)
        with dma_counts.fori("slabs_b", 1, 4, [ET.SP]) as i:
            for n_, c in enumerate(B_COLS):
                tall(n_ % 4, w2, i * P + c)
        for half, order in enumerate(((0, 4, 2, 6), (0, 2, 4, 6))):
            for k0 in order:
                s = nxt()
                wide(s, t["w_out_2"], k0, half * 512)
        with dma_counts.fori("slabs_up", 0, 8, [ET.SP]) as i:
            for c in range(4):
                s = nxt()
                tall(s, t["w_up_2"], i * 512 + c * P)
        for half in range(2):
            with dma_counts.fori(f"slabs_down{half}", 0, 4, [ET.SP]) as i:
                for c in range(4):
                    s = nxt()
                    wide(s, t["w_down_2"], i * 8 + 2 * c, half * 512)

    sp_stream()
    wab_in, mats_in, small_in = wab_dma.now(), mats_dma.now(), small_dma.now()

    def split(s):
        filled[s].count.add(32)
        A.wait((filled[s].sem, filled[s].count.value(), filled[s].count.base + filled[s].count.local, counts.loop))
        A.wait(used[s].now())
        h = hi_done[s].by(act.copy(ring[:, s, 0, :], slot(s)))
        G.wait(h)
        lo_done[s].by(pool.tensor_tensor(ring[:, s, 1, :], slot(s), ring[:, s, 0, :].bitcast(F32), ALU.subtract))

    acc_free = [Signal(counts, f"acc{b}_free") for b in range(2)]

    def product(s, terms, first_wait=(), opened=False, k_ready=None):
        PE.wait(lo_done[s].now(), *first_wait)
        for j, (o, l, r, a, b) in enumerate(terms):
            if k_ready and j % 3 == 0:
                PE.wait(k_ready[j // 3])
            m = pe.matmul(o, l, r, start=a, stop=b, skip_group_check=opened)
            if j == len(terms) - 1:
                used[s].by(m)
            yield 0

    def terms_T(s, acc, ks, src=hT):
        w = ring[:, s].rearrange("p two (k n) -> p two k n", k=8)
        out_ = []
        for n, (kw, kx) in enumerate(ks):
            for m, (a, b) in enumerate(((0, 0), (0, 1), (1, 0))):
                out_.append((acc, w[:, a, kw, :], src[:, b, kx, :], n == 0 and m == 0, n == len(ks) - 1 and m == 2))
        return out_

    all_k = [(k, k) for k in range(KT)]

    act.preload_act_table_set("natural_log_exp_and_others")
    V.did(dve.memset(eps_c, EPS))
    V.did(dve.memset(one_c, 1.0))
    half_c = little("half_c", 4)
    neghalf = V.did(dve.memset(half_c, -0.5))
    G.wait(neghalf)
    A.wait(neghalf)
    lam_init = 0.8 - 0.6 * float(np.exp(-0.3 * 0))
    PE.wait(rows_in)
    tok = PE.did(pe.transpose(banks[2][:, 0:row], stage[0:row, :], ident[0:row, 0:row]))
    A.wait(tok)
    cols_ready = A.did(act.copy(colp[:, 0:row], banks[2][:, 0:row]))

    def small_constants():
        yield 20
        V.wait(mats_in, small_in)
        V.did(dve.tensor_copy(ident_b, ident))
        V.did(dve.tensor_copy(causal_b, mat["causal"]))
        V.did(dve.tensor_copy(notbefore_b, mat["notbefore"]))
        lq1, lk1, lq2, lk2 = lam_v
        V.did(dve.tensor_tensor(lq1, lq1, lk1, ALU.mult))
        tok = V.did(dve.tensor_tensor(lq2, lq2, lk2, ALU.mult))
        V.wait(tok)
        V.did(dve.tensor_reduce(stat[:, 60:61], lq1, AXX, ALU.add))
        tok = V.did(dve.tensor_reduce(stat[:, 61:62], lq2, AXX, ALU.add))
        A.wait(tok)
        tok = A.did(act.activation(stat[:, 62:64], stat[:, 60:62], ACT.Exp))
        V.wait(tok)
        tok = V.did(dve.tensor_tensor(lam_c, stat[:, 62:63], stat[:, 63:64], ALU.subtract))
        V.wait(tok)
        V.did(dve.tensor_scalar(lam_c, lam_c, lam_init, None, ALU.add))

    far = little("far", 4)
    skew = nc.dram_tensor("skew", (4, P * 384 + 128), F32, kind="Internal").ap()
    skew_dma = Signal(counts, "skew_written", 16)

    def distance_bias():
        relb = at("relb", r4 + 57 * KB, [32, 4, P])
        fw = at("fw", r4 + 60 * KB, [P, 4, 384])
        yield 24
        V.wait(small_in)
        rb = V.did(dve.tensor_copy(relb, rel.unsqueeze(2).broadcast_to([32, 4, P])))
        yield 2
        PE.wait(rb, *bank_free)
        for h in range(4):
            m = pe.matmul(banks[2 + h][:, 0:384], relb[:, h, :], hot, start=True, stop=True)
        p_ = PE.did(m)
        A.wait(p_)
        for h in range(4):
            fr = A.did(act.copy(fw[:, h, :], banks[2 + h][:, 0:384]))
        A.wait(fr)
        V.wait(fr)
        V.did(dve.tensor_copy(far, fw[:, :, 0]))
        for h in range(4):
            skew_dma.by(act.dma_start(skew[h, 0:P * 384].rearrange("(p m) -> p m", p=P), fw[:, h, :]))

    FIRST_NORM_US, NORM_TAIL_US = 5.2, 6.0
    pool_held = nc.alloc_semaphore("pool_held")

    def rstd(dst, total, n, ready):
        G.wait(ready)
        if counts.loop:
            G.hold(pool_held)
        a = G.did(pool.tensor_scalar(dst, total, 1.0 / n, EPS, ALU.mult, ALU.add))
        G.wait(a)
        w = dst.shape[1]
        return G.did(pool.tensor_tensor(dst, dst, half_c[:, 0:1].broadcast_to([P, w]) if w > 1 else half_c[:, 0:1], ALU.pow))

    def keep_warm(bank, us):
        for _ in range(int(us * 2400 / (4 * T))):
            m = pe.matmul(bank, ident, over4(ident), start=True, stop=True)
        return m

    def norm_tile(j, src, scratch, stats, ready):
        A.wait(ready)
        a = A.did(act.activation(scratch[:, j, :], src[:, j, :], ACT.Square, accum_out=stats[:, j:j + 1]))
        r = rstd(stats[:, j:j + 1], stats[:, j:j + 1], D, a)
        V.wait(r)
        return V.did(dve.tensor_scalar(scratch[:, j, :], src[:, j, :], stats[:, j:j + 1], None, ALU.mult))

    def transpose_normed(scratch, weight_col, scaled):
        norm_banks = (2, 3, 4, 5, 6, 7, 1)
        free = {b: None for b in norm_banks}
        ready = []
        split(0)
        for k in range(KT):
            b = norm_banks[k % len(norm_banks)]
            PE.wait(free[b], *scaled)
            for j in range(NT):
                m = pe.transpose(banks[b][:, j * P:(j + 1) * P], scratch[:, j, k * P:(k + 1) * P], ident)
            tp = PE.did(m)
            A.wait(tp)
            h = A.did(act.activation(hT[:, 0, k, :], banks[b], ACT.Copy, scale=weight_col[:, k:k + 1]))
            V.wait(h)
            free[b] = V.did(dve.scalar_tensor_tensor(hT[:, 1, k, :], banks[b], weight_col[:, k:k + 1],
                                                     hT[:, 0, k, :].bitcast(F32), ALU.mult, ALU.subtract))
            ready.append(free[b])
            if k == 1:
                split(1)
        return ready

    PE.did(keep_warm(banks[3], FIRST_NORM_US))
    scr = at("norm_scratch", r4 + 2 * KB, [P, NT, D])
    scaled = [norm_tile(j, x1, scr, stat[:, 0:4], x_in[j]) for j in range(NT)]
    PE.wait(cols_ready)
    A.wait(cols_ready)
    h_ready = bank_free = transpose_normed(scr, prew_col, scaled)

    def narrow(w, sums, accT, acc, free):
        PE.wait(*free)
        for k in range(KT):
            for m, (a, b) in enumerate(((0, 0), (0, 1), (1, 0))):
                q = pe.matmul(accT[0:8, :], w[:, a, k, :], hT[:, b, k, :], start=k == 0 and m == 0, stop=k == KT - 1 and m == 2)
        tok = PE.did(q)
        V.wait(tok)
        tok = V.did(dve.tensor_copy(sums, accT[0:8, :]))
        yield 1.5
        PE.wait(tok)
        for j in range(NT):
            q = pe.transpose(acc[:, j * 8:(j + 1) * 8], sums[:, j * P:(j + 1) * P], ident[0:8, 0:8])
        return PE.did(q)

    def step_gates():
        yield 16
        ab = at("ab", r4 + 20 * KB, [P, 4, 8])
        wab_s = at("wab_s", r4 + 20 * KB + 256, [P, 2, 64], F32R)
        A.wait(wab_in)
        tok = A.did(act.copy(wab_s[:, 0, :], wab))
        V.wait(tok)
        tok = V.did(dve.tensor_tensor(wab_s[:, 1, :], wab, wab_s[:, 0, :].bitcast(F32), ALU.subtract))
        yield 2
        wabk = wab_s.rearrange("p two (k n) -> p two k n", k=8)

        tok = yield from narrow(wabk, at("ab_sums", r4 + 22 * KB, [8, T]), banks[5], banks[6], (tok, *bank_free))
        V.wait(tok)
        tok = V.did(dve.tensor_copy(ab, banks[6][:, 0:32].rearrange("p (c n) -> p c n", c=4)))
        V.wait(tok, small_in, mats_in)
        sp_z = at("sp_z", r4 + 21 * KB, [P, 4, 4])
        sp_e = at("sp_e", r4 + 21 * KB + 64, [P, 4, 4])
        be = at("be", r4 + 21 * KB + 128, [P, 4, 4])
        ea = at("ea", r4 + 21 * KB + 192, [P, 4])
        tok = V.did(dve.tensor_tensor(sp_z, ab[:, :, 0:4], dtb.unsqueeze(1).broadcast_to([P, 4, 4]), ALU.add))
        V.wait(tok)
        A.wait(tok)
        tok = A.did(act.activation(sp_e, sp_z, ACT.Abs))
        A.wait(tok)
        tok = A.did(act.activation(sp_e, sp_e, ACT.Exp, scale=-1.0))
        A.wait(tok)
        A.did(act.activation(sp_e, sp_e, ACT.Ln, bias=one_c))
        A.did(act.activation(ea, alog, ACT.Exp))
        tok = A.did(act.activation(be, ab[:, :, 4:8], ACT.Exp, scale=-1.0))
        V.wait(tok)
        tok = V.did(dve.scalar_tensor_tensor(sp_z, sp_z, 0.0, sp_e, ALU.max, ALU.add))
        V.did(dve.tensor_scalar(be, be, 1.0, None, ALU.add))
        tok = V.now()
        V.wait(tok)
        V.did(dve.scalar_tensor_tensor(gates[:, :, 0, :].rearrange("p h c -> p c h"), sp_z, -1.0,
                                       ea.unsqueeze(1).broadcast_to([P, 4, 4]), ALU.mult, ALU.mult))
        tok = V.did(dve.reciprocal(gates[:, :, 1, :].rearrange("p h c -> p c h"), be))
        g_all = gates[:, :, 0, :]
        yield 3
        PE.wait(tok)
        gb = banks[7].rearrange("p (a n) -> p a n", a=8)
        for n, m in enumerate(("upper", "after", "ones")):
            q = pe.matmul(gb[:, n, 0:16].rearrange("p (h c) -> p h c", h=4), mat[m], g_all, start=True, stop=True)
        tok = PE.did(q)
        A.wait(tok)
        for n in range(3):
            tok = A.did(act.activation(gates[:, :, 2 + n, :], gb[:, n, 0:16].rearrange("p (h c) -> p h c", h=4), ACT.Exp))
        V.wait(tok)
        V.did(dve.tensor_tensor(gates[:, :, 2, :], gates[:, :, 2, :], gates[:, :, 1, :], ALU.mult))

    off = [r4]

    def take(name, shape, dt=F32):
        n = int(np.prod(shape[1:])) * 4
        a = at(name, off[0], shape, dt)
        off[0] += n
        return a

    osb = take("osb", [P, 2, 4, T], F32R)
    ogd = take("ogd", [P, 2, 4, T], F32R)
    rawA = off[0]
    cin = take("cin", [P, 3, T + 4])
    rawg = take("rawg", [P, T])
    rawsb = take("rawsb", [P, 4, T])
    gbuf = [take(f"g{n}", [P, T]) for n in range(16)]
    sbuf_ = [take(f"s{n}", [P, T]) for n in range(10)]
    assert off[0] <= nc.sbuf_usable_end, off[0] - r4

    zeros = V.did(dve.memset(cin[:, :, 0:4], 0.0))

    raw_tiles = [cin[:, 0, 3:3 + T], cin[:, 1, 3:3 + T], cin[:, 2, 3:3 + T]] + [rawsb[:, n, :] for n in range(4)] + [rawg]

    def project(reads, k_ready=None):
        for n, dst in enumerate(raw_tiles):
            s, b = n % 4, n % 2
            yield from product(s, terms_T(s, banks[b], all_k), first_wait=(acc_free[b].now(),),
                               k_ready=None if n else k_ready)
            split((s + 2) % 4)
            assert reads is None or n in reads, n
            A.wait(used[s].now(), reads[n] if reads else None)
            acc_free[b].by(act.copy(dst, banks[b]))

    def fence():
        return [e.now() for e in engines] + [a.now() for a in acc_free]

    def sigmoid_ln(dst, x, ready):
        A.wait(ready)
        a = A.did(act.activation(dst, x, ACT.Abs))
        A.wait(a)
        a = A.did(act.activation(dst, dst, ACT.Exp, scale=-1.0))
        A.wait(a)
        return A.did(act.activation(dst, dst, ACT.Ln, bias=one_c))

    def sigmoid_exp(dst, x, ready):
        V.wait(ready)
        b = V.did(dve.scalar_tensor_tensor(dst, x, 0.0, dst, ALU.min, ALU.subtract))
        A.wait(b)
        return A.did(act.activation(dst, dst, ACT.Exp))

    def times(dst, x, y, ready):
        V.wait(ready)
        return V.did(dve.tensor_tensor(dst, x, y, ALU.mult))

    heads_end = [None, None]

    def delta_head(i, reads, marks, pace):
        qT, kT, bv, bk, kd, qg, intra, MT, Ca, Cb, X, XT, PP, misc, tmp, gate = gbuf
        S = misc[:, 0:P]
        for e in engines:
            e.wait(*marks)
        V.did(dve.tensor_copy(hs, gates[:, i]))
        tok = V.did(dve.tensor_copy(cw, conv_col[:, :, :, i]))
        G.wait(tok)
        ug = G.did(pool.tensor_tensor(v4(Ca), over4(mat["upper"]), along(hs[:, 0, :]), ALU.mult))
        slg = G.did(pool.tensor_tensor(v4(Cb), over4(mat["after"]), along(hs[:, 0, :]), ALU.mult))
        V.wait(tok)

        def conv(n, dst):
            tok = V.did(dve.tensor_scalar(dst, cin[:, n, 0:T], cw[:, n, 0:1], None, ALU.mult))
            for j in range(1, 4):
                V.wait(tok)
                tok = V.did(dve.scalar_tensor_tensor(dst, cin[:, n, j:j + T], cw[:, n, j:j + 1], dst, ALU.mult, ALU.add))
            reads[n] = tok
            return tok

        cq = conv(0, qT)
        yield pace[0]
        lq = sigmoid_ln(tmp, qT, cq)
        ck = conv(1, kT)
        PE.wait(ug)
        pe.matmul(banks[5], mat["after"], Ca, start=True, stop=True)
        p3 = PE.did(pe.matmul(banks[7], mat["ones"], Ca, start=True, stop=True))
        yield pace[1]
        lk = sigmoid_ln(XT, kT, ck)
        sq_ = sigmoid_exp(tmp, qT, lq)
        cv = conv(2, PP)
        PE.wait(slg)
        p2 = PE.did(pe.matmul(banks[6], mat["upper"], Cb, start=True, stop=True))
        yield pace[2]
        sk_ = sigmoid_exp(XT, kT, lk)
        cq = times(qT, qT, tmp, sq_)
        A.wait(cq)
        aq = A.did(act.activation(tmp, qT, ACT.Square))
        A.wait(p2)
        eDT = A.did(act.activation(Ca, banks[5], ACT.Exp))
        yield pace[3]
        lv = sigmoid_ln(X, PP, cv)
        ck = times(kT, kT, XT, sk_)
        A.wait(ck)
        ak = A.did(act.activation(XT, kT, ACT.Square))
        PE.wait(aq, eDT)
        pq = PE.did(pe.matmul(banks[5], mat["ones"], tmp, start=True, stop=True))
        yield pace[4]
        eD = A.did(act.activation(Cb, banks[6], ACT.Exp))
        er = A.did(act.activation(misc, banks[7], ACT.Exp))
        G.wait(eDT)
        mDT = G.did(pool.tensor_tensor(v4(Ca), v4(Ca), over4(mat["upper"]), ALU.mult))
        G.wait(eD)
        a = G.did(pool.tensor_tensor(v4(Cb), v4(Cb), over4(mat["after"]), ALU.mult))
        G.wait(a)
        mD = G.did(pool.tensor_tensor(v4(Cb), v4(Cb), along(hs[:, 1, :]), ALU.mult))
        sv_ = sigmoid_exp(X, PP, lv)
        cv = times(PP, PP, X, sv_)
        yield pace[5]
        PE.wait(ak, eD)
        pk = PE.did(pe.matmul(banks[6], mat["ones"], XT, start=True, stop=True))
        PE.wait(cv, er)
        for c in range(4):
            m = pe.transpose(banks[7][:, c * P:(c + 1) * P], PP[:, c * P:(c + 1) * P], ident)
        pv = PE.did(m)
        A.wait(pq)
        a = A.did(act.activation(tmp, banks[5], ACT.Ln, bias=eps_c))
        A.wait(pk)
        b = A.did(act.activation(XT, banks[6], ACT.Ln, bias=eps_c))
        A.wait(a)
        a = A.did(act.activation(tmp, tmp, ACT.Exp, scale=-0.5))
        A.wait(b)
        b = A.did(act.activation(XT, XT, ACT.Exp, scale=-0.5))
        V.wait(a)
        nq = V.did(dve.scalar_tensor_tensor(qT, qT, P ** -0.5, tmp, ALU.mult, ALU.mult))
        V.wait(b)
        nk = times(kT, kT, XT, b)
        V.wait(pv)
        vready = V.did(dve.tensor_tensor(v4(bv), v4(banks[7]), along(hs[:, 1, :]), ALU.mult))
        yield pace[6]
        lg = sigmoid_ln(gate, rawg, None)
        yield pace[7]
        PE.wait(nq, nk)
        for c in range(4):
            k_ = kT[:, c * P:(c + 1) * P]
            m = pe.matmul(banks[5][:, c * P:(c + 1) * P], k_, k_, start=True, stop=True)
        kk = PE.did(m)
        V.wait(kk, mD)
        mready = V.did(dve.tensor_tensor(X, banks[5], Cb, ALU.mult))
        for c in range(4):
            m = pe.matmul(banks[6][:, c * P:(c + 1) * P], kT[:, c * P:(c + 1) * P], qT[:, c * P:(c + 1) * P], start=True, stop=True)
        qk = PE.did(m)
        PE.wait(vready)
        for c in range(4):
            m = pe.transpose(banks[7][:, c * P:(c + 1) * P], kT[:, c * P:(c + 1) * P], ident)
        pk = PE.did(m)
        V.wait(qk, mDT)
        iready = V.did(dve.tensor_tensor(intra, banks[6], Ca, ALU.mult))
        PE.wait(mready)
        for c in range(4):
            m = pe.transpose(banks[5][:, c * P:(c + 1) * P], X[:, c * P:(c + 1) * P], ident)
        p_ = PE.did(m)
        A.wait(p_)
        mt = A.did(act.copy(MT, banks[5]))
        V.wait(p_)
        a = V.did(dve.tensor_tensor(v4(X), v4(X), over4(level0), ALU.mult))
        V.wait(a, mt)
        V.did(dve.tensor_tensor(v4(X), over4(ident), v4(X), ALU.subtract))
        a = V.did(dve.tensor_tensor(v4(XT), v4(MT), over4(levelT[0]), ALU.mult))
        V.wait(a)
        xr = V.did(dve.tensor_tensor(v4(XT), over4(ident), v4(XT), ALU.subtract))
        G.wait(mt, iready, mready)
        cm = {}
        Cs = (Ca, Cb)
        for l in (1, 2):
            cm[l] = G.did(pool.tensor_tensor(v4(Cs[l % 2]), v4(MT), over4(levelT[l]), ALU.mult))
        yield pace[8]
        kr = None
        CX = (PP, tmp)

        def halves_of(x, l):
            return x.rearrange("p (cb two w) -> p cb two w", two=2, w=1 << l)

        V.wait(nq)
        zeroed = {1: V.did(dve.memset(halves_of(CX[1], 1)[:, :, 1, :], 0.0))}
        for l in range(1, LEVELS):
            C, w_ = Cs[l % 2], 1 << l
            PP = CX[l % 2]
            halves = lambda x: halves_of(x, l)
            chunk_half = lambda x, c, h_: halves(x[:, c * P:(c + 1) * P])[:, :, h_, :]
            compact = lambda x: x[:, 0:T // 2].rearrange("p (cb w) -> p cb w", w=w_)
            PE.wait(cm[l], xr)
            for c in range(4):
                f = slice(c * P, (c + 1) * P)
                o = banks[5][:, c * 64:(c + 1) * 64].rearrange("p (b w) -> p b w", w=w_)
                m = pe.matmul(o, C[:, f], chunk_half(X, c, 0), start=True, stop=True)
            p1 = PE.did(m)
            A.wait(p1)
            pr = A.did(act.copy(halves(PP)[:, :, 0, :], compact(banks[5])))
            if l + 1 < LEVELS:
                zeroed[l + 1] = V.did(dve.memset(halves_of(CX[(l + 1) % 2], l + 1)[:, :, 1, :], 0.0))
            if l == 1:
                V.wait(pk)
                V.did(dve.tensor_tensor(v4(bk), v4(banks[7]), along(hs[:, 2, :]), ALU.mult))
                kr = V.did(dve.tensor_tensor(v4(kd), v4(banks[7]), along(hs[:, 3, :]), ALU.mult))
            elif l == 2:
                V.wait(er)
                qgr = V.did(dve.tensor_tensor(qg, qT, misc, ALU.mult))
            elif l == 3:
                sg_ = sigmoid_exp(gate, rawg, lg)
            elif l == 4:
                reads[7] = times(gate, rawg, gate, sg_)
            if l + 2 < LEVELS:
                G.wait(p1)
                cm[l + 2] = G.did(pool.tensor_tensor(v4(C), v4(MT), over4(levelT[l + 2]), ALU.mult))
            yield pace[9]
            PE.wait(pr, kr, zeroed[l])
            for c in range(4):
                f = slice(c * P, (c + 1) * P)
                o = banks[6][:, c * 64:(c + 1) * 64].rearrange("p (b w) -> p b w", w=w_)
                m = pe.matmul(o, PP[:, f], chunk_half(XT, c, 1), start=True, stop=True)
            p2 = PE.did(m)
            if l < LEVELS - 1:
                for c in range(4):
                    f = slice(c * P, (c + 1) * P)
                    o = banks[7][:, c * 64:(c + 1) * 64].rearrange("p (b w) -> p b w", w=w_)
                    m = pe.matmul(o, XT[:, f], chunk_half(PP, c, 0), start=True, stop=True)
                p3 = PE.did(m)
                V.wait(p3)
                V.did(dve.tensor_tensor(halves(XT)[:, :, 1, :], halves(XT)[:, :, 1, :], compact(banks[6]), ALU.subtract))
                xr = V.did(dve.tensor_tensor(halves(X)[:, :, 0, :], halves(X)[:, :, 0, :], compact(banks[7]), ALU.subtract))
            else:
                V.wait(p2)
                xr = V.did(dve.tensor_tensor(halves(XT)[:, :, 1, :], halves(XT)[:, :, 1, :], compact(banks[6]), ALU.subtract))
            yield pace[10]
        PE.wait(xr)
        for c in range(4):
            f = slice(c * P, (c + 1) * P)
            m = pe.matmul(banks[5][:, f], XT[:, f], bv[:, f], start=True, stop=True)
        pu = PE.did(m)
        V.wait(pu)
        u, wT = Ca, Cb
        ur = V.did(dve.tensor_copy(u, banks[5]))
        for c in range(4):
            f = slice(c * P, (c + 1) * P)
            m = pe.matmul(banks[7][:, f], bk[:, f], XT[:, f], start=True, stop=True)
        pw = PE.did(m)
        A.wait(pw)
        wr = A.did(act.copy(wT, banks[7]))
        yield pace[11]
        V.wait(qgr)
        srd = None
        for c in range(4):
            f = slice(c * P, (c + 1) * P)
            if c:
                PE.wait(srd, wr)
                pa = PE.did(pe.matmul(banks[5][:, 0:P], wT[:, f], S, start=True, stop=True))
                V.wait(pa)
                ur = V.did(dve.tensor_tensor(u[:, f], u[:, f], banks[5][:, 0:P], ALU.subtract))
                pe.matmul(banks[7][:, f], S, qg[:, f], start=True, stop=False)
                yield pace[12]
            PE.wait(ur, iready, wr)
            po = PE.did(pe.matmul(banks[7][:, f], u[:, f], intra[:, f], start=c == 0, stop=True))
            if c < 3:
                ps = PE.did(pe.matmul(banks[6][:, 0:P], kd[:, f], u[:, f], start=True, stop=True))
                V.wait(ps)
                if c == 0:
                    srd = V.did(dve.tensor_copy(S, banks[6][:, 0:P]))
                else:
                    srd = V.did(dve.scalar_tensor_tensor(S, S, hs[:, 4, c:c + 1], banks[6][:, 0:P], ALU.mult, ALU.add))
                yield pace[13]
        yield pace[14]
        V.wait(po)
        oc = V.did(dve.tensor_copy(X, banks[7]))
        A.wait(oc)
        a = A.did(act.activation(tmp, X, ACT.Square))
        PE.wait(a)
        p_ = PE.did(pe.matmul(banks[5], mat["ones"], tmp, start=True, stop=True))
        A.wait(p_)
        b = A.did(act.activation(tmp, banks[5], ACT.Ln, bias=eps_c, scale=1.0 / P))
        A.wait(b)
        b = A.did(act.activation(tmp, tmp, ACT.Exp, scale=-0.5))
        V.wait(b, oc)
        d_ = V.did(dve.scalar_tensor_tensor(X, X, gnw_col, tmp, ALU.mult, ALU.mult))
        V.wait(d_)
        d_ = V.did(dve.tensor_tensor(X, X, gate, ALU.mult))
        A.wait(d_)
        a = A.did(act.copy(ogd[:, 0, i, :], X))
        V.wait(a)
        heads_end[1] = V.did(dve.tensor_tensor(ogd[:, 1, i, :], X, ogd[:, 0, i, :].bitcast(F32), ALU.subtract))

    def stick_pair(i, reads, marks, pace):
        qc, kc, vn, La, Lb, pa, pb, Csa, Csb, gate = sbuf_
        state = {}

        def start():
            for e in engines:
                e.wait(*marks)
            reads[3] = V.did(dve.tensor_scalar(qc, rawsb[:, 0, :], 64 ** -0.5, None, ALU.mult))
            reads[4] = state["qk"] = V.did(dve.tensor_copy(kc, rawsb[:, 1, :]))
            for c in range(4):
                m = pe.transpose(banks[4][:, c * P:(c + 1) * P], rawsb[:, 2, c * P:(c + 1) * P], ident)
            reads[5] = p_ = PE.did(m)
            A.wait(p_)
            state["v"] = A.did(act.copy(vn, banks[4]))

        def head(h):
            yield pace[0]
            if not h:
                start()
            yield pace[1]
            L, a_buf, Cs, bank = ((La, pa, Csa, banks[2]), (Lb, pb, Csb, banks[3]))[h]
            hp = slice(64 * h, 64 * h + 64)
            PE.wait(state["qk"], state["v"])
            z = PE.did(pe.matmul(bank[:, 0:P], kc[hp, 3 * P:T], qc[hp, 3 * P:T], start=True, stop=True))
            csum = av = None
            for j in (3, 2, 1, 0):
                q0, w = P * j, T - P * j
                A.wait(z, av)
                s_ = A.did(act.activation(a_buf[:, 0:w], bank[:, 0:w], ACT.Abs))
                A.wait(s_)
                s_ = A.did(act.activation(a_buf[:, 0:w], a_buf[:, 0:w], ACT.Exp, scale=-1.0))
                A.wait(s_)
                s_ = A.did(act.activation(a_buf[:, 0:w], a_buf[:, 0:w], ACT.Ln, bias=one_c))
                V.wait(s_, csum)
                l_ = V.did(dve.scalar_tensor_tensor(L[:, 0:w], bank[:, 0:w], 0.0, a_buf[:, 0:w], ALU.max, ALU.add))
                V.wait(l_)
                l_ = V.did(dve.tensor_tensor(L[:, 0:P], L[:, 0:P], mat["before"], ALU.mult))
                yield pace[2] + pace[3] * w / 1000
                PE.wait(l_, csum)
                pe.matmul(bank[:, 0:P], ident_b, notbefore_b, start=False, stop=True, skip_group_check=True)
                m = pe.matmul(bank[:, 0:w], mat["negtri"], L[:, 0:w], start=False, stop=True, skip_group_check=True)
                if j < 3:
                    m = pe.matmul(bank[:, P:w], mat["negones"], Cs[:, q0 + P:T], start=False, stop=True, skip_group_check=True)
                la = PE.did(m)
                A.wait(la)
                a_ = A.did(act.activation(a_buf[:, 0:w], bank[:, 0:w], ACT.Exp))
                if j:
                    G.wait(la)
                    if j < 3:
                        G.did(pool.tensor_tensor(Cs[:, q0 + P:T], Cs[:, q0 + P:T], L[:, P:w], ALU.add))
                    csum = G.did(pool.tensor_tensor(Cs[:, q0:q0 + P], L[:, 0:P], mat["ones"], ALU.mult))
                if h == 0 and j == 2:
                    b = sigmoid_ln(gate, rawsb[:, 3, :], None)
                    b = sigmoid_exp(gate, rawsb[:, 3, :], b)
                    state["gate"] = reads[6] = times(gate, rawsb[:, 3, :], gate, b)
                yield pace[4] + w / 1000
                PE.wait(a_)
                if j:
                    z = PE.did(pe.matmul(bank[:, 0:w + P], kc[hp, q0 - P:q0], qc[hp, q0 - P:T], start=True, stop=True))
                av = PE.did(pe.matmul(banks[4][hp, q0:T], vn[:, j * P + 64 * h:j * P + 64 * h + 64],
                                      a_buf[:, 0:w], start=j == 3, stop=True, skip_group_check=True))
            state[h] = av
            if (1 - h) in state:
                V.wait(state[0], state[1], state["gate"])
                b = V.did(dve.tensor_tensor(La, gate, banks[4], ALU.mult))
                A.wait(b)
                a = A.did(act.copy(osb[:, 0, i, :], La))
                V.wait(a)
                heads_end[0] = V.did(dve.tensor_tensor(osb[:, 1, i, :], La, osb[:, 0, i, :].bitcast(F32), ALU.subtract))

        return [head(0), head(1)]

    A.wait(zeros)
    interleave(pe, project(None, h_ready), [step_gates(), distance_bias(), small_constants()])
    skew_written = skew_dma.now()
    for e in engines:
        e.wait(skew_written)
    with loop("stage_a", 1, 4) as i:
        reads, marks = {}, fence()
        interleave(pe, project(reads), [delta_head(i - 1, reads, marks, PACE["delta"]), *stick_pair(i - 1, reads, marks, PACE["stick"])])

    sig_sb = at("sig_sb", r_res, [P, 8, T])
    sig_gd = at("sig_gd", rawA, [P, 8, T])
    reads, marks = {}, fence()

    def merge_gates():
        last_exp = None
        for n in range(16):
            s, b = n % 4, n % 2
            yield from product(s, terms_T(s, banks[b], all_k), first_wait=(acc_free[b].now(),))
            split((s + 2) % 4)
            if last_exp:
                A.wait(last_exp[1])
                A.did(act.activation(last_exp[0], last_exp[0], ACT.Exp))
            dst = sig_sb[:, n, :] if n < 8 else sig_gd[:, n - 8, :]
            A.wait(used[s].now())
            if n == 8:
                A.wait(*[reads[r] for r in range(8)])
            e_ = A.did(act.activation(dst, banks[b], ACT.Abs))
            A.wait(e_)
            e_ = A.did(act.activation(dst, dst, ACT.Exp, scale=-1.0))
            A.wait(e_)
            e_ = A.did(act.activation(dst, dst, ACT.Ln, bias=one_c))
            V.wait(e_)
            last_exp = dst, acc_free[b].by(dve.scalar_tensor_tensor(dst, banks[b], 0.0, dst, ALU.min, ALU.subtract))
        A.wait(last_exp[1])
        A.did(act.activation(last_exp[0], last_exp[0], ACT.Exp))

    interleave(pe, merge_gates(), [delta_head(3, reads, marks, PACE["last delta"]), *stick_pair(3, reads, marks, PACE["last stick"])])
    merged = at("merged", rawA + 16 * KB + 512, [P, 2, 8, T], F32R)
    mtmp = at("mtmp", rawA + 48 * KB + 512, [P, 2, 2, T])
    marks = fence()
    PE.wait(*heads_end)
    gates_read = acc_free[0].now(), acc_free[1].now()
    pair_free = [Signal(counts, f"pair{b}_free") for b in range(2)]
    mhi = [Signal(counts, f"mtmp{b}_hi") for b in range(2)]
    mlo = [Signal(counts, f"mtmp{b}_lo") for b in range(2)]
    for x in pair_free + mhi + mlo:
        x.prime(V)
    for e in (A, V, G):
        e.wait(*marks)
    with loop("branch", 0, 2) as i:
        for c in range(4):
            s, b = c, c % 2
            ba, bb = banks[2 - 2 * b], banks[3 - 2 * b]
            terms = terms_T(s, ba, [(k, k) for k in range(4)], osb) + terms_T(s, bb, [(4 + k, k) for k in range(4)], ogd)
            for _ in product(s, terms, first_wait=(pair_free[b].now(), *(gates_read if b else ()))):
                pass
            split((s + 2) % 4)
            m = 4 * i + c
            V.wait(used[s].now(), mhi[b].now(), mlo[b].now())
            a1 = V.did(dve.tensor_tensor(mtmp[:, b, 0, :], ba, sig_sb[:, m, :], ALU.mult))
            a2 = pair_free[b].by(dve.tensor_tensor(mtmp[:, b, 1, :], bb, sig_gd[:, m, :], ALU.mult))
            V.wait(a1, a2)
            a3 = V.did(dve.tensor_tensor(mtmp[:, b, 0, :], mtmp[:, b, 0, :], mtmp[:, b, 1, :], ALU.add))
            A.wait(a3)
            h_ = mhi[b].by(act.copy(merged[:, 0, m, :], mtmp[:, b, 0, :]))
            V.wait(h_)
            mlo[b].by(dve.tensor_tensor(merged[:, 1, m, :], mtmp[:, b, 0, :], merged[:, 0, m, :].bitcast(F32), ALU.subtract))

    def half_terms(s, src, kk, half_banks, first, last):
        w = ring[:, s].rearrange("p two (k n) -> p two k n", k=2)
        o = []
        for kl in range(2):
            for j in range(NT):
                for m, (a, b) in enumerate(((0, 0), (0, 1), (1, 0))):
                    o.append((banks[half_banks[j]], src[:, a, kk + kl, j * P:(j + 1) * P], w[:, b, kl, :],
                              first and kl == 0 and m == 0, last and kl == 1 and m == 2))
        return o

    def token_terms(src, j, bank):
        o = []
        for s in range(4):
            w = ring[:, s].rearrange("p two (k n) -> p two k n", k=2)
            for kl in range(2):
                for m, (a, b) in enumerate(((0, 0), (0, 1), (1, 0))):
                    o.append((s, banks[bank], src[:, a, 2 * s + kl, j * P:(j + 1) * P], w[:, b, kl, :],
                              s == 0 and kl == 0 and m == 0, s == 3 and kl == 1 and m == 2, kl == 1 and m == 2))
        return o

    def add_normed(j, lo_bank, hi_bank, w_bc, junk, res, stats, done_hi, done_lo, junk_free):
        A.wait(done_lo, junk_free)
        A.did(act.activation(junk[:, 0:512], banks[lo_bank], ACT.Square, accum_out=stats[:, 3 * j:3 * j + 1]))
        A.wait(done_hi)
        a = A.did(act.activation(junk[:, 512:1024], banks[hi_bank], ACT.Square, accum_out=stats[:, 3 * j + 1:3 * j + 2]))
        V.wait(a)
        a = V.did(dve.tensor_tensor(stats[:, 3 * j + 2:3 * j + 3], stats[:, 3 * j:3 * j + 1], stats[:, 3 * j + 1:3 * j + 2], ALU.add))
        r = rstd(stats[:, 3 * j + 2:3 * j + 3], stats[:, 3 * j + 2:3 * j + 3], D, a)
        V.wait(r)
        halves = [(slice(0, 512), lo_bank), (slice(512, 1024), hi_bank)]
        scaled = [V.did(dve.scalar_tensor_tensor(junk[:, f], banks[bank], stats[:, 3 * j + 2:3 * j + 3], w_bc[:, f],
                                                 ALU.mult, ALU.mult)) for f, bank in halves]
        added = []
        for (f, _), s_ in zip(halves, scaled):
            V.wait(s_)
            added.append(V.did(dve.tensor_tensor(res[:, j, f], res[:, j, f], junk[:, f], ALU.add)))
        return added

    def project_half0(src, tiles_done):
        for s in range(4):
            PE.wait(*tiles_done.get(s, ()))
            for _ in product(s, half_terms(s, src, 2 * s, (4, 5, 6, 7), s == 0, s == 3)):
                pass
            split((s + 2) % 4)

    def project_half1(src, lo_banks, hi_banks, w_bc, junk, res, res_ready, stats, scratch, norm_stats):
        left = used[3].now()
        V.wait(res_ready)
        ready, scaled = [], []
        for j in range(NT):
            for (s, o, l, r, a, b, slab_end) in token_terms(src, j, hi_banks[j]):
                if j == 0:
                    PE.wait(lo_done[s].now())
                m = pe.matmul(o, l, r, start=a, stop=b)
                if j == NT - 1 and slab_end:
                    used[s].by(m)
                if j == 0 and slab_end and s < 2:
                    split(s + 2)
            multiplied = PE.did(m) if j < NT - 1 else used[3].now()
            ready.append(add_normed(j, lo_banks[j], hi_banks[j], w_bc, junk[:, j % 2, :], res, stats, multiplied, left,
                                    ready[j - 2] if j > 1 else None)[-1])
            if j:
                scaled.append(norm_tile(j - 1, res, scratch, norm_stats, ready[j - 1]))
        scaled.append(norm_tile(NT - 1, res, scratch, norm_stats, ready[-1]))
        PE.wait(ready[0])
        keep_warm(banks[hi_banks[0]], NORM_TAIL_US)
        return scaled

    A.wait(*[x.now() for x in pair_free + used])
    ydma = Signal(counts, "reload_x", 16)
    wdma = Signal(counts, "post_w_loaded", 16)
    post_bc = at("post_bc", r4, [P, D])
    junk1 = at("junk1", r4 + 4 * KB, [P, 2, D])
    scr2 = at("norm_scratch2", r4 + 12 * KB, [P, NT, D])
    for j in range(NT):
        xr_ = ydma.by(act.dma_start(x1[:, j, :], t["x"][0, j * P:(j + 1) * P, :]))
    wr_ = wdma.by(act.dma_start(post_bc, t["post_norm_w"][0].partition_broadcast(P)))
    bias_w = at("bias_w", r4 + 32 * KB, [P, 4, T])
    skew_read = Signal(counts, "skew_read", 16)
    for h in range(4):
        src = skew[h, 127:127 + P * 383].rearrange("(p m) -> p m", m=383)[:, 0:256]
        bias_in = skew_read.by(act.dma_start(bias_w[:, h, 256:512], src))
    V.wait(wr_)
    tiles_done = {0: tuple(x.before(1) for x in mlo), 3: tuple(x.now() for x in mlo)}
    project_half0(merged, tiles_done)
    scaled = project_half1(merged, (4, 5, 6, 7), (0, 1, 2, 3), post_bc, junk1, x1, xr_, stat[:, 8:20], scr2, stat[:, 4:8])
    h_ready = transpose_normed(scr2, aprew_col, scaled)

    off[0] = r4
    mix = take("mix", [P, 2, 8, T], F32R)
    off[0] += 8 * KB
    rawb = take("rawb", [P, 6, T])
    pick = take("pick", [8, 8 * P])
    pick_h = take("pick_h", [8, 2 * P])
    cumT = take("cumT", [8, T])
    wf = take("wf", [P, 64])
    wf_s = take("wf_s", [P, 2, 64], F32R)
    sg_bc = take("sg_bc", [P, P])
    bbuf = [take(f"b{n}", [P, T]) for n in range(17)]
    assert off[0] <= nc.sbuf_usable_end, off[0] - r4
    b2_dma = Signal(counts, "forget_in", 16)
    A.wait(h_ready[-1], PE.now())
    for dst, src in ((wf.rearrange("p (k n) -> p k n", k=8), w2[0].rearrange("(k p) n -> p k n", p=P)[:, :, 3072:3080]),
                     (sg_bc, t["subln_g_2"][0].partition_broadcast(P)), (pick, t["bias_consts"][0:8, 384:])):
        forget_in = b2_dma.by(act.dma_start(dst, src))

    def forget_gates():
        V.wait(bias_in)
        V.did(dve.tensor_copy(bias_w[:, :, 0:256], far.unsqueeze(2).broadcast_to([P, 4, 256])))
        for h in range(4):
            V.did(dve.tensor_tensor(bias_w[:, h, 384:512], bias_w[:, h, 384:512], mat["causal"], ALU.add))
        yield 4
        A.wait(forget_in)
        a = A.did(act.copy(wf_s[:, 0, :], wf))
        V.wait(a)
        V.did(dve.tensor_scalar(sg_bc, sg_bc, 1.0 - lam_init, None, ALU.mult))
        a = V.did(dve.tensor_tensor(wf_s[:, 1, :], wf, wf_s[:, 0, :].bitcast(F32), ALU.subtract))
        yield 2
        p_ = yield from narrow(wf_s.rearrange("p two (k n) -> p two k n", k=8), cumT, banks[5], banks[6], (a, *h_ready))
        fz, fe = stat[:, 0:32].rearrange("p (t h) -> p t h", t=4), stat[:, 32:64].rearrange("p (t h) -> p t h", t=4)
        V.wait(p_)
        a = V.did(dve.tensor_tensor(fz, banks[6][:, 0:32].rearrange("p (t h) -> p t h", t=4),
                                    bfb.unsqueeze(1).broadcast_to([P, 4, 8]), ALU.add))
        A.wait(a)
        a = A.did(act.activation(fe, fz, ACT.Abs))
        A.wait(a)
        a = A.did(act.activation(fe, fe, ACT.Exp, scale=-1.0))
        A.wait(a)
        a = A.did(act.activation(fe, fe, ACT.Ln, bias=one_c))
        V.wait(a)
        a = V.did(dve.scalar_tensor_tensor(fl, fz, 0.0, fe, ALU.min, ALU.subtract))
        yield 4
        PE.wait(a)
        for j in range(NT):
            p_ = pe.matmul(banks[7][0:8, j * P:(j + 1) * P], fl[:, j, :], mat["upper"], start=j == 0, stop=j == 3, skip_group_check=True)
            if j < 3:
                pe.matmul(banks[7][0:8, (j + 1) * P:T].rearrange("p (c f) -> p c f", f=P), fl[:, j, :],
                          mat["ones"].unsqueeze(1).broadcast_to([P, 3 - j, P]), start=False, stop=False, skip_group_check=True)
        V.wait(PE.did(p_))
        V.did(dve.tensor_copy(cumT, banks[7][0:8, :]))

    v_wait = nc.alloc_semaphore("dve_held")

    HALF0_K = (0, 4, 2, 6)

    def project_b(reads, k_ready=None):
        for n in range(6):
            s, b = n % 4, n % 2
            yield from product(s, terms_T(s, banks[b], all_k), first_wait=(acc_free[b].now(),),
                               k_ready=None if n else k_ready)
            split((n + 2) % 6 % 4)
            assert reads is None or n in reads, n
            A.wait(used[s].now(), reads[n] if reads else None)
            acc_free[b].by(act.copy(rawb[:, n, :], banks[b]))

    (qd, kd, vd, od, bias_h, *diff_rows) = bbuf[:9]
    (qf, kf, vf, of_, *fox_rows) = bbuf[9:]

    def softmax_scores(bank, w, in1, dst, mx, sm, ready):
        V.wait(*ready)
        V.hold(v_wait)
        a = V.did(dve.tensor_tensor_reduce(out=dst[:, 0:w], in0=bank[:, 0:w], in1=in1, scale=1.0, scalar=-3.0e38,
                                           op0=ALU.add, op1=ALU.max, accum_out=mx))
        read = a
        V.wait(a)
        a = V.did(dve.tensor_scalar(mx, mx, -1.0, None, ALU.mult))
        A.wait(a)
        return read, A.did(act.activation(dst[:, 0:w], dst[:, 0:w], ACT.Exp, bias=mx, accum_out=sm))

    def transposed(bank, src, w, ready):
        PE.wait(*ready)
        for c in range(w // P):
            m = pe.transpose(bank[:, c * P:(c + 1) * P], src[:, c * P:(c + 1) * P], ident)
        p_ = PE.did(m)
        A.wait(p_)
        return A.did(act.copy(src[:, 0:w], bank[:, 0:w]))

    def prepare_b(q, k, v, bank, reads, n0):
        reads[n0] = V.did(dve.tensor_scalar(q, rawb[:, n0, :], 64 ** -0.5, None, ALU.mult))
        reads[n0 + 1] = qk = V.did(dve.tensor_copy(k, rawb[:, n0 + 1, :]))
        for c in range(4):
            m = pe.transpose(bank[:, c * P:(c + 1) * P], rawb[:, n0 + 2, c * P:(c + 1) * P], ident)
        reads[n0 + 2] = p_ = PE.did(m)
        A.wait(p_)
        return qk, A.did(act.copy(v, bank))

    def to_mix(src, bank, m, ready):
        PE.wait(*ready)
        for c in range(4):
            q = pe.transpose(bank[:, c * P:(c + 1) * P], src[:, c * P:(c + 1) * P], ident)
        p_ = PE.did(q)
        A.wait(p_)
        a = A.did(act.copy(mix[:, 0, m, :], bank))
        V.wait(a)
        return V.did(dve.tensor_tensor(mix[:, 1, m, :], bank, mix[:, 0, m, :].bitcast(F32), ALU.subtract))

    def diff_head(i, reads, marks, pace, pairs):
        done = {}

        def rows(n):
            X, Y = (banks[b] for b in pairs[n])
            scA, scB = diff_rows[2 * n:2 * n + 2]
            st = stat[:, 8 * n:8 * n + 8]
            yield pace[0]
            if n == 0:
                for e in engines:
                    e.wait(*marks)
                done["qk"], done["v"] = prepare_b(qd, kd, vd, X, reads, 0)
                done["bias"] = V.did(dve.tensor_copy(bias_h, bias_w[:, i, :]))
            yield pace[1]
            free = squared = None
            for t_ in ((3, 0), (2, 1))[n]:
                w = (t_ + 1) * P
                es, read = [], None
                for m_, (bank, dst) in enumerate(((X, scA), (Y, scB))):
                    hp = slice(64 * m_, 64 * m_ + 64)
                    PE.wait(done["qk"], done["v"], free, read)
                    z = PE.did(pe.matmul(bank[:, 0:w], qd[hp, t_ * P:w], kd[hp, 0:w], start=True, stop=True))
                    V.wait(squared)
                    read, e_ = softmax_scores(bank, w, bias_h[:, T - w:T], dst, st[:, 2 * m_:2 * m_ + 1],
                                              st[:, 2 * m_ + 1:2 * m_ + 2], (z, done["bias"]))
                    es.append(e_)
                    if X is not Y:
                        read = None
                    elif m_ == 0:
                        yield pace[2]
                V.wait(es[0])
                V.did(dve.reciprocal(st[:, 4:5], st[:, 1:2]))
                V.wait(es[1])
                a = V.did(dve.reciprocal(st[:, 5:6], st[:, 3:4]))
                V.wait(a)
                a = V.did(dve.scalar_tensor_tensor(st[:, 5:6], st[:, 5:6], -1.0, lam_c, ALU.mult, ALU.mult))
                b_ = V.did(dve.tensor_scalar(scA[:, 0:w], scA[:, 0:w], st[:, 4:5], None, ALU.mult))
                V.wait(b_)
                pr = V.did(dve.scalar_tensor_tensor(scA[:, 0:w], scB[:, 0:w], st[:, 5:6], scA[:, 0:w], ALU.mult, ALU.add))
                yield pace[3] + pace[4] * w / T
                ev = transposed(X, scA, w, (pr,))
                yield pace[5] + pace[6] * w / T
                PE.wait(ev)
                for c in range(t_ + 1):
                    q = pe.matmul(Y[:, 0:P], scA[:, c * P:(c + 1) * P], vd[:, c * P:(c + 1) * P], start=c == 0, stop=c == t_)
                p_ = PE.did(q)
                V.wait(p_)
                free = V.did(dve.tensor_copy(od[:, t_ * P:w], Y[:, 0:P]))
                A.wait(free)
                squared = done[t_] = A.did(act.activation(scA[:, 0:P], od[:, t_ * P:w], ACT.Square,
                                                accum_out=stat[:, 24 + t_:25 + t_]))
                yield pace[7]
            if all(t_ in done for t_ in range(NT)) and "normed" not in done:
                done["normed"] = True
                r = rstd(stat[:, 24:28], stat[:, 24:28], P, A.now())
                V.wait(r)
                for t_ in range(NT):
                    f = slice(t_ * P, (t_ + 1) * P)
                    a = V.did(dve.scalar_tensor_tensor(od[:, f], od[:, f], stat[:, 24 + t_:25 + t_], sg_bc, ALU.mult, ALU.mult))
                yield pace[8]
                to_mix(od, X, i, (a,))

        return [rows(0), rows(1)]

    def fox_pair(i, reads, marks, pace):
        done = {}

        def head(h):
            bank = banks[6 + h]
            sc, negcum = fox_rows[2 * h:2 * h + 2]
            st = stat[:, 16 + 4 * h:20 + 4 * h]
            hp = slice(64 * h, 64 * h + 64)
            yield pace[0]
            if h == 0:
                for e in engines:
                    e.wait(*marks)
                done["qk"], done["v"] = prepare_b(qf, kf, vf, bank, reads, 3)
                done["pick"] = V.did(dve.tensor_copy(pick_h, pick[:, bass.ds(2 * i * P, 2 * P)]))
            yield pace[1]
            PE.wait(done["pick"], done["v"])
            p_ = PE.did(pe.matmul(bank, pick_h[:, h * P:(h + 1) * P], cumT, start=True, stop=True))
            A.wait(p_)
            free = A.did(act.copy(negcum, bank))
            yield pace[2]
            for t_ in range(NT):
                w = (t_ + 1) * P
                PE.wait(done["qk"], free)
                pe.matmul(bank[:, 0:w], qf[hp, t_ * P:w], kf[hp, 0:w], start=True, stop=True)
                z = PE.did(pe.matmul(bank[:, t_ * P:w], ident_b, causal_b, start=False, stop=True, skip_group_check=True))
                _, ex = softmax_scores(bank, w, negcum[:, 0:w], sc, st[:, 0:1], st[:, 1:2], (z, free))
                V.wait(ex)
                r = V.did(dve.reciprocal(st[:, 2:3], st[:, 1:2]))
                yield pace[3] + pace[4] * w / T
                ev = transposed(bank, sc, w, (ex,))
                yield pace[5] + pace[6] * w / T
                PE.wait(ev)
                for c in range(t_ + 1):
                    q = pe.matmul(bank[:, 0:64], sc[:, c * P:(c + 1) * P], vf[:, c * P + 64 * h:c * P + 64 * h + 64],
                                  start=c == 0, stop=c == t_)
                p_ = PE.did(q)
                V.wait(p_, r)
                free = V.did(dve.tensor_scalar(of_[:, t_ * P + 64 * h:t_ * P + 64 * h + 64], bank[:, 0:64],
                                               st[:, 2:3], None, ALU.mult))
                yield pace[7]
            done[h] = free
            if (1 - h) in done:
                to_mix(of_, bank, 4 + i, (done[0], done[1]))

        return [head(0), head(1)]

    interleave(pe, project_b(None, h_ready), [forget_gates()])
    with loop("stage_b", 1, 4) as i:
        reads, marks = {}, fence()
        interleave(pe, project_b(reads), [*diff_head(i - 1, reads, marks, PACE["diff"], ((2, 3), (4, 5))),
                                              *fox_pair(i - 1, reads, marks, PACE["fox"])])
    reads, marks = {}, fence()

    def heads_products():
        PE.wait(*[a.now() for a in acc_free])
        for s, k0 in enumerate(HALF0_K):
            terms = half_terms(s, mix, k0, (0, 1, 2, 3), s == 0, False)
            if s < 2:
                yield from product(s, terms)
            else:
                PE.wait(lo_done[s].now())
                for o, l, r, a, b in terms[:len(terms) // 2]:
                    pe.matmul(o, l, r, start=a, stop=b)
                    yield 0
            split((s + 2) % 4)

    interleave(pe, heads_products(), [*diff_head(3, reads, marks, PACE["last diff"], ((4, 4), (5, 5))),
                                      *fox_pair(3, reads, marks, PACE["last fox"])])

    marks = fence()
    for e in engines:
        e.wait(*marks)
    for s in (2, 3):
        terms = half_terms(s, mix, HALF0_K[s], (0, 1, 2, 3), False, s == 3)
        for o, l, r, a, b in terms[len(terms) // 2:]:
            m = pe.matmul(o, l, r, start=a, stop=b)
        used[s].by(m)
    b2dma = Signal(counts, "post_w2_loaded", 16)
    post2 = at("post2", r4 + 32 * KB, [P, D])
    junk2 = at("junk2", r4 + 36 * KB, [P, 2, D])
    scr3 = at("norm_scratch3", r4 + 44 * KB, [P, NT, D])
    V.wait(b2dma.by(act.dma_start(post2, t["ln_attn_post_2"][0].partition_broadcast(P))))
    scaled = project_half1(mix, (0, 1, 2, 3), (4, 5, 6, 7), post2, junk2, x1, None, stat[:, 8:20], scr3, stat[:, 4:8])
    h_ready = transpose_normed(scr3, mprew_col, scaled)
    u = at("u", r4, [P, 34, T])
    ring_u = at("ring_u", r4 + 68 * KB, [P, 4, 2, 2 * T], F32R)
    relu_done = [Signal(counts, f"relu{b}") for b in range(2)]

    def up_slab(i, c, k_ready=None):
        s, b = c, c % 2
        for _ in product(s, terms_T(s, banks[b], all_k), first_wait=(relu_done[b].now(),), k_ready=k_ready):
            pass
        split((s + 2) % 4)
        A.wait(used[s].now())
        r_ = relu_done[b].by(act.activation(u[:, 4 * i + c, :], banks[b], ACT.Relu))
        V.wait(r_)
        V.did(dve.tensor_tensor(u[:, 4 * i + c, :], u[:, 4 * i + c, :], u[:, 4 * i + c, :], ALU.mult))

    for c in range(4):
        up_slab(0, c, None if c else h_ready)
    u_split = [Signal(counts, f"u{s}_split") for s in range(4)]
    r1 = base
    post3 = at("post3", r1, [P, D])
    junk3 = at("junk3", r1 + 4 * KB, [P, 2, D])

    def split_u(k0, s):
        x = u[:, bass.ds(k0, 2), :].rearrange("p a b -> p (a b)")
        A.wait(used[s].now())
        h_ = A.did(act.copy(ring_u[:, s, 0, :], x))
        V.wait(h_)
        u_split[s].by(dve.tensor_tensor(ring_u[:, s, 1, :], x, ring_u[:, s, 0, :].bitcast(F32), ALU.subtract))

    V.wait(V.now())
    A.wait(V.did(dve.tensor_copy(u[:, 32:34, :], u[:, 0:2, :])))
    split_u(0, 0)
    zeros_b = notbefore_b
    zeroed = V.did(dve.memset(zeros_b, 0.0))
    with loop("up", 1, 8) as i:
        for c in range(4):
            up_slab(i, c)
    A.wait(V.now())
    b3dma = Signal(counts, "post_w3_loaded", 16)
    w3 = b3dma.by(act.dma_start(post3, t["ln_mlp_post_2"][0].partition_broadcast(P)))

    def down_slab(i, s, hb, opened=True):
        w = ring[:, s].rearrange("p two (k n) -> p two k n", k=2)
        xs = ring_u[:, s].rearrange("p two (k n) -> p two k n", k=2)
        PE.wait(u_split[s].now())
        split_u(i * 8 + 2 * s + 2, (s + 1) % 4)
        terms = []
        for kl in range(2):
            for j in range(NT):
                for a, b in ((0, 0), (0, 1), (1, 0)):
                    terms.append((banks[hb[j]], xs[:, a, kl, j * P:(j + 1) * P], w[:, b, kl, :], False, True))
        for _ in product(s, terms, opened=True):
            pass
        split((s + 2) % 4)

    PE.wait(zeroed)
    for half in range(2):
        hb = [4 - 4 * half + j for j in range(4)]
        PE.wait(*([x.now() for x in relu_done] if half else ()))
        for j in range(4):
            pe.matmul(banks[hb[j]], zeros_b, over4(ident_b), start=True, stop=True)
        with loop(f"down{half}", 0, 4 - half) as i:
            for s in range(4):
                down_slab(i, s, hb)
    split_u(26, 1)
    split(2)
    split_u(28, 2)
    split(3)
    split_u(30, 3)
    last_half0 = used[3].now()
    V.wait(w3)
    outs = Signal(counts, "out_stored", 16)
    done = []
    for j in range(NT):
        for s in range(4):
            w = ring[:, s].rearrange("p two (k n) -> p two k n", k=2)
            xs = ring_u[:, s].rearrange("p two (k n) -> p two k n", k=2)
            PE.wait(u_split[s].now(), lo_done[s].now())
            for kl in range(2):
                for a, b in ((0, 0), (0, 1), (1, 0)):
                    m = pe.matmul(banks[j], xs[:, a, kl, j * P:(j + 1) * P], w[:, b, kl, :], start=False, stop=True,
                                  skip_group_check=True)
        done.append(add_normed(j, 4 + j, j, post3, junk3[:, j % 2, :], x1, stat[:, 8:20], PE.did(m), last_half0,
                               done[j - 2][-1] if j > 1 else None))
        for half, added in enumerate(done[j]):
            nc.sync.wait_ge(*added[:2])
            f = slice(512 * half, 512 * half + 512)
            outs.by(nc.sync.dma_start(out[0, j * P:(j + 1) * P, f], x1[:, j, f]))
    nc.sync.wait_ge(outs.sem, outs.count.value())
    return counts.found | dma_counts.found


_INS = ["x", "pre_norm_w", "post_norm_w", "w_in", "conv_w", "a_log", "dt_bias", "gdn_norm_w", "w_branch_sb",
        "w_branch_gdn", "w_out", "ln_attn_pre_2", "w_in_2", "b_f_2", "lam_q1_2", "lam_k1_2", "lam_q2_2",
        "lam_k2_2", "subln_g_2", "rel_bias_2", "w_out_2", "ln_attn_post_2", "ln_mlp_pre_2", "w_up_2",
        "w_down_2", "ln_mlp_post_2"]


def declared(nc, shapes, per):
    t = {n: nc.dram_tensor(f"in_{n}", s, F32, kind="ExternalInput").ap() for n, s in shapes.items()}
    out = nc.dram_tensor("out_0", shapes["x"], F32, kind="ExternalOutput").ap()
    return program(nc, t, out, per)


def kernel(**inputs):
    import concourse.bacc as _bacc
    from concourse.bass_utils import run_bass_kernel_spmd as _run

    arrays = {n: np.ascontiguousarray(inputs[n]) for n in _INS}
    arrays["shape_consts"] = shape_constants()
    arrays["bias_consts"] = bias_constants()
    shapes = {n: a.shape for n, a in arrays.items()}
    per = declared(_bacc.Bacc("TRN2", target_bir_lowering=False, num_devices=1), shapes, {})
    nc = _bacc.Bacc("TRN2", target_bir_lowering=False, num_devices=1)
    declared(nc, shapes, per)
    r = _run(nc, [{f"in_{n}": a for n, a in arrays.items()}], core_ids=[0])
    return r.results[0]["out_0"]
```
